# Optimizing a Trainium2 kernel written in Bass

```python
import math
import jax, jax.numpy as jnp
from jax import lax
import numpy as np

D_MODEL = 1024
BATCH = 1
SEQ = 256
DEPTH = 2
DEC_BATCH = 1
DEC_SEQ = 64
PAST_LEN = 512

CHUNK = 64
Q_BLOCK = 128
N_MIXERS = 2
N_DIFF_LAYERS = (DEPTH + 1) // 2
N_FOX_LAYERS = DEPTH // 2
DIFF_HEADS = 8
DIFF_HD = D_MODEL // (2 * DIFF_HEADS)
FOX_HEADS = 16
FOX_HD = D_MODEL // FOX_HEADS
N_GROUPS = 4
EXPERTS_PER_GROUP = 4
N_EXPERTS = N_GROUPS * EXPERTS_PER_GROUP
TOP_K_IN_GROUP = 2
D_EXPERT = 512
EPS = 1e-6
NEG_INF = -1e30

kernel_name = 'hybrid_diff_fox_hmoe_stream_step'

def rms_norm(x, gain):
    xf = x.astype(jnp.float32)
    y = xf * lax.rsqrt(jnp.mean(xf * xf, axis=-1, keepdims=True) + EPS)
    return (y * gain.astype(jnp.float32)).astype(x.dtype)

def masked_softmax(logits, mask):
    return jax.nn.softmax(jnp.where(mask, logits, NEG_INF), axis=-1)

def alibi_slopes(n_heads):
    return jnp.asarray(2.0 ** (-8.0 * np.arange(1, n_heads + 1) / n_heads), dtype=jnp.float32)

def sweep_query_blocks(attend, n_q, p0, n_keys, chunk_causal):
    outs = []
    for qs in range(0, n_q, Q_BLOCK):
        qe = min(qs + Q_BLOCK, n_q)
        last = p0 + qe
        reach = -(-last // CHUNK) * CHUNK if chunk_causal else last
        outs.append(attend(qs, qe, min(reach, n_keys)))
    return jnp.concatenate(outs, axis=1)

def diff_attention(h, k_past, v_past, w_in, w_out, q_gain, k_gain, lq1, lk1, lq2, lk2, subln_gain, lambda_init):
    b, s, _ = h.shape
    q, k, v = jnp.split(h @ w_in, 3, axis=-1)
    q = rms_norm(q.reshape(b, s, DIFF_HEADS, 2, DIFF_HD), q_gain)
    k = rms_norm(k.reshape(b, s, DIFF_HEADS, 2, DIFF_HD), k_gain)
    k_rows = k.reshape(b, s, DIFF_HEADS, 2 * DIFF_HD)
    v_rows = v.reshape(b, s, DIFF_HEADS, 2 * DIFF_HD)
    if k_past is None:
        p0 = 0
        keys, vals = k_rows, v_rows
    else:
        p0 = k_past.shape[1]
        keys = jnp.concatenate([k_past.astype(k_rows.dtype), k_rows], axis=1)
        vals = jnp.concatenate([v_past.astype(v_rows.dtype), v_rows], axis=1)
    n_keys = keys.shape[1]
    keys = keys.reshape(b, n_keys, DIFF_HEADS, 2, DIFF_HD)
    lam = (jnp.exp(jnp.sum(lq1.astype(jnp.float32) * lk1.astype(jnp.float32)))
           - jnp.exp(jnp.sum(lq2.astype(jnp.float32) * lk2.astype(jnp.float32))) + lambda_init)
    slopes = alibi_slopes(DIFF_HEADS)
    q_pos = p0 + jnp.arange(s, dtype=jnp.int32)
    k_pos = jnp.arange(n_keys, dtype=jnp.int32)
    scale = DIFF_HD ** -0.5

    def attend(qs, qe, ke):
        qp, kp = q_pos[qs:qe], k_pos[:ke]
        dist = jnp.abs(qp[:, None] - kp[None, :]).astype(jnp.float32)
        bias = -slopes[:, None, None] * dist[None]
        mask = (kp[None, :] // CHUNK) <= (qp[:, None] // CHUNK)

        def probs(c):
            logits = jnp.einsum('bqhd,bkhd->bhqk', q[:, qs:qe, :, c], keys[:, :ke, :, c]).astype(jnp.float32)
            return masked_softmax(logits * scale + bias, mask)

        diff_map = probs(0) - lam * probs(1)
        return jnp.einsum('bhqk,bkhe->bqhe', diff_map.astype(vals.dtype), vals[:, :ke])

    o = sweep_query_blocks(attend, s, p0, n_keys, chunk_causal=True)
    o = rms_norm(o, subln_gain) * (1.0 - lambda_init)
    return o.reshape(b, s, D_MODEL) @ w_out, k_rows, v_rows

def fox_attention(h, k_past, v_past, logf_past, w_in, b_f, w_out, q_gain, k_gain):
    b, s, _ = h.shape
    d = D_MODEL
    q, k, v, g, f_logit = jnp.split(h @ w_in, [d, 2 * d, 3 * d, 4 * d], axis=-1)
    q = rms_norm(q.reshape(b, s, FOX_HEADS, FOX_HD), q_gain)
    k = rms_norm(k.reshape(b, s, FOX_HEADS, FOX_HD), k_gain)
    v = v.reshape(b, s, FOX_HEADS, FOX_HD)
    logf = jax.nn.log_sigmoid((f_logit + b_f).astype(jnp.float32))
    q_off = lax.cumsum(logf, axis=1)
    if k_past is None:
        p0 = 0
        keys, vals, k_off = k, v, q_off
    else:
        p0 = k_past.shape[1]
        lp = logf_past.astype(jnp.float32)
        k_off_past = lp - lax.cumsum(lp, axis=1, reverse=True)
        keys = jnp.concatenate([k_past.astype(k.dtype), k], axis=1)
        vals = jnp.concatenate([v_past.astype(v.dtype), v], axis=1)
        k_off = jnp.concatenate([k_off_past, q_off], axis=1)
    n_keys = keys.shape[1]
    q_pos = p0 + jnp.arange(s, dtype=jnp.int32)
    k_pos = jnp.arange(n_keys, dtype=jnp.int32)
    q_off_t = jnp.transpose(q_off, (0, 2, 1))
    k_off_t = jnp.transpose(k_off, (0, 2, 1))
    scale = FOX_HD ** -0.5

    def attend(qs, qe, ke):
        qp, kp = q_pos[qs:qe], k_pos[:ke]
        mask = kp[None, :] <= qp[:, None]
        decay = q_off_t[:, :, qs:qe, None] - k_off_t[:, :, None, :ke]
        logits = jnp.einsum('bqhd,bkhd->bhqk', q[:, qs:qe], keys[:, :ke]).astype(jnp.float32) * scale + decay
        p = masked_softmax(logits, mask)
        return jnp.einsum('bhqk,bkhd->bqhd', p.astype(vals.dtype), vals[:, :ke])

    o = sweep_query_blocks(attend, s, p0, n_keys, chunk_causal=False)
    o = o.reshape(b, s, D_MODEL) * jax.nn.sigmoid(g)
    return o @ w_out, k, v, logf

def hier_moe(t, w_group, b_group, w_expert, b_expert, w_gate, w_up, w_down):
    n = t.shape[0]
    group_prob = jax.nn.softmax((t @ w_group + b_group).astype(jnp.float32), axis=-1)
    p_top, g_idx = lax.top_k(group_prob, 1)
    expert_logits = (t @ w_expert + b_expert).astype(jnp.float32).reshape(n, N_GROUPS, EXPERTS_PER_GROUP)
    in_group = jnp.einsum('ng,nge->ne', jax.nn.one_hot(g_idx[:, 0], N_GROUPS, dtype=jnp.float32), expert_logits)
    top_vals, top_idx = lax.top_k(in_group, TOP_K_IN_GROUP)
    w_sel = jax.nn.softmax(top_vals, axis=-1) * p_top
    expert_id = g_idx * EXPERTS_PER_GROUP + top_idx
    gates = jnp.sum(w_sel[..., None] * jax.nn.one_hot(expert_id, N_EXPERTS, dtype=jnp.float32), axis=1)
    gates = gates.astype(t.dtype)
    y = jnp.zeros_like(t)
    for e in range(N_EXPERTS):
        hid = jax.nn.silu(t @ w_gate[e]) * (t @ w_up[e])
        y = y + gates[:, e:e + 1] * (hid @ w_down[e])
    return y

def setup_inputs(seed: int = 0) -> dict:
    key = jax.random.key(seed)
    ks = jax.random.split(key, 32)
    f32 = jnp.float32
    D = D_MODEL

    def nrm(k, shape, scale):
        return jax.random.normal(k, shape, f32) * scale

    return {
        'x_prompt': nrm(ks[0], (BATCH, SEQ, D), 1.0),
        'x_sample': nrm(ks[1], (DEC_BATCH, DEC_SEQ, D), 1.0),
        'cache_diff_k': nrm(ks[2], (N_DIFF_LAYERS, DEC_BATCH, PAST_LEN, DIFF_HEADS, 2 * DIFF_HD), 1.0),
        'cache_diff_v': nrm(ks[3], (N_DIFF_LAYERS, DEC_BATCH, PAST_LEN, DIFF_HEADS, 2 * DIFF_HD), 1.0),
        'cache_fox_k': nrm(ks[4], (N_FOX_LAYERS, DEC_BATCH, PAST_LEN, FOX_HEADS, FOX_HD), 1.0),
        'cache_fox_v': nrm(ks[5], (N_FOX_LAYERS, DEC_BATCH, PAST_LEN, FOX_HEADS, FOX_HD), 1.0),
        'cache_fox_logf': jax.nn.log_sigmoid(2.0 + nrm(ks[6], (N_FOX_LAYERS, DEC_BATCH, PAST_LEN, FOX_HEADS), 1.0)),
        'norm_mix': 1.0 + nrm(ks[7], (DEPTH, D), 0.02),
        'norm_ffn': 1.0 + nrm(ks[8], (DEPTH, D), 0.02),
        'diff_w_in': nrm(ks[9], (N_DIFF_LAYERS, D, 3 * D), D ** -0.5),
        'diff_w_out': nrm(ks[10], (N_DIFF_LAYERS, D, D), D ** -0.5),
        'diff_q_norm': 1.0 + nrm(ks[11], (N_DIFF_LAYERS, DIFF_HD), 0.02),
        'diff_k_norm': 1.0 + nrm(ks[12], (N_DIFF_LAYERS, DIFF_HD), 0.02),
        'diff_lambda_q1': nrm(ks[13], (N_DIFF_LAYERS, DIFF_HD), 0.1),
        'diff_lambda_k1': nrm(ks[14], (N_DIFF_LAYERS, DIFF_HD), 0.1),
        'diff_lambda_q2': nrm(ks[15], (N_DIFF_LAYERS, DIFF_HD), 0.1),
        'diff_lambda_k2': nrm(ks[16], (N_DIFF_LAYERS, DIFF_HD), 0.1),
        'diff_subln': 1.0 + nrm(ks[17], (N_DIFF_LAYERS, 2 * DIFF_HD), 0.02),
        'fox_w_in': nrm(ks[18], (N_FOX_LAYERS, D, 4 * D + FOX_HEADS), D ** -0.5),
        'fox_b_f': 1.0 + 2.0 * jax.random.uniform(ks[19], (N_FOX_LAYERS, FOX_HEADS), f32),
        'fox_w_out': nrm(ks[20], (N_FOX_LAYERS, D, D), D ** -0.5),
        'fox_q_norm': 1.0 + nrm(ks[21], (N_FOX_LAYERS, FOX_HD), 0.02),
        'fox_k_norm': 1.0 + nrm(ks[22], (N_FOX_LAYERS, FOX_HD), 0.02),
        'moe_w_group': nrm(ks[23], (DEPTH, D, N_GROUPS), D ** -0.5),
        'moe_b_group': nrm(ks[24], (DEPTH, N_GROUPS), 0.01),
        'moe_w_expert': nrm(ks[25], (DEPTH, D, N_EXPERTS), D ** -0.5),
        'moe_b_expert': nrm(ks[26], (DEPTH, N_EXPERTS), 0.01),
        'moe_w_gate': nrm(ks[27], (DEPTH, N_EXPERTS, D, D_EXPERT), D ** -0.5),
        'moe_w_up': nrm(ks[28], (DEPTH, N_EXPERTS, D, D_EXPERT), D ** -0.5),
        'moe_w_down': nrm(ks[29], (DEPTH, N_EXPERTS, D_EXPERT, D), D_EXPERT ** -0.5),
    }

def reference(x_prompt, x_sample, cache_diff_k, cache_diff_v, cache_fox_k, cache_fox_v, cache_fox_logf,
              norm_mix, norm_ffn, diff_w_in, diff_w_out, diff_q_norm, diff_k_norm, diff_lambda_q1,
              diff_lambda_k1, diff_lambda_q2, diff_lambda_k2, diff_subln, fox_w_in, fox_b_f, fox_w_out,
              fox_q_norm, fox_k_norm, moe_w_group, moe_b_group, moe_w_expert, moe_b_expert, moe_w_gate,
              moe_w_up, moe_w_down):
    n_p = x_prompt.shape[0] * x_prompt.shape[1]
    xp, xs = x_prompt, x_sample
    dkp, dvp, dks, dvs = [], [], [], []
    fkp, fvp, flp, fks, fvs, fls = [], [], [], [], [], []
    for i in range(DEPTH):
        j = i // N_MIXERS
        hp = rms_norm(xp, norm_mix[i])
        hs = rms_norm(xs, norm_mix[i])
        if i % N_MIXERS == 0:
            lambda_init = 0.8 - 0.6 * math.exp(-0.3 * i)
            w = (diff_w_in[j], diff_w_out[j], diff_q_norm[j], diff_k_norm[j], diff_lambda_q1[j],
                 diff_lambda_k1[j], diff_lambda_q2[j], diff_lambda_k2[j], diff_subln[j])
            yp, k_p, v_p = diff_attention(hp, None, None, *w, lambda_init)
            ys, k_s, v_s = diff_attention(hs, cache_diff_k[j], cache_diff_v[j], *w, lambda_init)
            dkp.append(k_p); dvp.append(v_p); dks.append(k_s); dvs.append(v_s)
        else:
            w = (fox_w_in[j], fox_b_f[j], fox_w_out[j], fox_q_norm[j], fox_k_norm[j])
            yp, k_p, v_p, l_p = fox_attention(hp, None, None, None, *w)
            ys, k_s, v_s, l_s = fox_attention(hs, cache_fox_k[j], cache_fox_v[j], cache_fox_logf[j], *w)
            fkp.append(k_p); fvp.append(v_p); flp.append(l_p)
            fks.append(k_s); fvs.append(v_s); fls.append(l_s)
        xp = xp + yp
        xs = xs + ys
        tok = jnp.concatenate([xp.reshape(n_p, D_MODEL), xs.reshape(-1, D_MODEL)], axis=0)
        m = hier_moe(rms_norm(tok, norm_ffn[i]), moe_w_group[i], moe_b_group[i], moe_w_expert[i],
                     moe_b_expert[i], moe_w_gate[i], moe_w_up[i], moe_w_down[i])
        xp = xp + m[:n_p].reshape(xp.shape)
        xs = xs + m[n_p:].reshape(xs.shape)
    new_diff_k_prompt = jnp.stack(dkp)
    new_diff_v_prompt = jnp.stack(dvp)
    new_fox_k_prompt = jnp.stack(fkp)
    new_fox_v_prompt = jnp.stack(fvp)
    new_fox_logf_prompt = jnp.stack(flp)
    new_diff_k_sample = jnp.stack(dks)
    new_diff_v_sample = jnp.stack(dvs)
    new_fox_k_sample = jnp.stack(fks)
    new_fox_v_sample = jnp.stack(fvs)
    new_fox_logf_sample = jnp.stack(fls)
    return (xp, xs, new_diff_k_prompt, new_diff_v_prompt, new_fox_k_prompt, new_fox_v_prompt,
            new_fox_logf_prompt, new_diff_k_sample, new_diff_v_sample, new_fox_k_sample,
            new_fox_v_sample, new_fox_logf_sample)


_drawn_inputs = setup_inputs


def setup_inputs(seed=0):
    import zlib

    import numpy as np

    out = dict(_drawn_inputs(seed))
    spreads = {}
    factors = {'cache_fox_logf': 4.106, 'fox_q_norm': 6.481, 'fox_k_norm': 3.507, 'moe_b_expert': 3.558}
    for name, (base, spread) in spreads.items():
        noise = np.random.default_rng([zlib.crc32(name.encode()), seed]).standard_normal(out[name].shape)
        drawn = base * np.exp(spread * noise) if base else spread * noise
        out[name] = __import__('jax').numpy.asarray(drawn.astype(out[name].dtype))
    for name, factor in factors.items():
        out[name] = (out[name] * factor).astype(out[name].dtype)
    return out
```

```python
from contextlib import ExitStack
import math

import numpy as np
import concourse.bass as bass
from concourse import mybir

F32 = mybir.dt.float32
F32R = mybir.dt.float32r
I32 = mybir.dt.int32
ALU = mybir.AluOpType
ACT = mybir.ActivationFunctionType
AX = mybir.AxisListType.X

P = 128
D = 1024
SEQ, DEC, PAST = 256, 64, 512
TILES = 3
TOK = TILES * P
KB = D // P
HD = 64
PAIRS = D // P
FOX_HEADS = 16
GROUPS, PER_GROUP, EXPERTS = 4, 4, 16
F = 512
EPS = 1e-6
SCALE = HD ** -0.5
CHUNK = 64
CAP = 128
LAMBDA_INIT = 0.8 - 0.6 * math.exp(0.0)
ROWS = [128, 128, 64]
PTILES = PAST // P

RAW, HI = 6, 4
UNIT = 2048
PER_LOOP = 2 * 3 * PER_GROUP
IN_BLOCKS = [6, 8]
OUT_BLOCKS = D // F
BASE_IN, BASE_OUT, BASE_MOE = [0, 0], [0, 0], [0, 0]
_n = 0
for _l in range(2):
    BASE_IN[_l] = _n
    BASE_OUT[_l] = BASE_IN[_l] + 2 * IN_BLOCKS[_l]
    BASE_MOE[_l] = BASE_OUT[_l] + 2 * OUT_BLOCKS
    _n = BASE_MOE[_l] + GROUPS * PER_LOOP
UNITS = _n

FIRST = [("g", 0), ("u", 0)]
ORDER = [("g", 1), ("u", 1), ("d", 0), ("g", 2), ("u", 2), ("d", 1), ("g", 3), ("u", 3), ("d", 2),
         ("g", 4), ("d", 3), ("u", 4)]
BACK = [5, 6, 3, 4, 5, 6]
LAST = [m for m in ORDER if m[1] < PER_GROUP]

C_ID, C_IOTA, C_TRI, C_BEFORE, C_AFTER, C_ONE = (i * P for i in range(6))
C_VALID = 6 * P
C_PRIO = C_VALID + TILES
C_WIDTH = C_PRIO + 4 + 1
KEYS = [128, 256, 576]
BCOL = [0, 128, 384]
BIAS = 960


def constants():
    c = np.zeros((P, C_WIDTH), np.float32)
    i = np.arange(P)
    c[:, C_ID:C_ID + P] = np.eye(P)
    c[:, C_IOTA:C_IOTA + P] = np.where(i < CAP, i, -7)[None]
    c[:, C_TRI:C_TRI + P] = i[:, None] <= i[None]
    c[:, C_BEFORE:C_BEFORE + P] = i[:, None] < i[None]
    c[:, C_AFTER:C_AFTER + P] = i[:, None] > i[None]
    c[:, C_ONE:C_ONE + P] = 1
    c[:, C_VALID:C_VALID + TILES] = 1
    c[DEC:, C_VALID + 2] = 0
    c[:, C_PRIO:C_PRIO + 4] = [4, 3, 2, 1]
    dist = np.zeros((P, BIAS), np.float32)
    mask = np.zeros((P, BIAS), np.float32)
    for t, (keys, at, q0) in enumerate(zip(KEYS, BCOL, (0, P, PAST))):
        q = q0 + (i if t < 2 else i % DEC)[:, None]
        k = np.arange(keys)[None]
        dist[:, at:at + keys] = np.where(k // CHUNK <= q // CHUNK, -np.abs(q - k) / SCALE, -1e34)
        mask[:, at:at + keys] = np.where(k <= q, 0, -1e30 / SCALE)
    return c, dist, mask


class Unit:

    def __init__(self, base, i, g=0):
        n = base + i
        self.slot, self.hslot, self.static = n % RAW, n % HI, n
        self.n = g * PER_LOOP + n
        self.arrivals = g * (16 * PER_LOOP // RAW) + 16 * (n // RAW + 1)


def build(nc, A):
    with ExitStack() as ctx:
        S = lambda name: ctx.enter_context(nc.semaphore(name))

        start = (nc.sbuf_base + 63) // 32 * 32
        at = [start]

        def sb(name, shape, dt=F32, offset=None):
            size = (int(np.prod(shape[1:])) * 4 + 31) // 32 * 32
            if offset is None:
                offset = at[0]
                at[0] += size
            return nc.alloc_sbuf_tensor_at(name, shape, dt, offset=offset)

        ring_at = at[0]
        w_raw = sb("w_raw", [P, RAW, UNIT])
        w_lo = sb("w_lo", [P, RAW, UNIT], F32R, offset=ring_at)
        w_hi = sb("w_hi", [P, HI, UNIT], F32R)
        x = sb("x", [P, TILES, D])
        cst = sb("cst", [P, C_WIDTH])
        ident = cst[:, C_ID:C_ID + P]
        iota = cst[:, C_IOTA:C_IOTA + P]
        tri = cst[:, C_TRI:C_TRI + P]
        before = cst[:, C_BEFORE:C_BEFORE + P]
        after = cst[:, C_AFTER:C_AFTER + P]
        ones = cst[:, C_ONE:C_ONE + P]
        valid = cst[:, C_VALID:C_VALID + TILES]
        prio = cst[:, C_PRIO:C_PRIO + 4]
        neghalf = sb("neghalf", [P, 24])
        gain_at = at[0]
        gain = sb("gain", [P, 2, D])
        qk_gain = sb("qk_gain", [P, 4, HD])
        subln = sb("subln", [P, P])
        lamv = sb("lamv", [P, 4, HD])
        lamw = sb("lamw", [P, 8])
        ident2 = sb("ident2", [P, HD])
        w_router = sb("w_router", [P, 2, KB, 20])
        b_router = sb("b_router", [P, 2, 20])
        b_forget = sb("b_forget", [P, FOX_HEADS])
        ident_r = sb("ident_r", [P, FOX_HEADS], F32R)
        stat = sb("stat", [P, 160])
        ss, mean, rstd = stat[:, 0:3], stat[:, 3:6], stat[:, 6:9]
        mx, nmx, sm, rs = (stat[:, a:a + 6].rearrange("p (j c) -> p j c", j=3) for a in (12, 18, 24, 30))
        ms = [stat[:, 40 + 24 * i:64 + 24 * i] for i in range(2)]
        rr = [stat[:, 88 + 24 * i:112 + 24 * i] for i in range(2)]
        flag = sb("flag", [1, 8], I32)
        region = at[0]

        hT_hi = sb("hT_hi", [P, KB, TOK], F32R, offset=region)
        hT_lo = sb("hT_lo", [P, KB, TOK], F32R, offset=region + 12288)
        oT_hi = sb("oT_hi", [P, KB, TOK], F32R, offset=region)
        oT_lo = sb("oT_lo", [P, KB, TOK], F32R, offset=region + 12288)
        dist = sb("dist", [P, BIAS], offset=region)
        bias = sb("bias", [P, 2, BIAS], offset=region + 3840)
        pick_heads = sb("pick_heads", [FOX_HEADS, PAIRS, P], F32R, offset=region)
        probs = sb("probs", [P, 3, 576], offset=region + 11520)
        dT = sb("dT", [P, 2, 640], offset=region + 18432)
        assert 18432 + 5120 <= 24576
        at[0] = region + 24576
        h_at = at[0]
        h = sb("h", [P, TILES, D])
        o = sb("o", [P, TILES, D], offset=h_at)
        k_past = sb("k_past", [P, 2, PTILES, P])
        v_past = sb("v_past", [P, 2, PTILES, P])
        kT_past = sb("kT_past", [P, 2, PAST])
        qT = sb("qT", [P, PAIRS, SEQ])
        q_diag = sb("q_diag", [P, PAIRS, P])
        kT_at = at[0]
        kT_new = sb("kT_new", [P, PAIRS, SEQ + DEC])
        o_sq = sb("o_sq", [P, 2, D], offset=kT_at)
        v_new = sb("v_new", [P, TILES, D])
        qk_at = at[0]
        qk = sb("qk", [P, 2, TILES, F])
        gate = sb("gate", [P, TILES, D], offset=qk_at)
        diag = sb("diag", [P, 2, 2 * P])
        w_f = sb("w_f", [P, KB, FOX_HEADS])
        w_f_hi = sb("w_f_hi", [P, KB, FOX_HEADS], F32R)
        w_f_lo = sb("w_f_lo", [P, KB, FOX_HEADS], F32R)
        lf = sb("lf", [P, 8, TILES * FOX_HEADS])
        logf = sb("logf", [P, TILES, FOX_HEADS])
        logf_past = sb("logf_past", [P, PTILES, FOX_HEADS])
        off_hi = sb("off_hi", [FOX_HEADS, 832], F32R, offset=gain_at)
        off_lo = sb("off_lo", [FOX_HEADS, 832], F32R, offset=gain_at + 4 * D)
        top = at[0]

        at[0] = region
        h2 = sb("h2", [P, TILES, D])
        h2_hi = sb("h2_hi", [P, TILES, D], F32R)
        h2_lo = sb("h2_lo", [P, TILES, D], F32R)
        h2T = sb("h2T", [P, KB, TOK])
        xT_hi = sb("xT_hi", [P, KB, P], F32R)
        xT_lo = sb("xT_lo", [P, KB, P], F32R)
        pick = sb("pick", [P, TILES, P], F32R)
        pickT = sb("pickT", [P, TILES, P], F32R)
        act_g = sb("act_g", [P, F])
        hid = sb("hid", [P, F])
        hidT_hi = sb("hidT_hi", [P, 4, P], F32R)
        hidT_lo = sb("hidT_lo", [P, 4, P], F32R)
        y_hi = sb("y_hi", [P, D], F32R)
        y_lo = sb("y_lo", [P, D], F32R)
        over_w = sb("over_w", [P, UNIT])
        over_gate = sb("over_gate", [P, TILES, EXPERTS])
        over_col = sb("over_col", [P, TILES])
        over_hT = sb("over_hT", [P, F])
        r_ = sb("router", [P, 640])
        gates_hl = sb("gates_hl", [P, TILES, 8], F32R)
        slot_gate = sb("slot_gate", [P, 4])
        pos_g = sb("pos_g", [P, TILES])
        top = max(top, at[0])
        assert top <= nc.sbuf_usable_end, (top, nc.sbuf_usable_end)
        rcol = [0]

        def rt(*shape):
            n = int(np.prod(shape))
            ap = r_[:, rcol[0]:rcol[0] + n]
            rcol[0] += n
            if len(shape) == 2:
                ap = ap.rearrange("p (a b) -> p a b", a=shape[0])
            return ap

        lg = rt(3, 20)
        gmx, gsum, ptop, v1, v2, dv, e2, w1, w2, rank, over = (rt(3) for _ in range(11))
        gd, ge, oh, ig, oh1, oh2, ig2, t4, gate4, t4b = (rt(3, 4) for _ in range(10))
        pos = rt(3, 4)
        total = rt(1)
        t16 = rt(48)

        ps = ctx.enter_context(nc.psum_tensor("ps", [P, 8, 512], F32))

        raw_ready = [S(f"raw_ready{i}") for i in range(RAW)]
        hi_ready, lo_ready, units_used = S("hi_ready"), S("lo_ready"), S("units_used")
        x_loaded, const_loaded, small_loaded = S("x_loaded"), S("const_loaded"), S("small_loaded")
        gain_loaded = [[S(f"gain_loaded{l}{i}") for i in range(2)] for l in range(2)]
        x_padded, pads_ready, halves_ready, lam_ready = S("x_padded"), S("pads_ready"), S("halves_ready"), S("lam_ready")
        lam_dots, lam_exps = S("lam_dots"), S("lam_exps")
        dve_chain, pool_chain = S("dve_chain"), S("pool_chain")
        chain = {"dve": 0, "pool": 0}

        def link(eng, which, ins):
            chain[which] += 1
            s = dve_chain if which == "dve" else pool_chain
            ins.then_inc(s, 1)
            eng.wait_ge(s, chain[which])

        per_layer = dict(
            sq0=3, rstd0=1, h_ready0=3, tr0=6, hi0=6, lo0=6, proj_done=12, qk_sq=12, qk_ms=12, qk_r=4, qk_n1=12,
            qk_normed=12, qk_tr=12, qk_evac=12, v_copied=6, g_exp=0, g_done=0, k_stored=16 * 2 * TILES, v_stored=16 * TILES,
            k_loaded0=64, k_loaded1=64, v_loaded0=64, v_loaded1=64,
            dist_ready=9, alibi=16, past_tr=8, past_ev=8, scores_done=24, max_done=24, neg_done=24, exp_done=24,
            diag_done=24, dT_done=24, dT_copied=24, pv_done=24, o_done=24, o_zeroed=1, o_sqd=3, o_ms=3, o_r=3, o_normed=3, o_tr=6,
            o_hi=6, o_lo=6, out_done=4, x_mid=6,
            sq1=3, rstd1=1, h_ready1=3, tr1=6, ev1=6, h2hi=3, h2lo=3, logits=1, logit_sb=2, gexp=2, onehot=1, ranks=1,
            routed=1, pos_copied=4, pick_ready=4, gathered=8, slot_done=4, slot_gated=4, x_hi=8, x_lo=8, silu_done=16, hid_done=16,
            hT_done=16, hT_hi=16, hT_lo=16, y_hi=8, y_lo=8, back_done=24, x_added=24)
        L = {name: S(name) for name in per_layer}
        BEFORE = [{name: l * n for name, n in per_layer.items()} for l in range(2)]
        OV = [{name: S(f"{name}{l}") for name in ("flag_ready", "over_load", "over_used", "over_act", "over_hid", "over_tr",
                                                  "over_ht", "over_done", "over_x")} for l in range(2)]
        fox = {name: S(f"fox_{name}") for name in ("wf_loaded", "lp_loaded", "wf_hi", "wf_lo", "f_done", "f_z", "f_exp",
                                                   "logf_ready", "logf_stored", "heads_ready", "off_done", "off_hi", "off_lo")}
        stores_done = S("stores_done")

        W_IN = [A["diff_w_in"][0], A["fox_w_in"][0]]
        W_OUT = [A["diff_w_out"][0], A["fox_w_out"][0]]
        K_CACHE = [A["cache_diff_k"].rearrange("a b s h d -> (a b s) (h d)"), A["cache_fox_k"].rearrange("a b s h d -> (a b s) (h d)")]
        V_CACHE = [A["cache_diff_v"].rearrange("a b s h d -> (a b s) (h d)"), A["cache_fox_v"].rearrange("a b s h d -> (a b s) (h d)")]
        K_OUT = [[A[n].rearrange("a b s h d -> (a b s) (h d)") for n in ("new_diff_k_prompt", "new_diff_k_sample")],
                 [A[n].rearrange("a b s h d -> (a b s) (h d)") for n in ("new_fox_k_prompt", "new_fox_k_sample")]]
        V_OUT = [[A[n].rearrange("a b s h d -> (a b s) (h d)") for n in ("new_diff_v_prompt", "new_diff_v_sample")],
                 [A[n].rearrange("a b s h d -> (a b s) (h d)") for n in ("new_fox_v_prompt", "new_fox_v_sample")]]
        x_p = A["x_prompt"][0]
        x_s = A["x_sample"][0]

        def token_rows(prompt, sample, t):
            return prompt[t * P:(t + 1) * P, :] if t < 2 else sample[0:DEC, :]

        def items():
            for j in range(3 * PAIRS):
                yield j, j // 3, j % 3

        def in_kind(b):
            return "qqkkvvgg"[b]

        def acc(b, t):
            return ps[:, 3 * (b % 2) + t, :]

        def src_proj(w, b, half):
            return w[half * 512:(half + 1) * 512, b * F:(b + 1) * F].rearrange("(k p) n -> p k n", p=P)

        def src_moe(l, e, kind, half):
            name = {"g": "moe_w_gate", "u": "moe_w_up", "d": "moe_w_down"}[kind]
            w = A[name][l]
            w = w[bass.ds(e, 1), :, :]
            n = 512 if kind != "d" else 256
            return w[:, half * n:(half + 1) * n, :].rearrange("e (k p) n -> p (e k) n", p=P)

        def wait_sum(eng, B, name, base, b, t):
            if t < TILES - 1:
                eng.wait_ge(L[name], B[name] + 2 * b + t + 1)
            else:
                eng.wait_ge(units_used, Unit(base, 2 * b + 1).n + 1)

        def wait_matrix(eng, l, order, what, g):
            m0 = 0 if order is FIRST else 2
            eng.wait_ge(units_used, Unit(BASE_MOE[l], 2 * (m0 + order.index(what)) + 1, g).n + 1)

        def raw_view(slot, kind):
            return w_raw[:, slot, :].rearrange("p (k n) -> p k n", n=F if kind != "d" else D)

        block = ctx.enter_context(nc.Block())

        @block.sync
        def _(sp):
            for t in range(TILES):
                sp.dma_start(x[0:ROWS[t], t, :], token_rows(x_p, x_s, t)).then_inc(x_loaded, 16)
            sp.dma_start(cst[:, :], A["c_consts"]).then_inc(const_loaded, 16)
            sp.dma_start(gain[:, 0, :], A["norm_mix"][0, :].partition_broadcast(P)).then_inc(gain_loaded[0][0], 16)

            def load_unit(U, kind, src):
                if U.static >= RAW:
                    sp.wait_ge(units_used, U.n - RAW + 1)
                sp.dma_start(raw_view(U.slot, kind), src).then_inc(raw_ready[U.slot], 16)

            def load_matrices(l, order, m0, g):
                for m, (kind, e) in enumerate(order):
                    for half in range(2):
                        load_unit(Unit(BASE_MOE[l], 2 * (m0 + m) + half, g), kind, src_moe(l, g * PER_GROUP + e, kind, half))

            for l in range(2):
                for b in range(2 * l, IN_BLOCKS[l]):
                    for half in range(2):
                        load_unit(Unit(BASE_IN[l], 2 * b + half), "p", src_proj(W_IN[l], b, half))
                for b in range(OUT_BLOCKS):
                    for half in range(2):
                        load_unit(Unit(BASE_OUT[l], 2 * b + half), "p", src_proj(W_OUT[l], b, half))
                load_matrices(l, FIRST, 0, 0)
                with sp.Fori(0, GROUPS - 1) as g:
                    load_matrices(l, ORDER, 2, g)
                load_matrices(l, LAST, 2, GROUPS - 1)
                if l == 0:
                    for b in range(2):
                        for half in range(2):
                            load_unit(Unit(BASE_IN[1], 2 * b + half), "p", src_proj(W_IN[1], b, half))
                sp.wait_ge(OV[l]["flag_ready"], 1)
                flag_v = sp.value_load(flag[0:1, 0:1])
                with sp.If(flag_v > 0):
                    with sp.Fori(0, EXPERTS) as e:
                        for t in range(TILES):
                            for j, (kind, half) in enumerate([("g", 0), ("g", 1), ("u", 0), ("u", 1), ("d", 0), ("d", 1)]):
                                sp.wait_ge(OV[l]["over_used"], e * 18 + 6 * t + j + 1)
                                sp.dma_start(over_w[:, :].rearrange("p (k n) -> p k n", n=F if kind != "d" else D),
                                             src_moe(l, e, kind, half)).then_inc(OV[l]["over_load"], 16)
                    sp.wait_ge(OV[l]["over_x"], EXPERTS * TILES)
            sp.wait_ge(L["x_added"], 2 * 6 * GROUPS)
            for t in range(TILES):
                sp.dma_start(token_rows(A["y_prompt"][0], A["y_sample"][0], t), x[0:ROWS[t], t, :]).then_inc(stores_done, 16)
            sp.wait_ge(stores_done, 16 * TILES)

        @block.gpsimd
        def _(pool):
            pool.memset(neghalf[:, :], -0.5).then_inc(halves_ready, 1)
            pool.wait_ge(halves_ready, 1)
            small = [
                (gain[:, 1, :], A["norm_ffn"][0, :].partition_broadcast(P)),
                (qk_gain[:, 0, :], A["diff_q_norm"][0, :].partition_broadcast(P)),
                (qk_gain[:, 1, :], A["diff_k_norm"][0, :].partition_broadcast(P)),
                (qk_gain[:, 2, :], A["fox_q_norm"][0, :].partition_broadcast(P)),
                (qk_gain[:, 3, :], A["fox_k_norm"][0, :].partition_broadcast(P)),
                (subln[:, :], A["diff_subln"][0, :].partition_broadcast(P)),
                (lamv[:, 0, :], A["diff_lambda_q1"][0, :].partition_broadcast(P)),
                (lamv[:, 1, :], A["diff_lambda_k1"][0, :].partition_broadcast(P)),
                (lamv[:, 2, :], A["diff_lambda_q2"][0, :].partition_broadcast(P)),
                (lamv[:, 3, :], A["diff_lambda_k2"][0, :].partition_broadcast(P)),
                (b_forget[:, :], A["fox_b_f"][0, :].partition_broadcast(P)),
            ]
            for l in range(2):
                small += [
                    (w_router[:, l, :, 0:4], A["moe_w_group"][l].rearrange("(k p) n -> p k n", p=P)),
                    (w_router[:, l, :, 4:20], A["moe_w_expert"][l].rearrange("(k p) n -> p k n", p=P)),
                    (b_router[:, l, 0:4], A["moe_b_group"][l, :].partition_broadcast(P)),
                    (b_router[:, l, 4:20], A["moe_b_expert"][l, :].partition_broadcast(P)),
                ]
            n_small = len(small)

            def rms(B, squares, done):
                pool.wait_ge(L[squares], B[squares] + TILES)
                link(pool, "pool", pool.tensor_scalar(mean, ss, 1.0 / D, EPS, ALU.mult, ALU.add))
                pool.tensor_tensor(rstd, mean, neghalf[:, 0:TILES], ALU.pow).then_inc(L[done], 1)

            for l in range(2):
                B = BEFORE[l]
                if l == 0:
                    rms(B, "sq0", "rstd0")
                    for dst, src in small:
                        pool.dma_start(dst, src).then_inc(small_loaded, 16)
                else:
                    rms(B, "sq0", "rstd0")
                pool.memset(q_diag[:, :, :], 0.0).then_inc(L["dist_ready"], 1)
                if l == 1:
                    pool.dma_start(w_f[:, :, :], W_IN[1][:, 4 * D:4 * D + FOX_HEADS].rearrange("(k p) n -> p k n", p=P)).then_inc(fox["wf_loaded"], 16)
                    pool.dma_start(logf_past[:, :, :], A["cache_fox_logf"].rearrange("a b (i p) h -> p (a b i) h", p=P)).then_inc(fox["lp_loaded"], 16)

                def load_pair(p):
                    cols = slice(p * P, (p + 1) * P)
                    if p >= 2:
                        pool.wait_ge(L["past_tr"], B["past_tr"] + p - 1)
                    pool.dma_start(k_past[:, p % 2, :, :], K_CACHE[l][:, cols].rearrange("(i p) n -> p i n", p=P)).then_inc(L[f"k_loaded{p % 2}"], 16)
                    if p >= 2:
                        pool.wait_ge(L["pv_done"], B["pv_done"] + 3 * (p - 2) + 3)
                    pool.dma_start(v_past[:, p % 2, :, :], V_CACHE[l][:, cols].rearrange("(i p) n -> p i n", p=P)).then_inc(L[f"v_loaded{p % 2}"], 16)

                load_pair(0)
                load_pair(1)
                if l == 0:
                    pool.wait_ge(L["h_ready0"], B["h_ready0"] + TILES)
                    pool.dma_start(gain[:, 0, :], A["norm_mix"][1, :].partition_broadcast(P)).then_inc(gain_loaded[1][0], 16)
                for b in range(4):
                    pool.wait_ge(L["qk_ms"], B["qk_ms"] + 3 * b + 3)
                    link(pool, "pool", pool.tensor_scalar(ms[b % 2], ms[b % 2], 1.0 / HD, EPS, ALU.mult, ALU.add))
                    pool.tensor_tensor(rr[b % 2], ms[b % 2], neghalf[:, :], ALU.pow).then_inc(L["qk_r"], 1)
                    if b >= 2:
                        for t in range(TILES):
                            pool.wait_ge(L["qk_normed"], B["qk_normed"] + 3 * b + t + 1)
                            out = token_rows(K_OUT[l][0], K_OUT[l][1], t)[:, (b - 2) * F:(b - 1) * F]
                            pool.dma_start(out, qk[0:ROWS[t], b % 2, t, :]).then_inc(L["k_stored"], 16)
                if l == 1:
                    pool.wait_ge(fox["logf_ready"], 1)
                    for t in range(TILES):
                        prompt, sample = (A[n].rearrange("a b s h -> (a b s) h") for n in ("new_fox_logf_prompt", "new_fox_logf_sample"))
                        pool.dma_start(token_rows(prompt, sample, t), logf[0:ROWS[t], t, :]).then_inc(fox["logf_stored"], 16)
                for t in range(TILES):
                    pool.wait_ge(L["v_copied"], B["v_copied"] + 3 + t + 1)
                    pool.dma_start(token_rows(V_OUT[l][0], V_OUT[l][1], t), v_new[0:ROWS[t], t, :]).then_inc(L["v_stored"], 16)
                pool.wait_ge(units_used, Unit(BASE_OUT[l], 0).n)
                if l == 0:
                    pool.dma_start(dist[:, :], A["c_dist"]).then_inc(L["alibi"], 16)
                    pool.wait_ge(L["alibi"], B["alibi"] + 16)
                else:
                    pool.dma_start(bias[:, 1, :], A["c_mask"]).then_inc(L["alibi"], 16)
                for p in range(PAIRS):
                    if l == 0:
                        if p >= 2:
                            pool.wait_ge(L["max_done"], B["max_done"] + 3 * (p - 2) + 3)
                        pool.tensor_scalar(bias[:, p % 2, :], dist[:, :], 2.0 ** -(p + 1), None, ALU.mult).then_inc(L["dist_ready"], 1)
                    if p + 1 >= 2 and p + 1 < PAIRS:
                        load_pair(p + 1)
                if l == 0:
                    for t in range(TILES):
                        pool.wait_ge(L["o_ms"], B["o_ms"] + t + 1)
                        m, r = ms[0][:, 8 * t:8 * t + 8], rr[0][:, 8 * t:8 * t + 8]
                        link(pool, "pool", pool.tensor_scalar(m, m, 1.0 / P, EPS, ALU.mult, ALU.add))
                        link(pool, "pool", pool.tensor_tensor(r, m, neghalf[:, 0:8], ALU.pow))
                        pool.tensor_scalar(r, r, 1.0 - LAMBDA_INIT, None, ALU.mult).then_inc(L["o_r"], 1)
                else:
                    pool.wait_ge(L["scores_done"], B["scores_done"] + 3 * PAIRS)
                    pool.dma_start(gain[:, 1, :], A["norm_ffn"][1, :].partition_broadcast(P)).then_inc(gain_loaded[1][1], 16)
                rms(B, "sq1", "rstd1")
                pool.wait_ge(L["k_stored"], B["k_stored"] + 16 * 2 * TILES)
                pool.wait_ge(L["v_stored"], B["v_stored"] + 16 * TILES)
                if l == 1:
                    pool.wait_ge(fox["logf_stored"], 16 * TILES)
                pool.wait_ge(OV[l]["flag_ready"], 1)
                flag_v = pool.value_load(flag[0:1, 0:1])
                with pool.If(flag_v > 0):
                    pool.wait_ge(OV[l]["over_x"], EXPERTS * TILES)

        @block.scalar
        def _(act):
            A_ = nc.scalar.activation

            def split_hi(U):
                act.wait_ge(raw_ready[U.slot], U.arrivals)
                if U.static >= HI:
                    act.wait_ge(units_used, U.n - HI + 1)
                A_(w_hi[:, U.hslot, :], w_raw[:, U.slot, :], ACT.Copy).then_inc(hi_ready, 1)

            def split_slab(base, k, g=0):
                for half in range(2):
                    split_hi(Unit(base, 2 * k + half, g))

            split_slab(0, 0)
            split_slab(0, 1)
            for l in range(2):
                B = BEFORE[l]
                for t in range(TILES):
                    if l == 0:
                        act.wait_ge(x_loaded, 16 * TILES)
                        act.wait_ge(x_padded, 1)
                    elif t == 0:
                        act.wait_ge(L["x_added"], 6 * GROUPS)
                    A_(h[:, t, :], x[:, t, :], ACT.Square, accum_out=ss[:, t:t + 1]).then_inc(L["sq0"], 1)
                if l == 0:
                    act.wait_ge(lam_dots, 2)
                    A_(lamw[:, 2:4], lamw[:, 0:2], ACT.Exp).then_inc(lam_exps, 1)
                for i in range(2 * TILES):
                    t, half = divmod(i, 2)
                    act.wait_ge(L["tr0"], B["tr0"] + i + 1)
                    A_(hT_hi[:, 4 * half:4 * half + 4, t * P:(t + 1) * P], ps[:, i, :].rearrange("p (k n) -> p k n", k=4), ACT.Copy).then_inc(L["hi0"], 1)
                if l == 1:
                    act.wait_ge(fox["wf_loaded"], 16)
                    A_(w_f_hi[:, :, :], w_f[:, :, :], ACT.Copy).then_inc(fox["wf_hi"], 1)
                    act.wait_ge(fox["f_z"], 1)
                    A_(lf[:, 2, :], lf[:, 1, :], ACT.Exp, scale=-1.0).then_inc(fox["f_exp"], 1)
                    act.wait_ge(fox["off_done"], 1)
                    A_(off_hi[:, 0:320], ps[0:FOX_HEADS, 7, 0:320], ACT.Copy, scale=-1.0 / SCALE).then_inc(fox["off_hi"], 1)
                    A_(off_hi[:, 320:832], ps[0:FOX_HEADS, 6, 0:512], ACT.Copy, scale=1.0 / SCALE).then_inc(fox["off_hi"], 1)

                def evacuate_qk(b):
                    for t in range(TILES):
                        i = 3 * b + t
                        act.wait_ge(L["qk_tr"], B["qk_tr"] + i + 1)
                        bank = ps[:, 6 + i % 2, :].rearrange("p (k n) -> p k n", k=4)
                        pr = slice(4 * (b % 2), 4 * (b % 2) + 4)
                        if b < 2 and t < 2:
                            A_(qT[:, pr, t * P:(t + 1) * P], bank, ACT.Copy).then_inc(L["qk_evac"], 1)
                        elif b < 2:
                            act.wait_ge(L["dist_ready"], B["dist_ready"] + 1)
                            A_(q_diag[0:HD, pr, 0:DEC], bank[0:HD, :, 0:DEC], ACT.Copy)
                            A_(q_diag[HD:P, pr, DEC:P], bank[HD:P, :, 0:DEC], ACT.Copy).then_inc(L["qk_evac"], 1)
                        else:
                            n = ROWS[t]
                            A_(kT_new[:, pr, t * P:t * P + n], bank[:, :, 0:n], ACT.Copy).then_inc(L["qk_evac"], 1)

                for b in range(IN_BLOCKS[l]):
                    kind = in_kind(b)
                    split_slab(BASE_IN[l], b + 2)
                    for t in range(TILES):
                        wait_sum(act, B, "proj_done", BASE_IN[l], b, t)
                        if kind in "qk":
                            if b >= 2:
                                act.wait_ge(L["qk_tr"], B["qk_tr"] + 3 * (b - 2) + t + 1)
                            A_(qk[:, b % 2, t, :], acc(b, t), ACT.Square).then_inc(L["qk_sq"], 1)
                        elif kind == "v":
                            A_(v_new[:, t, (b - 4) * F:(b - 3) * F], acc(b, t), ACT.Copy).then_inc(L["v_copied"], 1)
                        else:
                            if b == 6 and t == 0:
                                act.wait_ge(L["qk_tr"], B["qk_tr"] + 12)
                                act.wait_ge(L["k_stored"], B["k_stored"] + 16 * 2 * TILES)
                            A_(gate[:, t, (b - 6) * F:(b - 5) * F], acc(b, t), ACT.Exp, scale=-1.0).then_inc(L["g_exp"], 1)
                    if 1 <= b <= 4:
                        evacuate_qk(b - 1)

                def past_keys(p):
                    act.wait_ge(L["past_tr"], B["past_tr"] + p + 1)
                    A_(kT_past[:, p % 2, :], ps[:, 5, :], ACT.Copy).then_inc(L["past_ev"], 1)

                def exps(j, t):
                    act.wait_ge(L["neg_done"], B["neg_done"] + j + 1)
                    n = KEYS[t]
                    for c in range(2 if t < 2 else 1):
                        s = probs[:, j % 3, c * n:(c + 1) * n]
                        ins = A_(s, s, ACT.Exp, bias=nmx[:, j % 3, c:c + 1], scale=SCALE, accum_out=sm[:, j % 3, c:c + 1])
                    ins.then_inc(L["exp_done"], 1)

                def copy_dT(j, t):
                    act.wait_ge(L["dT_done"], B["dT_done"] + j + 1)
                    if t < 2:
                        n = KEYS[t] * (1 if l == 0 else 2)
                        A_(dT[:, j % 2, 0:n], ps[:, 4, 0:n], ACT.Copy).then_inc(L["dT_copied"], 1)
                    else:
                        q = DEC if l == 0 else P
                        A_(dT[:, j % 2, 0:4 * q], ps[:, 4, 0:4 * q], ACT.Copy)
                        last = ps[0:DEC, 7, 0:q]
                        A_(dT[0:DEC, j % 2, 4 * q:5 * q], last, ACT.Copy).then_inc(L["dT_copied"], 1)

                its = list(items())
                past_keys(0)
                for j, p, t in its:
                    exps(j, t)
                    if t == 0 and p + 1 < PAIRS:
                        past_keys(p + 1)
                    if j >= 1:
                        copy_dT(j - 1, its[j - 1][2])
                copy_dT(its[-1][0], its[-1][2])
                if l == 0:
                    for t in range(TILES):
                        act.wait_ge(L["o_done"], B["o_done"] + 3 * PAIRS)
                        if t >= 2:
                            act.wait_ge(L["o_ms"], B["o_ms"] + t - 1)
                        A_(o_sq[:, t % 2, :], o[:, t, :], ACT.Square).then_inc(L["o_sqd"], 1)
                for i in range(2 * TILES):
                    t, half = divmod(i, 2)
                    act.wait_ge(L["o_tr"], B["o_tr"] + i + 1)
                    A_(oT_hi[:, 4 * half:4 * half + 4, t * P:(t + 1) * P], ps[:, i, :].rearrange("p (k n) -> p k n", k=4), ACT.Copy).then_inc(L["o_hi"], 1)
                for b in range(OUT_BLOCKS):
                    split_slab(BASE_OUT[l], b + 2)

                for t in range(TILES):
                    act.wait_ge(L["x_mid"], B["x_mid"] + TILES * OUT_BLOCKS)
                    if t == 0:
                        act.wait_ge(L["k_stored"], B["k_stored"] + 16 * 2 * TILES)
                        act.wait_ge(L["v_stored"], B["v_stored"] + 16 * TILES)
                        if l == 1:
                            act.wait_ge(fox["logf_stored"], 16 * TILES)
                    A_(h2[:, t, :], x[:, t, :], ACT.Square, accum_out=ss[:, t:t + 1]).then_inc(L["sq1"], 1)
                for i in range(2 * TILES):
                    t, half = divmod(i, 2)
                    act.wait_ge(L["tr1"], B["tr1"] + i + 1)
                    A_(h2T[:, 4 * half:4 * half + 4, t * P:(t + 1) * P], ps[:, i, :].rearrange("p (k n) -> p k n", k=4), ACT.Copy).then_inc(L["ev1"], 1)
                for t in range(TILES):
                    A_(h2_hi[:, t, :], h2[:, t, :], ACT.Copy).then_inc(L["h2hi"], 1)
                act.wait_ge(L["logit_sb"], B["logit_sb"] + 1)
                A_(ge, gd, ACT.Exp).then_inc(L["gexp"], 1)
                act.wait_ge(L["logit_sb"], B["logit_sb"] + 2)
                A_(e2, dv, ACT.Exp).then_inc(L["gexp"], 1)

                def silu(order, e, g):
                    wait_matrix(act, l, order, ("g", e), g)
                    if order is not FIRST:
                        act.wait_ge(L["hid_done"], B["hid_done"] + g * 4 + e)
                    A_(act_g[:, :], ps[:, 0, :], ACT.Silu).then_inc(L["silu_done"], 1)

                def hidden_hi(e, g):
                    act.wait_ge(L["hT_done"], B["hT_done"] + g * 4 + e + 1)
                    A_(hidT_hi[:, :, :].rearrange("p k n -> p (k n)"), ps[:, 2, :], ACT.Copy).then_inc(L["hT_hi"], 1)

                def gathered_hi(g):
                    for i in range(2):
                        act.wait_ge(L["gathered"], B["gathered"] + g * 2 + i + 1)
                        A_(xT_hi[:, 4 * i:4 * i + 4, :].rearrange("p k n -> p (k n)"), ps[:, 5 + i, :], ACT.Copy).then_inc(L["x_hi"], 1)

                def moe_round(order, g):
                    last = order is LAST
                    for m, (kind, e) in enumerate(order):
                        ahead = not (last and m >= len(order) - 2 and l == 1)
                        if ahead:
                            split_hi(Unit(BASE_MOE[l], 2 * (m + 4), g))
                        if kind == "g":
                            silu(order, e, g)
                        if (kind, e) in (("g", 1), ("g", 2), ("g", 3)):
                            hidden_hi(e - 1, g)
                        if (kind, e) == ("u", 3) and not last:
                            gathered_hi(g + 1)
                        if (kind, e) == ("d", 2):
                            hidden_hi(3, g)
                        if (kind, e) == ("d", 3):
                            wait_matrix(act, l, order, ("d", 3), g)
                            for i in range(2):
                                A_(y_hi[:, i * F:(i + 1) * F], ps[:, 3 + i, :], ACT.Copy).then_inc(L["y_hi"], 1)
                        if ahead:
                            split_hi(Unit(BASE_MOE[l], 2 * (m + 4) + 1, g))

                gathered_hi(0)
                silu(FIRST, 0, 0)
                split_slab(BASE_MOE[l], 2)
                split_slab(BASE_MOE[l], 3)
                with act.Fori(0, GROUPS - 1) as g:
                    moe_round(ORDER, g)
                moe_round(LAST, GROUPS - 1)

                act.wait_ge(OV[l]["flag_ready"], 1)
                flag_v = act.value_load(flag[0:1, 0:1])
                with act.If(flag_v > 0):
                    with act.Fori(0, EXPERTS) as e:
                        for t in range(TILES):
                            act.wait_ge(OV[l]["over_used"], e * 18 + 6 * t + 3)
                            A_(act_g[:, :], ps[:, 0, :], ACT.Silu).then_inc(OV[l]["over_act"], 1)
                            act.wait_ge(OV[l]["over_tr"], e * TILES + t + 1)
                            A_(over_hT[:, :], ps[:, 2, :], ACT.Copy).then_inc(OV[l]["over_ht"], 1)
                            act.wait_ge(OV[l]["over_x"], e * TILES + t + 1)

        @block.tensor
        def _(pe):
            mm, tr = nc.tensor.matmul, nc.tensor.transpose

            def split_mm(out, a_hi, a_lo, b_hi, b_lo, start, stop):
                mm(out, a_hi, b_hi, start=start, stop=False)
                mm(out, a_hi, b_lo, start=False, stop=False)
                return mm(out, a_lo, b_hi, start=False, stop=stop)

            def unit_parts(U, n):
                hi = w_hi[:, U.hslot, :].rearrange("p (k n) -> p k n", n=n)
                lo = w_lo[:, U.slot, :].rearrange("p (k n) -> p k n", n=n)
                return hi, lo

            def transposes(B, src, ready, done, counts=(1, 2, 3)):
                for i in range(2 * TILES):
                    t, half = divmod(i, 2)
                    pe.wait_ge(L[ready], B[ready] + counts[t])
                    for k in range(4):
                        c = (4 * half + k) * P
                        ins = tr(ps[:, i, k * P:(k + 1) * P], src[:, t, c:c + P], ident)
                    ins.then_inc(L[done], 1)

            def project(B, base, b, a_hi, a_lo, low, done, free):
                for half in range(2):
                    U = Unit(base, 2 * b + half)
                    pe.wait_ge(lo_ready, U.n + 1)
                    hi, lo = unit_parts(U, F)
                    for t in range(TILES):
                        if b == 0:
                            pe.wait_ge(L[low], B[low] + 2 * t + half + 1)
                        if half == 0:
                            free(b, t)
                        for k in range(4):
                            kb = 4 * half + k
                            ts = slice(t * P, (t + 1) * P)
                            ins = split_mm(acc(b, t), a_hi[:, kb, ts], a_lo[:, kb, ts], hi[:, k, :], lo[:, k, :],
                                           start=(kb == 0), stop=(kb == KB - 1))
                        if half == 1 and t < TILES - 1:
                            ins.then_inc(L[done], 1)
                    ins.then_inc(units_used, 1)

            pe.wait_ge(const_loaded, 16)
            for l in range(2):
                B = BEFORE[l]
                transposes(B, h, "h_ready0", "tr0")
                if l == 1:
                    pe.wait_ge(fox["wf_lo"], 1)
                    pe.wait_ge(L["lo0"], B["lo0"] + 2 * TILES)
                    for t in range(TILES):
                        for kb in range(KB):
                            ts = slice(t * P, (t + 1) * P)
                            ins = split_mm(ps[:, 7, t * 16:(t + 1) * 16], hT_hi[:, kb, ts], hT_lo[:, kb, ts],
                                           w_f_hi[:, kb, :], w_f_lo[:, kb, :], start=(kb == 0), stop=(kb == KB - 1))
                    ins.then_inc(fox["f_done"], 1)
                    pe.wait_ge(fox["logf_ready"], 1)
                    pe.wait_ge(fox["lp_loaded"], 16)
                    off = ps[0:FOX_HEADS, 7, :]
                    mm(off[:, 0:128], logf[:, 0, :], tri, start=True, stop=True)
                    mm(off[:, 128:256], logf[:, 0, :], ones, start=True, stop=False)
                    mm(off[:, 128:256], logf[:, 1, :], tri, start=False, stop=True)
                    mm(off[:, 256:320], logf[0:DEC, 2, :], tri[0:DEC, 0:DEC], start=True, stop=True)
                    for i in range(PTILES):
                        out = ps[0:FOX_HEADS, 6, i * P:(i + 1) * P]
                        ins = mm(out, logf_past[:, i, :], after, start=True, stop=(i == PTILES - 1))
                        for k in range(i + 1, PTILES):
                            ins = mm(out, logf_past[:, k, :], ones, start=False, stop=(k == PTILES - 1))
                    ins.then_inc(fox["off_done"], 1)

                def free_in(b, t):
                    if b >= 2:
                        if in_kind(b - 2) in "qk":
                            pe.wait_ge(L["qk_n1"], B["qk_n1"] + 3 * (b - 2) + t + 1)
                        else:
                            pe.wait_ge(L["v_copied"], B["v_copied"] + 3 * (b - 6) + t + 1)

                def transpose_qk(b):
                    for t in range(TILES):
                        i = 3 * b + t
                        pe.wait_ge(L["qk_normed"], B["qk_normed"] + i + 1)
                        if i >= 2:
                            pe.wait_ge(L["qk_evac"], B["qk_evac"] + i - 1)
                        elif l == 1:
                            pe.wait_ge(fox["off_lo"], 2)
                        for k in range(4):
                            ins = tr(ps[:, 6 + i % 2, k * P:(k + 1) * P], qk[:, b % 2, t, k * P:(k + 1) * P], ident)
                        ins.then_inc(L["qk_tr"], 1)

                for b in range(IN_BLOCKS[l]):
                    project(B, BASE_IN[l], b, hT_hi, hT_lo, "lo0", "proj_done", free_in)
                    if 1 <= b <= 4:
                        transpose_qk(b - 1)

                its = list(items())

                def past_keys(p):
                    pe.wait_ge(L[f"k_loaded{p % 2}"], B["k_loaded0"] + 16 * (p // 2 + 1))
                    if p == 0:
                        (pe.wait_ge(L["v_copied"], B["v_copied"] + 6) if l == 0 else pe.wait_ge(L["g_exp"], B["g_exp"] + 6))
                    else:
                        pe.wait_ge(L["past_ev"], B["past_ev"] + p)
                    for i in range(PTILES):
                        ins = tr(ps[:, 5, i * P:(i + 1) * P], k_past[:, p % 2, i, :], ident)
                    ins.then_inc(L["past_tr"], 1)

                def offsets(out, head, n, width, a, stop=True):
                    if width == P:
                        sel = ident_r[0:FOX_HEADS, head:head + 1].to_broadcast([FOX_HEADS, P])
                    else:
                        sel = pick_heads[:, head // 2, :]
                    mm(out, sel, off_hi[:, a:a + n], start=False, stop=False)
                    return mm(out, sel, off_lo[:, a:a + n], start=False, stop=True)

                def scores(j, p, t):
                    s = 2 * (j % 2)
                    if j >= 2:
                        pe.wait_ge(L["max_done"], B["max_done"] + j - 1)
                    fx = l == 1
                    if t < 2:
                        n = KEYS[t]
                        for c in range(2):
                            out = ps[:, s + c, 0:n]
                            cs = slice(c * HD, (c + 1) * HD)
                            ins = mm(out, qT[cs, p, t * P:(t + 1) * P], kT_new[cs, p, 0:n], start=True, stop=not fx)
                            if fx:
                                ins = offsets(out, 2 * p + c, n, P, 0)
                    else:
                        pe.wait_ge(L["past_ev"], B["past_ev"] + p + 1)
                        ins = mm(ps[:, s, :], q_diag[:, p, :], kT_past[:, p % 2, :], start=True, stop=not fx)
                        if fx:
                            offsets(ps[:, s, :], 2 * p, PAST, DEC, 320)
                        ins = mm(ps[:, s + 1, 0:DEC], q_diag[:, p, :], kT_new[:, p, SEQ:SEQ + DEC], start=True, stop=not fx)
                        if fx:
                            ins = offsets(ps[:, s + 1, 0:DEC], 2 * p, DEC, DEC, 256)
                    ins.then_inc(L["scores_done"], 1)

                def probs_T(j, p, t):
                    pe.wait_ge(L["diag_done"], B["diag_done"] + j + 1)
                    if j >= 1:
                        pe.wait_ge(L["dT_copied"], B["dT_copied"] + j)
                    pr = probs[:, j % 3, :]
                    dg = diag[:, j % 2, :]
                    if t < 2:
                        n = KEYS[t]
                        nb = n // P
                        for kb in range(nb):
                            for c in range(2):
                                lhs = pr[:, c * n + kb * P:c * n + (kb + 1) * P]
                                if l == 0:
                                    ins = mm(ps[:, 4, kb * P:(kb + 1) * P], lhs, dg[:, c * P:(c + 1) * P], start=(c == 0), stop=(c == 1))
                                else:
                                    a = (c * nb + kb) * P
                                    ins = mm(ps[:, 4, a:a + P], lhs, dg[:, c * P:(c + 1) * P], start=True, stop=True)
                    else:
                        q = DEC if l == 0 else P
                        for kb in range(PTILES):
                            mm(ps[:, 4, kb * q:(kb + 1) * q], pr[:, kb * P:(kb + 1) * P], dg[:, 0:q], start=True, stop=True)
                        ins = mm(ps[0:DEC, 7, 0:q], pr[:, PAST:PAST + DEC], dg[:, 0:q], start=True, stop=True)
                    ins.then_inc(L["dT_done"], 1)

                def values(j, p, t):
                    pe.wait_ge(L["dT_copied"], B["dT_copied"] + j + 1)
                    if j >= 1:
                        pe.wait_ge(L["o_done"], B["o_done"] + j)
                    if t == 2:
                        pe.wait_ge(L[f"v_loaded{p % 2}"], B["v_loaded0"] + 16 * (p // 2 + 1))
                    d = dT[:, j % 2, :]
                    col = p * P
                    members = [(0, P)] if l == 0 else [(0, HD), (HD, HD)]
                    for m, (c0, w) in enumerate(members):
                        out = ps[0:ROWS[t], 6, c0:c0 + w]
                        if t < 2:
                            nb = KEYS[t] // P
                            for kb in range(nb):
                                a = (m * nb + kb) * P
                                ins = mm(out, d[:, a:a + P], v_new[:, kb, col + c0:col + c0 + w], start=(kb == 0), stop=(kb == nb - 1))
                        else:
                            q = DEC if l == 0 else P
                            for kb in range(PTILES):
                                mm(out, d[:, kb * q + m * DEC:kb * q + m * DEC + DEC], v_past[:, p % 2, kb, c0:c0 + w], start=(kb == 0), stop=False)
                            ins = mm(out, d[0:DEC, PTILES * q + m * DEC:PTILES * q + m * DEC + DEC],
                                     v_new[0:DEC, 2, col + c0:col + c0 + w], start=False, stop=True)
                    ins.then_inc(L["pv_done"], 1)

                pe.wait_ge(L["qk_evac"], B["qk_evac"] + 12)
                past_keys(0)
                if l == 1:
                    pe.wait_ge(L["g_exp"], B["g_exp"] + 6)
                else:
                    pe.wait_ge(L["v_copied"], B["v_copied"] + 6)
                if l == 1:
                    pe.wait_ge(fox["heads_ready"], 1)
                scores(*its[0])
                scores(*its[1])
                for j, p, t in its:
                    if t == 0 and p + 1 < PAIRS:
                        past_keys(p + 1)
                    if j + 2 < len(its):
                        scores(*its[j + 2])
                    probs_T(j, p, t)
                    if j >= 1:
                        values(*its[j - 1])
                values(*its[-1])

                if l == 0:
                    transposes(B, o, "o_normed", "o_tr")
                else:
                    transposes(B, o, "o_done", "o_tr", counts=(3 * PAIRS,) * 3)

                def free_out(b, t):
                    pass

                for b in range(OUT_BLOCKS):
                    project(B, BASE_OUT[l], b, oT_hi, oT_lo, "o_lo", "out_done", free_out)

                transposes(B, h2, "h_ready1", "tr1")
                pe.wait_ge(L["ev1"], B["ev1"] + 2 * TILES)
                for t in range(TILES):
                    for kb in range(KB):
                        ins = mm(ps[:, 6, t * 20:(t + 1) * 20], h2T[:, kb, t * P:(t + 1) * P], w_router[:, l, kb, :],
                                 start=(kb == 0), stop=(kb == KB - 1))
                ins.then_inc(L["logits"], 1)
                pe.wait_ge(L["onehot"], B["onehot"] + 1)
                ohv = oh
                for t in range(TILES):
                    for s in range(t):
                        mm(ps[:, 7, 4 * t:4 * t + 4], ones, ohv[:, s, :], start=(s == 0), stop=False)
                    mm(ps[:, 7, 4 * t:4 * t + 4], before, ohv[:, t, :], start=(t == 0), stop=True)
                for s in range(TILES):
                    ins = mm(ps[:, 7, 12:16], ones, ohv[:, s, :], start=(s == 0), stop=(s == TILES - 1))
                ins.then_inc(L["ranks"], 1)
                pe.wait_ge(L["h2lo"], B["h2lo"] + TILES)
                pe.wait_ge(L["routed"], B["routed"] + 1)

                def gather(g):
                    pe.wait_ge(L["pick_ready"], B["pick_ready"] + g + 1)
                    for i in range(2):
                        for k in range(4):
                            kb = 4 * i + k
                            for t in range(TILES):
                                for part, src in enumerate((h2_hi, h2_lo)):
                                    ins = mm(ps[:, 5 + i, k * P:(k + 1) * P], src[:, t, kb * P:(kb + 1) * P], pick[:, t, :],
                                             start=(t == 0 and part == 0), stop=(t == TILES - 1 and part == 1))
                        ins.then_inc(L["gathered"], 1)
                    for t in range(TILES):
                        mm(ps[:, 7, 384:392], pick[:, t, :], gates_hl[:, t, :], start=(t == 0), stop=(t == TILES - 1))
                    for t in range(TILES):
                        ins = tr(ps[:, 7, t * P:(t + 1) * P], pick[:, t, :].bitcast(F32), ident)
                    ins.then_inc(L["slot_done"], 1)

                def into(m, bank, g):
                    for half in range(2):
                        U = Unit(BASE_MOE[l], 2 * m + half, g)
                        pe.wait_ge(lo_ready, U.n + 1)
                        hi, lo = unit_parts(U, F)
                        for k in range(4):
                            kb = 4 * half + k
                            ins = split_mm(ps[:, bank, :], xT_hi[:, kb, :], xT_lo[:, kb, :], hi[:, k, :], lo[:, k, :],
                                           start=(kb == 0), stop=(kb == KB - 1))
                        ins.then_inc(units_used, 1)

                def down(m, e, g):
                    pe.wait_ge(L["hT_lo"], B["hT_lo"] + g * 4 + e + 1)
                    for half in range(2):
                        U = Unit(BASE_MOE[l], 2 * m + half, g)
                        pe.wait_ge(lo_ready, U.n + 1)
                        hi, lo = unit_parts(U, D)
                        for k in range(2):
                            fb = 2 * half + k
                            for c in range(2):
                                cs = slice(c * F, (c + 1) * F)
                                ins = split_mm(ps[:, 3 + c, :], hidT_hi[:, fb, :], hidT_lo[:, fb, :], hi[:, k, cs], lo[:, k, cs],
                                               start=(e == 0 and fb == 0), stop=(e == 3 and fb == 3))
                        ins.then_inc(units_used, 1)

                def hidden_T(e, g):
                    pe.wait_ge(L["hid_done"], B["hid_done"] + g * 4 + e + 1)
                    for k in range(4):
                        ins = tr(ps[:, 2, k * P:(k + 1) * P], hid[:, k * P:(k + 1) * P], ident)
                    ins.then_inc(L["hT_done"], 1)

                def back(g):
                    pe.wait_ge(L["y_lo"], B["y_lo"] + g * 2 + 2)
                    for i in range(2 * TILES):
                        t, c = divmod(i, 2)
                        if i >= 4:
                            pe.wait_ge(L["x_added"], B["x_added"] + g * 6 + i - 3)
                        cs = slice(c * F, (c + 1) * F)
                        mm(ps[:, BACK[i], :], pickT[:, t, :], y_hi[:, cs], start=True, stop=False)
                        mm(ps[:, BACK[i], :], pickT[:, t, :], y_lo[:, cs], start=False, stop=True).then_inc(L["back_done"], 1)

                def moe_round(order, g):
                    last = order is LAST
                    for m, (kind, e) in enumerate(order):
                        if kind == "g":
                            pe.wait_ge(L["silu_done"], B["silu_done"] + g * 4 + e)
                            if e == PER_GROUP:
                                pe.wait_ge(L["x_lo"], B["x_lo"] + g * 2 + 4)
                            into(2 + m, 0, g)
                        elif kind == "u":
                            into(2 + m, 1, g)
                        else:
                            down(2 + m, e, g)
                        if (kind, e) in (("g", 1), ("g", 2), ("g", 3)):
                            hidden_T(e - 1, g)
                        if (kind, e) == ("u", 3) and not last:
                            gather(g + 1)
                        if (kind, e) == ("d", 2):
                            hidden_T(3, g)
                    back(g)

                gather(0)
                pe.wait_ge(L["x_lo"], B["x_lo"] + 2)
                into(0, 0, 0)
                into(1, 1, 0)
                with pe.Fori(0, GROUPS - 1) as g:
                    moe_round(ORDER, g)
                moe_round(LAST, GROUPS - 1)

                pe.wait_ge(OV[l]["flag_ready"], 1)
                flag_v = pe.value_load(flag[0:1, 0:1])
                with pe.If(flag_v > 0):
                    pe.sem_inc(OV[l]["over_used"], 1)
                    with pe.Fori(0, EXPERTS) as e:
                        for t in range(TILES):
                            ts = slice(t * P, (t + 1) * P)
                            wf = over_w[:, :].rearrange("p (k n) -> p k n", n=F)
                            wd = over_w[:, :].rearrange("p (k n) -> p k n", n=D)
                            for j in range(4):
                                pe.wait_ge(OV[l]["over_load"], e * 288 + 16 * (6 * t + j + 1))
                                bank, half = divmod(j, 2)
                                for k in range(4):
                                    kb = 4 * half + k
                                    ins = mm(ps[:, bank, :], h2T[:, kb, ts], wf[:, k, :], start=(kb == 0), stop=(kb == KB - 1))
                                ins.then_inc(OV[l]["over_used"], 1)
                            pe.wait_ge(OV[l]["over_hid"], e * TILES + t + 1)
                            for k in range(4):
                                ins = tr(ps[:, 2, k * P:(k + 1) * P], hid[:, k * P:(k + 1) * P], ident)
                            ins.then_inc(OV[l]["over_tr"], 1)
                            pe.wait_ge(OV[l]["over_ht"], e * TILES + t + 1)
                            for j in range(2):
                                pe.wait_ge(OV[l]["over_load"], e * 288 + 16 * (6 * t + 4 + j + 1))
                                for k in range(2):
                                    fb = 2 * j + k
                                    for c in range(2):
                                        ins = mm(ps[:, 3 + c, :], over_hT[:, fb * P:(fb + 1) * P], wd[:, k, c * F:(c + 1) * F],
                                                 start=(fb == 0), stop=(fb == 3))
                                ins.then_inc(OV[l]["over_used"], 1)
                            pe.wait_ge(OV[l]["over_x"], e * TILES + t + 1)

        @block.vector
        def _(dve):
            v = nc.vector

            def split_lo(U):
                dve.wait_ge(hi_ready, U.n + 1)
                v.tensor_tensor(w_lo[:, U.slot, :], w_raw[:, U.slot, :], w_hi[:, U.hslot, :].bitcast(F32), ALU.subtract).then_inc(lo_ready, 1)

            def split_slab(base, k, g=0):
                for half in range(2):
                    split_lo(Unit(base, 2 * k + half, g))

            def norm(B, rstd_name, which, l, dst, done):
                dve.wait_ge(L[rstd_name], B[rstd_name] + 1)
                for t in range(TILES):
                    v.scalar_tensor_tensor(dst[:, t, :], x[:, t, :], rstd[:, t:t + 1], gain[:, which, :], ALU.mult, ALU.mult).then_inc(L[done], 1)

            v.memset(x[DEC:P, 2, :], 0.0).then_inc(x_padded, 1)
            split_slab(0, 0)
            split_slab(0, 1)
            for l in range(2):
                B = BEFORE[l]
                if l == 0:
                    dve.wait_ge(gain_loaded[0][0], 16)
                    norm(B, "rstd0", 0, l, h, "h_ready0")
                    n_small = 19
                    dve.wait_ge(small_loaded, 16 * n_small)
                    for i in range(2):
                        v.tensor_tensor_reduce(lamv[:, 2 * i, :], lamv[:, 2 * i, :], lamv[:, 2 * i + 1, :], 1.0, 0.0,
                                               ALU.mult, ALU.add, lamw[:, i:i + 1]).then_inc(lam_dots, 1)
                    dve.wait_ge(lam_exps, 1)
                    link(dve, "dve", v.tensor_tensor(lamw[:, 4:5], lamw[:, 3:4], lamw[:, 2:3], ALU.subtract))
                    link(dve, "dve", v.tensor_scalar(lamw[:, 5:6], lamw[:, 4:5], -LAMBDA_INIT, None, ALU.add))
                    dve.wait_ge(const_loaded, 16)
                    link(dve, "dve", v.tensor_copy(lamw[0:HD, 6:7], ones[0:HD, 0:1]))
                    link(dve, "dve", v.tensor_copy(lamw[HD:P, 6:7], lamw[HD:P, 5:6]))
                    link(dve, "dve", v.tensor_tensor(ident2[:, :], ident[:, 0:HD], ident[:, HD:P], ALU.add))
                    link(dve, "dve", v.tensor_copy(ident_r[:, :], ident[:, 0:FOX_HEADS]))
                else:
                    dve.wait_ge(gain_loaded[1][0], 16)
                    norm(B, "rstd0", 0, l, h, "h_ready0")
                for i in range(2 * TILES):
                    t, half = divmod(i, 2)
                    dve.wait_ge(L["hi0"], B["hi0"] + i + 1)
                    a, b_ = slice(4 * half, 4 * half + 4), slice(t * P, (t + 1) * P)
                    v.tensor_tensor(hT_lo[:, a, b_], ps[:, i, :].rearrange("p (k n) -> p k n", k=4), hT_hi[:, a, b_].bitcast(F32),
                                    ALU.subtract).then_inc(L["lo0"], 1)
                if l == 1:
                    dve.wait_ge(fox["wf_hi"], 1)
                    v.tensor_tensor(w_f_lo[:, :, :], w_f[:, :, :], w_f_hi[:, :, :].bitcast(F32), ALU.subtract).then_inc(fox["wf_lo"], 1)
                    dve.wait_ge(fox["f_done"], 1)
                    z, az, e, s, s2, q, m0 = (lf[:, i, :] for i in range(7))
                    z3 = z.rearrange("p (t h) -> p t h", t=3)
                    link(dve, "dve", v.tensor_tensor(z3, ps[:, 7, 0:48].rearrange("p (t h) -> p t h", t=3),
                                                     b_forget[:, :].unsqueeze(1).to_broadcast([P, 3, 16]), ALU.add))
                    link(dve, "dve", v.tensor_scalar(m0, z, -1.0, None, ALU.mult))
                    v.tensor_tensor(az, z, m0, ALU.max).then_inc(fox["f_z"], 1)
                    dve.wait_ge(fox["f_exp"], 1)
                    link(dve, "dve", v.tensor_scalar(m0, z, 0.0, None, ALU.min))
                    link(dve, "dve", v.tensor_scalar(q, e, 2.0, None, ALU.add))
                    link(dve, "dve", v.reciprocal(s2, q))
                    link(dve, "dve", v.tensor_tensor(s, e, s2, ALU.mult))
                    link(dve, "dve", v.tensor_tensor(s2, s, s, ALU.mult))
                    link(dve, "dve", v.tensor_scalar(q, s2, 1.0 / 17, 1.0 / 15, ALU.mult, ALU.add))
                    for n in (13, 11, 9, 7, 5, 3, 1):
                        link(dve, "dve", v.tensor_tensor(q, q, s2, ALU.mult))
                        link(dve, "dve", v.tensor_scalar(q, q, 1.0 / n, None, ALU.add))
                    link(dve, "dve", v.tensor_tensor(q, q, s, ALU.mult))
                    v.scalar_tensor_tensor(logf[:, :, :].rearrange("p t h -> p (t h)"), q, -2.0, m0, ALU.mult, ALU.add).then_inc(fox["logf_ready"], 1)
                    dve.wait_ge(fox["off_hi"], 1)
                    v.scalar_tensor_tensor(off_lo[:, 0:320], ps[0:FOX_HEADS, 7, 0:320], -1.0 / SCALE, off_hi[:, 0:320].bitcast(F32),
                                           ALU.mult, ALU.subtract).then_inc(fox["off_lo"], 1)
                    dve.wait_ge(fox["off_hi"], 2)
                    v.scalar_tensor_tensor(off_lo[:, 320:832], ps[0:FOX_HEADS, 6, 0:512], 1.0 / SCALE, off_hi[:, 320:832].bitcast(F32),
                                           ALU.mult, ALU.subtract).then_inc(fox["off_lo"], 1)

                for b in range(IN_BLOCKS[l]):
                    kind = in_kind(b)
                    split_slab(BASE_IN[l], b + 2)
                    if kind in "qk":
                        gn = qk_gain[:, 2 * l + b // 2, :].unsqueeze(1).to_broadcast([P, 8, HD])
                        for t in range(TILES):
                            dve.wait_ge(L["qk_sq"], B["qk_sq"] + 3 * b + t + 1)
                            v.tensor_reduce(ms[b % 2][:, 8 * t:8 * t + 8], qk[:, b % 2, t, :].rearrange("p (n d) -> p n d", d=HD), AX, ALU.add).then_inc(L["qk_ms"], 1)
                        dve.wait_ge(L["qk_r"], B["qk_r"] + b + 1)
                        for t in range(TILES):
                            v.tensor_tensor(qk[:, b % 2, t, :].rearrange("p (n d) -> p n d", d=HD), acc(b, t).rearrange("p (n d) -> p n d", d=HD),
                                            rr[b % 2][:, 8 * t:8 * t + 8].unsqueeze(2).to_broadcast([P, 8, HD]), ALU.mult).then_inc(L["qk_n1"], 1)
                        for t in range(TILES):
                            dve.wait_ge(L["qk_n1"], B["qk_n1"] + 3 * b + t + 1)
                            vw = qk[:, b % 2, t, :].rearrange("p (n d) -> p n d", d=HD)
                            v.tensor_tensor(vw, vw, gn, ALU.mult).then_inc(L["qk_normed"], 1)
                    elif kind == "g":
                        for t in range(TILES):
                            dve.wait_ge(L["g_exp"], B["g_exp"] + 3 * (b - 6) + t + 1)
                            gv = gate[:, t, (b - 6) * F:(b - 5) * F]
                            link(dve, "dve", v.tensor_scalar(gv, gv, 1.0, None, ALU.add))
                            v.reciprocal(gv, gv).then_inc(L["g_done"], 1)

                its = list(items())
                v.memset(o[DEC:P, 2, :], 0.0).then_inc(L["o_zeroed"], 1)

                def row_max(j, p, t):
                    dve.wait_ge(L["scores_done"], B["scores_done"] + j + 1)
                    if l == 0:
                        dve.wait_ge(L["dist_ready"], B["dist_ready"] + p + 2)
                    else:
                        dve.wait_ge(L["alibi"], B["alibi"] + 16)
                    if j >= 3:
                        dve.wait_ge(L["dT_done"], B["dT_done"] + j - 2)
                    n, a = KEYS[t], BCOL[t]
                    s = 2 * (j % 2)
                    flat = ps[:, s:s + 2, :].rearrange("p b n -> p (b n)")
                    members = 2 if t < 2 else 1
                    for c in range(members):
                        src = flat[:, 0:n] if t == 2 else ps[:, s + c, 0:n]
                        ins = v.tensor_tensor_reduce(probs[:, j % 3, c * n:(c + 1) * n], src,
                                                     bias[:, (p % 2 if l == 0 else 1), a:a + n], 1.0, -3e38, ALU.add, ALU.max,
                                                     mx[:, j % 3, c:c + 1])
                    ins.then_inc(L["max_done"], 1)
                    dve.wait_ge(L["max_done"], B["max_done"] + j + 1)
                    v.tensor_scalar(nmx[:, j % 3, 0:members], mx[:, j % 3, 0:members], -SCALE, None, ALU.mult).then_inc(L["neg_done"], 1)

                def make_diag(j, p, t):
                    dve.wait_ge(L["exp_done"], B["exp_done"] + j + 1)
                    if j >= 2:
                        dve.wait_ge(L["dT_done"], B["dT_done"] + j - 1)
                    n = 2 if t < 2 else 1
                    r = rs[:, j % 3, 0:n]
                    link(dve, "dve", v.reciprocal(r, sm[:, j % 3, 0:n]))
                    if l == 0:
                        lamc = lamw[:, 5:6] if t < 2 else lamw[:, 6:7]
                        link(dve, "dve", v.tensor_tensor(r[:, n - 1:n], r[:, n - 1:n], lamc, ALU.mult))
                    if t < 2:
                        dg = diag[:, j % 2, :].rearrange("p (c n) -> p c n", c=2)
                        v.tensor_tensor(dg, ident.unsqueeze(1).to_broadcast([P, 2, P]), r.unsqueeze(2).to_broadcast([P, 2, P]),
                                        ALU.mult).then_inc(L["diag_done"], 1)
                    else:
                        src = ident2[:, :] if l == 0 else ident
                        q = DEC if l == 0 else P
                        v.tensor_scalar(diag[:, j % 2, 0:q], src, r, None, ALU.mult).then_inc(L["diag_done"], 1)

                def take_o(j, p, t):
                    dve.wait_ge(L["pv_done"], B["pv_done"] + j + 1)
                    n = ROWS[t]
                    cs = slice(p * P, (p + 1) * P)
                    if l == 0:
                        v.tensor_copy(o[0:n, t, cs], ps[0:n, 6, 0:P]).then_inc(L["o_done"], 1)
                    else:
                        v.tensor_tensor(o[0:n, t, cs], ps[0:n, 6, 0:P], gate[0:n, t, cs], ALU.mult).then_inc(L["o_done"], 1)

                if l == 1:
                    dve.wait_ge(units_used, Unit(BASE_OUT[l], 0).n)
                    v.tensor_copy(pick_heads[:, :, :].rearrange("h p (c n) -> h (p c) n", c=2),
                                  ident[0:FOX_HEADS, 0:FOX_HEADS].unsqueeze(2).to_broadcast([FOX_HEADS, FOX_HEADS, DEC])).then_inc(fox["heads_ready"], 1)
                    dve.wait_ge(L["g_done"], B["g_done"] + 6)
                row_max(*its[0])
                row_max(*its[1])
                dve.wait_ge(L["o_zeroed"], B["o_zeroed"] + 1)
                for j, p, t in its:
                    make_diag(j, p, t)
                    if j + 2 < len(its):
                        row_max(*its[j + 2])
                    if j >= 1:
                        take_o(*its[j - 1])
                take_o(*its[-1])
                if l == 0:
                    for t in range(TILES):
                        dve.wait_ge(L["o_sqd"], B["o_sqd"] + t + 1)
                        v.tensor_reduce(ms[0][:, 8 * t:8 * t + 8], o_sq[:, t % 2, :].rearrange("p (n d) -> p n d", d=P), AX, ALU.add).then_inc(L["o_ms"], 1)
                    for t in range(TILES):
                        dve.wait_ge(L["o_r"], B["o_r"] + t + 1)
                        vw = o[:, t, :].rearrange("p (n d) -> p n d", d=P)
                        link(dve, "dve", v.tensor_tensor(vw, vw, rr[0][:, 8 * t:8 * t + 8].unsqueeze(2).to_broadcast([P, 8, P]), ALU.mult))
                        v.tensor_tensor(vw, vw, subln[:, :].unsqueeze(1).to_broadcast([P, 8, P]), ALU.mult).then_inc(L["o_normed"], 1)
                for i in range(2 * TILES):
                    t, half = divmod(i, 2)
                    dve.wait_ge(L["o_hi"], B["o_hi"] + i + 1)
                    a, b_ = slice(4 * half, 4 * half + 4), slice(t * P, (t + 1) * P)
                    v.tensor_tensor(oT_lo[:, a, b_], ps[:, i, :].rearrange("p (k n) -> p k n", k=4), oT_hi[:, a, b_].bitcast(F32),
                                    ALU.subtract).then_inc(L["o_lo"], 1)
                for b in range(OUT_BLOCKS):
                    split_slab(BASE_OUT[l], b + 2)
                    for t in range(TILES):
                        wait_sum(dve, B, "out_done", BASE_OUT[l], b, t)
                        xs = x[:, t, b * F:(b + 1) * F]
                        v.tensor_tensor(xs, xs, acc(b, t), ALU.add).then_inc(L["x_mid"], 1)

                if l == 1:
                    dve.wait_ge(gain_loaded[1][1], 16)
                norm(B, "rstd1", 1, l, h2, "h_ready1")
                for t in range(TILES):
                    dve.wait_ge(L["h2hi"], B["h2hi"] + t + 1)
                    v.tensor_tensor(h2_lo[:, t, :], h2[:, t, :], h2_hi[:, t, :].bitcast(F32), ALU.subtract).then_inc(L["h2lo"], 1)
                K = lambda ins: link(dve, "dve", ins)
                b4 = lambda ap: ap.unsqueeze(2).to_broadcast([P, 3, 4])
                prio3 = prio.unsqueeze(1).to_broadcast([P, 3, 4])

                def first_of(dst, vals, top_):
                    K(v.tensor_tensor(t4, vals, b4(top_), ALU.is_equal))
                    K(v.tensor_tensor(t4, t4, prio3, ALU.mult))
                    K(v.tensor_reduce(dv, t4, AX, ALU.max))
                    K(v.tensor_tensor(dst, t4, b4(dv), ALU.is_equal))

                dve.wait_ge(L["logits"], B["logits"] + 1)
                K(v.tensor_tensor(lg, ps[:, 6, 0:60].rearrange("p (t n) -> p t n", t=3), b_router[:, l, :].unsqueeze(1).to_broadcast([P, 3, 20]), ALU.add))
                gl = lg[:, :, 0:4]
                K(v.tensor_reduce(gmx, gl, AX, ALU.max))
                v.tensor_tensor(gd, gl, b4(gmx), ALU.subtract).then_inc(L["logit_sb"], 1)
                first_of(oh, gl, gmx)
                v.tensor_tensor(oh, oh, b4(valid), ALU.mult).then_inc(L["onehot"], 1)
                dve.wait_ge(L["onehot"], B["onehot"] + 1)
                for gi in range(GROUPS):
                    K(v.tensor_tensor(t16[:, 12 * gi:12 * gi + 12].rearrange("p (t e) -> p t e", t=3), lg[:, :, 4 + 4 * gi:8 + 4 * gi],
                                      oh[:, :, gi:gi + 1].to_broadcast([P, 3, 4]), ALU.mult))
                K(v.tensor_tensor(t16[:, 0:24], t16[:, 0:24], t16[:, 24:48], ALU.add))
                K(v.tensor_tensor(ig, t16[:, 0:12].rearrange("p (t e) -> p t e", t=3), t16[:, 12:24].rearrange("p (t e) -> p t e", t=3), ALU.add))
                K(v.tensor_reduce(v1, ig, AX, ALU.max))
                first_of(oh1, ig, v1)
                K(v.scalar_tensor_tensor(ig2, oh1, -1e30, ig, ALU.mult, ALU.add))
                K(v.tensor_reduce(v2, ig2, AX, ALU.max))
                first_of(oh2, ig2, v2)
                v.tensor_tensor(dv, v2, v1, ALU.subtract).then_inc(L["logit_sb"], 1)
                dve.wait_ge(L["gexp"], B["gexp"] + 1)
                K(v.tensor_reduce(gsum, ge, AX, ALU.add))
                K(v.reciprocal(ptop, gsum))
                dve.wait_ge(L["gexp"], B["gexp"] + 2)
                K(v.tensor_scalar(w1, e2, 1.0, None, ALU.add))
                K(v.reciprocal(w1, w1))
                K(v.tensor_tensor(w1, w1, ptop, ALU.mult))
                K(v.tensor_tensor(w2, w1, e2, ALU.mult))
                K(v.tensor_tensor(t4, oh1, b4(w1), ALU.mult))
                K(v.tensor_tensor(t4b, oh2, b4(w2), ALU.mult))
                K(v.tensor_tensor(gate4, t4, t4b, ALU.add))
                K(v.tensor_copy(gates_hl[:, :, 0:4], gate4))
                K(v.tensor_tensor(gates_hl[:, :, 4:8], gate4, gates_hl[:, :, 0:4].bitcast(F32), ALU.subtract))
                dve.wait_ge(L["ranks"], B["ranks"] + 1)
                K(v.tensor_tensor(t4, ps[:, 7, 0:12].rearrange("p (t g) -> p t g", t=3), oh, ALU.mult))
                K(v.tensor_reduce(rank, t4, AX, ALU.add))
                K(v.tensor_tensor(t4b, t4, oh, ALU.add))
                K(v.tensor_scalar(pos, t4b, -1.0, None, ALU.add))
                K(v.tensor_reduce(total, ps[:, 7, 12:16], AX, ALU.max))
                v.tensor_scalar(flag[0:1, 0:1], total[0:1, :], float(CAP), None, ALU.is_gt).then_inc(OV[l]["flag_ready"], 1)
                v.tensor_scalar(over, rank, float(CAP), None, ALU.is_ge).then_inc(L["routed"], 1)

                def build_pick(g):
                    K_ = v.tensor_copy(pos_g[:, :], pos[:, :, bass.ds(g, 1)].rearrange("p t g -> p (t g)"))
                    K_.then_inc(L["pos_copied"], 1)
                    dve.wait_ge(L["pos_copied"], B["pos_copied"] + g + 1)
                    for t in range(TILES):
                        ins = v.tensor_scalar(pick[:, t, :], iota, pos_g[:, t:t + 1], None, ALU.is_equal)
                    ins.then_inc(L["pick_ready"], 1)

                def hidden(order, e, g):
                    wait_matrix(dve, l, order, ("u", e), g)
                    dve.wait_ge(L["silu_done"], B["silu_done"] + g * 4 + e + 1)
                    dve.wait_ge(L["slot_gated"], B["slot_gated"] + g + (2 if e == PER_GROUP else 1))
                    ge_ = slot_gate[:, e % PER_GROUP:e % PER_GROUP + 1]
                    v.scalar_tensor_tensor(hid[:, :], act_g[:, :], ge_, ps[:, 1, :], ALU.mult, ALU.mult).then_inc(L["hid_done"], 1)

                def hidden_lo(e, g):
                    dve.wait_ge(L["hT_hi"], B["hT_hi"] + g * 4 + e + 1)
                    v.tensor_tensor(hidT_lo[:, :, :].rearrange("p k n -> p (k n)"), ps[:, 2, :],
                                    hidT_hi[:, :, :].rearrange("p k n -> p (k n)").bitcast(F32), ALU.subtract).then_inc(L["hT_lo"], 1)

                def gathered_lo(g, first=False):
                    for i in range(2):
                        dve.wait_ge(L["x_hi"], B["x_hi"] + g * 2 + i + 1)
                        xs = slice(4 * i, 4 * i + 4)
                        v.tensor_tensor(xT_lo[:, xs, :].rearrange("p k n -> p (k n)"), ps[:, 5 + i, :],
                                        xT_hi[:, xs, :].rearrange("p k n -> p (k n)").bitcast(F32), ALU.subtract).then_inc(L["x_lo"], 1)
                    dve.wait_ge(L["slot_done"], B["slot_done"] + g + 1)
                    if not first:
                        dve.wait_ge(L["hid_done"], B["hid_done"] + g * 4)
                    v.tensor_reduce(slot_gate[:, :], ps[:, 7, 384:392].rearrange("p (a e) -> p e a", a=2), AX, ALU.add).then_inc(L["slot_gated"], 1)

                def add_back(g):
                    for i in range(2 * TILES):
                        t, c = divmod(i, 2)
                        dve.wait_ge(L["back_done"], B["back_done"] + g * 6 + i + 1)
                        xs = x[:, t, c * F:(c + 1) * F]
                        v.tensor_tensor(xs, xs, ps[:, BACK[i], :], ALU.add).then_inc(L["x_added"], 1)

                def take_pickT():
                    v.tensor_copy(pickT[:, :, :].rearrange("p t n -> p (t n)"), ps[:, 7, 0:384])

                def moe_round(order, g):
                    last = order is LAST
                    for m, (kind, e) in enumerate(order):
                        ahead = not (last and m >= len(order) - 2 and l == 1)
                        if ahead:
                            split_lo(Unit(BASE_MOE[l], 2 * (m + 4), g))
                        if kind == "u" and e < PER_GROUP:
                            hidden(order, e, g)
                        if (kind, e) in (("g", 1), ("g", 2), ("g", 3)):
                            hidden_lo(e - 1, g)
                        if (kind, e) == ("u", 1) and not last:
                            build_pick(g + 1)
                        if (kind, e) == ("u", 3) and not last:
                            gathered_lo(g + 1)
                        if (kind, e) == ("d", 2):
                            hidden_lo(3, g)
                        if (kind, e) == ("d", 3):
                            for i in range(2):
                                dve.wait_ge(L["y_hi"], B["y_hi"] + g * 2 + i + 1)
                                cs = slice(i * F, (i + 1) * F)
                                v.tensor_tensor(y_lo[:, cs], ps[:, 3 + i, :], y_hi[:, cs].bitcast(F32), ALU.subtract).then_inc(L["y_lo"], 1)
                        if (kind, e) == ("u", PER_GROUP):
                            hidden(order, e, g)
                            add_back(g)
                            take_pickT()
                        if ahead:
                            split_lo(Unit(BASE_MOE[l], 2 * (m + 4) + 1, g))
                    if last:
                        add_back(g)

                build_pick(0)
                gathered_lo(0, first=True)
                take_pickT()
                split_slab(BASE_MOE[l], 2)
                hidden(FIRST, 0, 0)
                split_slab(BASE_MOE[l], 3)
                with dve.Fori(0, GROUPS - 1) as g:
                    moe_round(ORDER, g)
                moe_round(LAST, GROUPS - 1)

                dve.wait_ge(OV[l]["flag_ready"], 1)
                flag_v = dve.value_load(flag[0:1, 0:1])
                kept = chain["dve"]
                with dve.If(flag_v > 0):
                    v.tensor_tensor(t4, gate4, b4(over), ALU.mult).then_inc(OV[l]["over_done"], 1)
                    dve.wait_ge(OV[l]["over_done"], 1)
                    for gi in range(GROUPS):
                        ins = v.tensor_tensor(over_gate[:, :, 4 * gi:4 * gi + 4], t4, oh[:, :, gi:gi + 1].to_broadcast([P, 3, 4]), ALU.mult)
                    ins.then_inc(OV[l]["over_done"], 1)
                    with dve.Fori(0, EXPERTS) as e:
                        dve.wait_ge(OV[l]["over_done"], e + 2)
                        v.tensor_copy(over_col[:, :], over_gate[:, :, bass.ds(e, 1)].rearrange("p t e -> p (t e)")).then_inc(OV[l]["over_done"], 1)
                        dve.wait_ge(OV[l]["over_done"], e + 3)
                        for t in range(TILES):
                            dve.wait_ge(OV[l]["over_used"], e * 18 + 6 * t + 5)
                            dve.wait_ge(OV[l]["over_act"], e * TILES + t + 1)
                            v.scalar_tensor_tensor(hid[:, :], act_g[:, :], over_col[:, t:t + 1], ps[:, 1, :], ALU.mult, ALU.mult).then_inc(OV[l]["over_hid"], 1)
                            dve.wait_ge(OV[l]["over_used"], e * 18 + 6 * t + 7)
                            for c in range(2):
                                xs = x[:, t, c * F:(c + 1) * F]
                                ins = v.tensor_tensor(xs, xs, ps[:, 3 + c, :], ALU.add)
                            ins.then_inc(OV[l]["over_x"], 1)
                assert chain["dve"] == kept


_OUT_SHAPES = [
    ("y_prompt", (1, SEQ, D)), ("y_sample", (1, DEC, D)),
    ("new_diff_k_prompt", (1, 1, SEQ, 8, 128)), ("new_diff_v_prompt", (1, 1, SEQ, 8, 128)),
    ("new_fox_k_prompt", (1, 1, SEQ, 16, 64)), ("new_fox_v_prompt", (1, 1, SEQ, 16, 64)),
    ("new_fox_logf_prompt", (1, 1, SEQ, 16)),
    ("new_diff_k_sample", (1, 1, DEC, 8, 128)), ("new_diff_v_sample", (1, 1, DEC, 8, 128)),
    ("new_fox_k_sample", (1, 1, DEC, 16, 64)), ("new_fox_v_sample", (1, 1, DEC, 16, 64)),
    ("new_fox_logf_sample", (1, 1, DEC, 16)),
]


def kernel(**inputs):
    import concourse.bacc as _bacc
    from concourse.bass_utils import run_bass_kernel_spmd as _run

    nc = _bacc.Bacc("TRN2", target_bir_lowering=False, num_devices=1)
    arrays, aps = {}, {}
    host = {name: np.ascontiguousarray(a) for name, a in inputs.items()}
    host["c_consts"], host["c_dist"], host["c_mask"] = constants()
    for name, a in host.items():
        arrays[f"in_{name}"] = a
        aps[name] = nc.dram_tensor(f"in_{name}", a.shape, mybir.dt.from_np(a.dtype), kind="ExternalInput").ap()
    for name, shape in _OUT_SHAPES:
        aps[name] = nc.dram_tensor(f"out_{name}", shape, F32, kind="ExternalOutput").ap()
    build(nc, aps)
    r = _run(nc, [arrays], core_ids=[0])
    return tuple(r.results[0][f"out_{name}"] for name, _ in _OUT_SHAPES)
```

```python
from contextlib import ExitStack
import math

import numpy as np
import concourse.bass as bass
from concourse import mybir

F32 = mybir.dt.float32
F32R = mybir.dt.float32r
I32 = mybir.dt.int32
ALU = mybir.AluOpType
ACT = mybir.ActivationFunctionType
AX = mybir.AxisListType.X

P = 128
D = 1024
SEQ, DEC, PAST = 256, 64, 512
TILES = 3
TOK = TILES * P
KB = D // P
HD = 64
PAIRS = D // P
FOX_HEADS = 16
GROUPS, PER_GROUP, EXPERTS = 4, 4, 16
F = 512
EPS = 1e-6
SCALE = HD ** -0.5
CHUNK = 64
CAP = 128
LAMBDA_INIT = 0.8 - 0.6 * math.exp(0.0)
ROWS = [128, 128, 64]
PTILES = PAST // P
SMALL = 9

RAW, HI = 6, 4
UNIT = 2048
PER_LOOP = 2 * 3 * PER_GROUP
IN_BLOCKS = [6, 8]
OUT_BLOCKS = D // F
BASE_IN, BASE_OUT, BASE_MOE = [0, 0], [0, 0], [0, 0]
_n = 0
for _l in range(2):
    BASE_IN[_l] = _n
    BASE_OUT[_l] = BASE_IN[_l] + 2 * IN_BLOCKS[_l]
    BASE_MOE[_l] = BASE_OUT[_l] + 2 * OUT_BLOCKS
    _n = BASE_MOE[_l] + GROUPS * PER_LOOP
UNITS = _n

FIRST = [("g", 0), ("u", 0)]
ORDER = [("g", 1), ("u", 1), ("d", 0), ("g", 2), ("u", 2), ("d", 1), ("g", 3), ("u", 3), ("d", 2),
         ("g", 4), ("d", 3), ("u", 4)]
DT_BANK = [4, 7]
BACK = [5, 6, 3, 4, 2, 5]
LAST = [m for m in ORDER if m[1] < PER_GROUP]

C_ID, C_IOTA, C_TRI, C_BEFORE, C_AFTER, C_ONE = (i * P for i in range(6))
C_VALID = 6 * P
C_PRIO = C_VALID + TILES
C_WIDTH = C_PRIO + 4 + 1
KEYS = [128, 256, 576]
BCOL = [0, 128, 384]
BIAS = 960


def constants():
    c = np.zeros((P, C_WIDTH), np.float32)
    i = np.arange(P)
    c[:, C_ID:C_ID + P] = np.eye(P)
    c[:, C_IOTA:C_IOTA + P] = np.where(i < CAP, i, -7)[None]
    c[:, C_TRI:C_TRI + P] = i[:, None] <= i[None]
    c[:, C_BEFORE:C_BEFORE + P] = i[:, None] < i[None]
    c[:, C_AFTER:C_AFTER + P] = i[:, None] > i[None]
    c[:, C_ONE:C_ONE + P] = 1
    c[:, C_VALID:C_VALID + TILES] = 1
    c[DEC:, C_VALID + 2] = 0
    c[:, C_PRIO:C_PRIO + 4] = [4, 3, 2, 1]
    dist = np.zeros((P, BIAS), np.float32)
    mask = np.zeros((P, BIAS), np.float32)
    for t, (keys, at, q0) in enumerate(zip(KEYS, BCOL, (0, P, PAST))):
        q = q0 + (i if t < 2 else i % DEC)[:, None]
        k = np.arange(keys)[None]
        dist[:, at:at + keys] = np.where(k // CHUNK <= q // CHUNK, -np.abs(q - k) / SCALE, -1e34)
        mask[:, at:at + keys] = np.where(k <= q, 0, -1e30 / SCALE)
    return c, dist, mask


class Unit:

    def __init__(self, base, i, g=0):
        n = base + i
        self.slot, self.hslot, self.static = n % RAW, n % HI, n
        self.n = g * PER_LOOP + n
        self.arrivals = g * (16 * PER_LOOP // RAW) + 16 * (n // RAW + 1)


def build(nc, A):
    with ExitStack() as ctx:
        S = lambda name: ctx.enter_context(nc.semaphore(name))

        start = (nc.sbuf_base + 63) // 32 * 32
        at = [start]

        def sb(name, shape, dt=F32, offset=None):
            size = (int(np.prod(shape[1:])) * 4 + 31) // 32 * 32
            if offset is None:
                offset = at[0]
                at[0] += size
            return nc.alloc_sbuf_tensor_at(name, shape, dt, offset=offset)

        ring_at = at[0]
        w_raw = sb("w_raw", [P, RAW, UNIT])
        w_lo = sb("w_lo", [P, RAW, UNIT], F32R, offset=ring_at)
        w_hi = sb("w_hi", [P, HI, UNIT], F32R)
        x = sb("x", [P, TILES, D])
        cst = sb("cst", [P, C_WIDTH])
        ident = cst[:, C_ID:C_ID + P]
        iota = cst[:, C_IOTA:C_IOTA + P]
        tri = cst[:, C_TRI:C_TRI + P]
        before = cst[:, C_BEFORE:C_BEFORE + P]
        after = cst[:, C_AFTER:C_AFTER + P]
        ones = cst[:, C_ONE:C_ONE + P]
        valid = cst[:, C_VALID:C_VALID + TILES]
        prio = cst[:, C_PRIO:C_PRIO + 4]
        neghalf = sb("neghalf", [P, 24])
        gain_at = at[0]
        gain = sb("gain", [P, 2, D])
        qk_gain = sb("qk_gain", [P, 4, HD])
        own_at = at[0]
        subln = sb("subln", [P, P])
        lamv = sb("lamv", [P, 4, HD])
        lamw = sb("lamw", [P, 8])
        ident2 = sb("ident2", [P, HD])
        diag = sb("diag", [P, DEC])
        o_sq = sb("o_sq", [P, 2, P])
        dist = sb("dist", [P, BIAS])
        own_end = at[0]
        at[0] = own_at
        pick_heads = sb("pick_heads", [FOX_HEADS, PAIRS, P], F32R)
        w_f = sb("w_f", [P, KB, FOX_HEADS])
        w_f_hi = sb("w_f_hi", [P, KB, FOX_HEADS], F32R)
        w_f_lo = sb("w_f_lo", [P, KB, FOX_HEADS], F32R)
        lf = sb("lf", [P, 7, TILES * FOX_HEADS])
        logf = sb("logf", [P, TILES, FOX_HEADS])
        logf_past = sb("logf_past", [P, PTILES, FOX_HEADS])
        at[0] = max(at[0], own_end)
        w_router = sb("w_router", [P, 2, KB, 20])
        b_router = sb("b_router", [P, 2, 20])
        b_forget = sb("b_forget", [P, FOX_HEADS])
        ident_r = sb("ident_r", [P, FOX_HEADS], F32R)
        stat = sb("stat", [P, 160])
        ss, mean, rstd = stat[:, 0:3], stat[:, 3:6], stat[:, 6:9]
        mx, nmx, sm, rs = (stat[:, a:a + 6].rearrange("p (j c) -> p j c", j=3) for a in (12, 18, 24, 30))
        ms = [stat[:, 40 + 24 * i:64 + 24 * i] for i in range(2)]
        rr = [stat[:, 88 + 24 * i:112 + 24 * i] for i in range(2)]
        flag = sb("flag", [1, 8], I32)
        region = at[0]

        hT_hi = sb("hT_hi", [P, KB, TOK], F32R, offset=region)
        hT_lo = sb("hT_lo", [P, KB, TOK], F32R, offset=region + 12288)
        oT_hi = sb("oT_hi", [P, KB, TOK], F32R, offset=region)
        oT_lo = sb("oT_lo", [P, KB, TOK], F32R, offset=region + 12288)
        bias = sb("bias", [P, 2, BIAS], offset=region + 3840)
        probs = sb("probs", [P, 3, 576], offset=region + 11520)
        dT = sb("dT", [P, 2, 640], offset=region + 18432)
        assert 18432 + 5120 <= 24576
        at[0] = region + 24576
        h_at = at[0]
        h = sb("h", [P, TILES, D])
        o = sb("o", [P, TILES, D], offset=h_at)
        k_past = sb("k_past", [P, 2, PTILES, P])
        v_past = sb("v_past", [P, 2, PTILES, P])
        kT_past = sb("kT_past", [P, 2, PAST])
        qT = sb("qT", [P, PAIRS, SEQ])
        q_diag = sb("q_diag", [P, PAIRS, P])
        kT_at = at[0]
        kT_new = sb("kT_new", [P, PAIRS, SEQ + DEC])
        v_new = sb("v_new", [P, TILES, D])
        qk_at = at[0]
        qk = sb("qk", [P, 2, TILES, F])
        gate = sb("gate", [P, TILES, D], offset=qk_at)
        off_hi = sb("off_hi", [FOX_HEADS, 832], F32R, offset=gain_at)
        off_lo = sb("off_lo", [FOX_HEADS, 832], F32R, offset=gain_at + 4 * D)
        top = at[0]

        at[0] = region
        xT_hi = sb("xT_hi", [P, KB, P], F32R)
        xT_lo = sb("xT_lo", [P, KB, P], F32R)
        pick = sb("pick", [P, TILES, P], F32R)
        pickT = sb("pickT", [P, TILES, P], F32R)
        act_g = sb("act_g", [P, F])
        hid = sb("hid", [P, F])
        hidT_hi = sb("hidT_hi", [P, 4, P], F32R)
        hidT_lo = sb("hidT_lo", [P, 4, P], F32R)
        r_ = sb("router", [P, 640])
        gates_hl = sb("gates_hl", [P, TILES, 8], F32R)
        slot_gate = sb("slot_gate", [P, 4])
        pos_g = sb("pos_g", [P, TILES])
        over_gate = sb("over_gate", [P, TILES, EXPERTS])
        over_col = sb("over_col", [P, TILES])
        assert at[0] <= h_at
        at[0] = h_at
        h2 = sb("h2", [P, TILES, D])
        h2_hi = sb("h2_hi", [P, TILES, D], F32R)
        h2_lo = sb("h2_lo", [P, TILES, D], F32R)
        h2T = sb("h2T", [P, KB, TOK])
        y_hi = sb("y_hi", [P, D], F32R)
        y_lo = sb("y_lo", [P, D], F32R)
        over_w = sb("over_w", [P, UNIT])
        over_hT = sb("over_hT", [P, F])
        top = max(top, at[0])
        assert top <= nc.sbuf_usable_end, (top, nc.sbuf_usable_end)
        rcol = [0]

        def rt(*shape):
            n = int(np.prod(shape))
            ap = r_[:, rcol[0]:rcol[0] + n]
            rcol[0] += n
            if len(shape) == 2:
                ap = ap.rearrange("p (a b) -> p a b", a=shape[0])
            return ap

        lg = rt(3, 20)
        gmx, gsum, ptop, v1, v2, dv, e2, w1, w2, rank, over = (rt(3) for _ in range(11))
        gd, ge, oh, ig, oh1, oh2, ig2, t4, gate4, t4b = (rt(3, 4) for _ in range(10))
        pos = rt(3, 4)
        total = rt(1)
        t16 = rt(48)

        ps = ctx.enter_context(nc.psum_tensor("ps", [P, 8, 512], F32))

        raw_ready = [S(f"raw_ready{i}") for i in range(RAW)]
        hi_ready, lo_ready, units_used = S("hi_ready"), S("lo_ready"), S("units_used")
        const_loaded, small_loaded = S("const_loaded"), S("small_loaded")
        x_loaded = [S(f"x_loaded{t}") for t in range(TILES)]
        qk_gains_loaded, lam_loaded = S("qk_gains_loaded"), S("lam_loaded")
        gain_loaded = [[S(f"gain_loaded{l}{i}") for i in range(2)] for l in range(2)]
        x_padded, pads_ready, halves_ready, lam_ready = S("x_padded"), S("pads_ready"), S("halves_ready"), S("lam_ready")
        lam_dots, lam_exps = S("lam_dots"), S("lam_exps")
        dve_chain, pool_chain = S("dve_chain"), S("pool_chain")
        chain = {"dve": 0, "pool": 0}

        def link(eng, which, ins):
            chain[which] += 1
            s = dve_chain if which == "dve" else pool_chain
            ins.then_inc(s, 1)
            eng.wait_ge(s, chain[which])

        per_layer = dict(
            sq0=3, rstd0=3, h_ready0=3, tr0=6, hi0=6, lo0=6, proj_done=12, qk_sq=12, qk_ms=12, qk_r=4, qk_n1=12,
            qk_normed=12, qk_tr=12, qk_evac=12, v_copied=6, g_done=0, k_stored=16 * 2 * TILES, v_stored=16 * TILES,
            k_loaded0=64, k_loaded1=64, v_loaded0=64, v_loaded1=64,
            q_zeroed=1, bias_ready=8, alibi=16, past_tr=8, past_ev=8, scores_done=24, max_done=24, neg_done=24, exp_done=24,
            mixed=24, dT_done=24, dT_copied=24, pv_done=24, o_done=24, o_zeroed=1, o_sqd=24, o_r=24, o_normed=24, o_tr=6,
            o_hi=6, o_lo=6, out_done=4, x_mid=6,
            sq1=3, rstd1=3, h_ready1=3, tr1=6, ev1=6, h2hi=3, h2lo=3, logits=1, logit_sb=2, gexp=2, onehot=1, ranks=1,
            routed=1, pos_copied=4, pickT_taken=4, pick_ready=4, gathered=8, slot_done=4, slot_gated=4, x_hi=8, x_lo=8, silu_done=16, hid_done=16,
            hT_done=16, hT_hi=16, hT_lo=16, y_hi=8, y_lo=8, back_done=24, x_added=24)
        L = {name: S(name) for name in per_layer}
        BEFORE = [{name: l * n for name, n in per_layer.items()} for l in range(2)]
        OV = [{name: S(f"{name}{l}") for name in ("flag_ready", "over_load", "over_used", "over_act", "over_hid", "over_tr",
                                                  "over_ht", "over_done", "over_x")} for l in range(2)]
        fox = {name: S(f"fox_{name}") for name in ("wf_loaded", "lp_loaded", "wf_hi", "wf_lo", "f_done", "f_z", "f_exp",
                                                   "logf_ready", "logf_stored", "heads_ready", "off_done", "off_hi", "off_lo")}
        stores_done = S("stores_done")

        W_IN = [A["diff_w_in"][0], A["fox_w_in"][0]]
        W_OUT = [A["diff_w_out"][0], A["fox_w_out"][0]]
        K_CACHE = [A["cache_diff_k"].rearrange("a b s h d -> (a b s) (h d)"), A["cache_fox_k"].rearrange("a b s h d -> (a b s) (h d)")]
        V_CACHE = [A["cache_diff_v"].rearrange("a b s h d -> (a b s) (h d)"), A["cache_fox_v"].rearrange("a b s h d -> (a b s) (h d)")]
        K_OUT = [[A[n].rearrange("a b s h d -> (a b s) (h d)") for n in ("new_diff_k_prompt", "new_diff_k_sample")],
                 [A[n].rearrange("a b s h d -> (a b s) (h d)") for n in ("new_fox_k_prompt", "new_fox_k_sample")]]
        V_OUT = [[A[n].rearrange("a b s h d -> (a b s) (h d)") for n in ("new_diff_v_prompt", "new_diff_v_sample")],
                 [A[n].rearrange("a b s h d -> (a b s) (h d)") for n in ("new_fox_v_prompt", "new_fox_v_sample")]]
        x_p = A["x_prompt"][0]
        x_s = A["x_sample"][0]

        def token_rows(prompt, sample, t):
            return prompt[t * P:(t + 1) * P, :] if t < 2 else sample[0:DEC, :]

        def items():
            for j in range(3 * PAIRS):
                yield j, j // 3, j % 3

        def new_keys_T(j, l):
            if l == 0:
                return ps[0:DEC, DT_BANK[j % 2], 4 * DEC:5 * DEC]
            return ps[0:DEC, 5, 0:P]

        def in_kind(b):
            return "qqkkvvgg"[b]

        def acc(b, t):
            return ps[:, 3 * (b % 2) + t, :]

        def src_proj(w, b, half):
            return w[half * 512:(half + 1) * 512, b * F:(b + 1) * F].rearrange("(k p) n -> p k n", p=P)

        def src_moe(l, e, kind, half):
            name = {"g": "moe_w_gate", "u": "moe_w_up", "d": "moe_w_down"}[kind]
            w = A[name][l]
            w = w[bass.ds(e, 1), :, :]
            n = 512 if kind != "d" else 256
            return w[:, half * n:(half + 1) * n, :].rearrange("e (k p) n -> p (e k) n", p=P)

        def wait_sum(eng, B, name, base, b, t):
            if t < TILES - 1:
                eng.wait_ge(L[name], B[name] + 2 * b + t + 1)
            else:
                eng.wait_ge(units_used, Unit(base, 2 * b + 1).n + 1)

        def wait_matrix(eng, l, order, what, g):
            m0 = 0 if order is FIRST else 2
            eng.wait_ge(units_used, Unit(BASE_MOE[l], 2 * (m0 + order.index(what)) + 1, g).n + 1)

        def raw_view(slot, kind):
            return w_raw[:, slot, :].rearrange("p (k n) -> p k n", n=F if kind != "d" else D)

        block = ctx.enter_context(nc.Block())

        @block.sync
        def _(sp):
            for t in range(TILES):
                sp.dma_start(x[0:ROWS[t], t, :], token_rows(x_p, x_s, t)).then_inc(x_loaded[t], 16)
            sp.dma_start(gain[:, 0, :], A["norm_mix"][0, :].partition_broadcast(P)).then_inc(gain_loaded[0][0], 16)
            sp.dma_start(cst[:, :], A["c_consts"]).then_inc(const_loaded, 16)

            def load_unit(U, kind, src):
                if U.static >= RAW:
                    sp.wait_ge(units_used, U.n - RAW + 1)
                sp.dma_start(raw_view(U.slot, kind), src).then_inc(raw_ready[U.slot], 16)

            def load_matrices(l, order, m0, g):
                for m, (kind, e) in enumerate(order):
                    for half in range(2):
                        load_unit(Unit(BASE_MOE[l], 2 * (m0 + m) + half, g), kind, src_moe(l, g * PER_GROUP + e, kind, half))

            for l in range(2):
                for b in range(2 * l, IN_BLOCKS[l]):
                    for half in range(2):
                        load_unit(Unit(BASE_IN[l], 2 * b + half), "p", src_proj(W_IN[l], b, half))
                for b in range(OUT_BLOCKS):
                    for half in range(2):
                        load_unit(Unit(BASE_OUT[l], 2 * b + half), "p", src_proj(W_OUT[l], b, half))
                load_matrices(l, FIRST, 0, 0)
                with sp.Fori(0, GROUPS - 1) as g:
                    load_matrices(l, ORDER, 2, g)
                load_matrices(l, LAST, 2, GROUPS - 1)
                if l == 0:
                    for b in range(2):
                        for half in range(2):
                            load_unit(Unit(BASE_IN[1], 2 * b + half), "p", src_proj(W_IN[1], b, half))
                sp.wait_ge(OV[l]["flag_ready"], 1)
                flag_v = sp.value_load(flag[0:1, 0:1])
                with sp.If(flag_v > 0):
                    with sp.Fori(0, EXPERTS) as e:
                        for t in range(TILES):
                            for j, (kind, half) in enumerate([("g", 0), ("g", 1), ("u", 0), ("u", 1), ("d", 0), ("d", 1)]):
                                sp.wait_ge(OV[l]["over_used"], e * 18 + 6 * t + j + 1)
                                sp.dma_start(over_w[:, :].rearrange("p (k n) -> p k n", n=F if kind != "d" else D),
                                             src_moe(l, e, kind, half)).then_inc(OV[l]["over_load"], 16)
                    sp.wait_ge(OV[l]["over_x"], EXPERTS * TILES)
            sp.wait_ge(L["x_added"], 2 * 6 * GROUPS)
            for t in range(TILES):
                sp.dma_start(token_rows(A["y_prompt"][0], A["y_sample"][0], t), x[0:ROWS[t], t, :]).then_inc(stores_done, 16)
            sp.wait_ge(stores_done, 16 * TILES)

        @block.gpsimd
        def _(pool):
            pool.memset(neghalf[:, :], -0.5).then_inc(halves_ready, 1)
            pool.wait_ge(halves_ready, 1)
            qk_gains = [
                (qk_gain[:, 0, :], A["diff_q_norm"][0, :].partition_broadcast(P)),
                (qk_gain[:, 1, :], A["diff_k_norm"][0, :].partition_broadcast(P)),
                (qk_gain[:, 2, :], A["fox_q_norm"][0, :].partition_broadcast(P)),
                (qk_gain[:, 3, :], A["fox_k_norm"][0, :].partition_broadcast(P)),
            ]
            head_vectors = [
                (subln[:, :], A["diff_subln"][0, :].partition_broadcast(P)),
                (lamv[:, 0, :], A["diff_lambda_q1"][0, :].partition_broadcast(P)),
                (lamv[:, 1, :], A["diff_lambda_k1"][0, :].partition_broadcast(P)),
                (lamv[:, 2, :], A["diff_lambda_q2"][0, :].partition_broadcast(P)),
                (lamv[:, 3, :], A["diff_lambda_k2"][0, :].partition_broadcast(P)),
            ]
            small = [(b_forget[:, :], A["fox_b_f"][0, :].partition_broadcast(P))]
            for l in range(2):
                small += [
                    (w_router[:, l, :, 0:4], A["moe_w_group"][l].rearrange("(k p) n -> p k n", p=P)),
                    (w_router[:, l, :, 4:20], A["moe_w_expert"][l].rearrange("(k p) n -> p k n", p=P)),
                    (b_router[:, l, 0:4], A["moe_b_group"][l, :].partition_broadcast(P)),
                    (b_router[:, l, 4:20], A["moe_b_expert"][l, :].partition_broadcast(P)),
                ]
            assert len(small) == SMALL

            def rms(B, squares, done):
                for t in range(TILES):
                    ts = slice(t, t + 1)
                    pool.wait_ge(L[squares], B[squares] + t + 1)
                    link(pool, "pool", pool.tensor_scalar(mean[:, ts], ss[:, ts], 1.0 / D, EPS, ALU.mult, ALU.add))
                    pool.tensor_tensor(rstd[:, ts], mean[:, ts], neghalf[:, 0:1], ALU.pow).then_inc(L[done], 1)

            for l in range(2):
                B = BEFORE[l]
                if l == 0:
                    for dst, src in qk_gains:
                        pool.dma_start(dst, src).then_inc(qk_gains_loaded, 16)
                rms(B, "sq0", "rstd0")
                pool.memset(q_diag[:, :, :], 0.0).then_inc(L["q_zeroed"], 1)
                if l == 1:
                    pool.dma_start(w_f[:, :, :], W_IN[1][:, 4 * D:4 * D + FOX_HEADS].rearrange("(k p) n -> p k n", p=P)).then_inc(fox["wf_loaded"], 16)
                    pool.dma_start(logf_past[:, :, :], A["cache_fox_logf"].rearrange("a b (i p) h -> p (a b i) h", p=P)).then_inc(fox["lp_loaded"], 16)

                def load_keys(p):
                    cols = slice(p * P, (p + 1) * P)
                    if p >= 2:
                        pool.wait_ge(L["past_tr"], B["past_tr"] + p - 1)
                    pool.dma_start(k_past[:, p % 2, :, :], K_CACHE[l][:, cols].rearrange("(i p) n -> p i n", p=P)).then_inc(L[f"k_loaded{p % 2}"], 16)

                def load_values(p):
                    cols = slice(p * P, (p + 1) * P)
                    if p >= 2:
                        pool.wait_ge(L["pv_done"], B["pv_done"] + 3 * (p - 2) + 3)
                    pool.dma_start(v_past[:, p % 2, :, :], V_CACHE[l][:, cols].rearrange("(i p) n -> p i n", p=P)).then_inc(L[f"v_loaded{p % 2}"], 16)

                for p in range(2):
                    load_keys(p)
                    load_values(p)
                if l == 0:
                    for dst, src in head_vectors:
                        pool.dma_start(dst, src).then_inc(lam_loaded, 16)
                    pool.dma_start(dist[:, :], A["c_dist"]).then_inc(L["alibi"], 16)
                    pool.dma_start(gain[:, 1, :], A["norm_ffn"][0, :].partition_broadcast(P)).then_inc(gain_loaded[0][1], 16)
                    pool.wait_ge(L["h_ready0"], B["h_ready0"] + TILES)
                    pool.dma_start(gain[:, 0, :], A["norm_mix"][1, :].partition_broadcast(P)).then_inc(gain_loaded[1][0], 16)
                for b in range(4):
                    pool.wait_ge(L["qk_ms"], B["qk_ms"] + 3 * b + 3)
                    link(pool, "pool", pool.tensor_scalar(ms[b % 2], ms[b % 2], 1.0 / HD, EPS, ALU.mult, ALU.add))
                    pool.tensor_tensor(rr[b % 2], ms[b % 2], neghalf[:, :], ALU.pow).then_inc(L["qk_r"], 1)
                    if b >= 2:
                        for t in range(TILES):
                            pool.wait_ge(L["qk_normed"], B["qk_normed"] + 3 * b + t + 1)
                            out = token_rows(K_OUT[l][0], K_OUT[l][1], t)[:, (b - 2) * F:(b - 1) * F]
                            pool.dma_start(out, qk[0:ROWS[t], b % 2, t, :]).then_inc(L["k_stored"], 16)
                if l == 0:
                    for dst, src in small:
                        pool.dma_start(dst, src).then_inc(small_loaded, 16)
                if l == 1:
                    pool.wait_ge(fox["logf_ready"], 1)
                    for t in range(TILES):
                        prompt, sample = (A[n].rearrange("a b s h -> (a b s) h") for n in ("new_fox_logf_prompt", "new_fox_logf_sample"))
                        pool.dma_start(token_rows(prompt, sample, t), logf[0:ROWS[t], t, :]).then_inc(fox["logf_stored"], 16)
                for t in range(TILES):
                    pool.wait_ge(L["v_copied"], B["v_copied"] + 3 + t + 1)
                    pool.dma_start(token_rows(V_OUT[l][0], V_OUT[l][1], t), v_new[0:ROWS[t], t, :]).then_inc(L["v_stored"], 16)
                if l == 1:
                    pool.wait_ge(units_used, Unit(BASE_OUT[l], 0).n)
                    pool.dma_start(bias[:, 1, :], A["c_mask"]).then_inc(L["alibi"], 16)

                def head_rms(c0, c1):
                    m, r = ms[0][:, c0:c1], rr[0][:, c0:c1]
                    k = (1.0 - LAMBDA_INIT) ** 2
                    pool.wait_ge(L["o_sqd"], B["o_sqd"] + c1)
                    link(pool, "pool", pool.tensor_scalar(m, m, 1.0 / (P * k), EPS / k, ALU.mult, ALU.add))
                    pool.tensor_tensor(r, m, neghalf[:, 0:c1 - c0], ALU.pow).then_inc(L["o_r"], c1 - c0)

                load_keys(2)
                load_keys(3)
                for p in range(2, PAIRS):
                    if p + 2 < PAIRS:
                        load_keys(p + 2)
                    load_values(p)
                    if l == 0:
                        head_rms(3 * (p - 2), 3 * (p - 1))
                if l == 0:
                    head_rms(3 * (PAIRS - 2), 3 * (PAIRS - 1))
                    for i in range(3 * (PAIRS - 1), 3 * PAIRS):
                        head_rms(i, i + 1)
                else:
                    pool.wait_ge(L["scores_done"], B["scores_done"] + 3 * PAIRS)
                    pool.dma_start(gain[:, 1, :], A["norm_ffn"][1, :].partition_broadcast(P)).then_inc(gain_loaded[1][1], 16)
                rms(B, "sq1", "rstd1")
                pool.wait_ge(L["k_stored"], B["k_stored"] + 16 * 2 * TILES)
                pool.wait_ge(L["v_stored"], B["v_stored"] + 16 * TILES)
                if l == 1:
                    pool.wait_ge(fox["logf_stored"], 16 * TILES)
                pool.wait_ge(OV[l]["flag_ready"], 1)
                flag_v = pool.value_load(flag[0:1, 0:1])
                with pool.If(flag_v > 0):
                    pool.wait_ge(OV[l]["over_x"], EXPERTS * TILES)

        @block.scalar
        def _(act):
            A_ = nc.scalar.activation

            def split_hi(U):
                act.wait_ge(raw_ready[U.slot], U.arrivals)
                if U.static >= HI:
                    act.wait_ge(units_used, U.n - HI + 1)
                A_(w_hi[:, U.hslot, :], w_raw[:, U.slot, :], ACT.Copy).then_inc(hi_ready, 1)

            def split_slab(base, k, g=0):
                for half in range(2):
                    split_hi(Unit(base, 2 * k + half, g))

            for l in range(2):
                B = BEFORE[l]
                for t in range(TILES):
                    if l == 0:
                        act.wait_ge(x_loaded[t], 16)
                        if t == 2:
                            act.wait_ge(x_padded, 1)
                    else:
                        act.wait_ge(L["x_added"], 6 * GROUPS - 6 + 2 * t + 2)
                    A_(h[:, t, :], x[:, t, :], ACT.Square, accum_out=ss[:, t:t + 1]).then_inc(L["sq0"], 1)
                if l == 0:
                    split_slab(0, 0)
                else:
                    split_hi(Unit(BASE_IN[1], 3))
                for i in range(2 * TILES):
                    t, half = divmod(i, 2)
                    act.wait_ge(L["tr0"], B["tr0"] + i + 1)
                    A_(hT_hi[:, 4 * half:4 * half + 4, t * P:(t + 1) * P], ps[:, i, :].rearrange("p (k n) -> p k n", k=4), ACT.Copy).then_inc(L["hi0"], 1)
                if l == 0:
                    split_slab(0, 1)
                if l == 1:
                    act.wait_ge(fox["wf_loaded"], 16)
                    A_(w_f_hi[:, :, :], w_f[:, :, :], ACT.Copy).then_inc(fox["wf_hi"], 1)
                    act.wait_ge(fox["f_z"], 1)
                    A_(lf[:, 2, :], lf[:, 1, :], ACT.Exp, scale=-1.0).then_inc(fox["f_exp"], 1)
                    act.wait_ge(fox["off_done"], 1)
                    A_(off_hi[:, 0:320], ps[0:FOX_HEADS, 7, 0:320], ACT.Copy, scale=-1.0 / SCALE).then_inc(fox["off_hi"], 1)
                    A_(off_hi[:, 320:832], ps[0:FOX_HEADS, 6, 0:512], ACT.Copy, scale=1.0 / SCALE).then_inc(fox["off_hi"], 1)

                def evacuate_qk(b):
                    for t in range(TILES):
                        i = 3 * b + t
                        act.wait_ge(L["qk_tr"], B["qk_tr"] + i + 1)
                        bank = ps[:, 6 + i % 2, :].rearrange("p (k n) -> p k n", k=4)
                        pr = slice(4 * (b % 2), 4 * (b % 2) + 4)
                        if b < 2 and t < 2:
                            A_(qT[:, pr, t * P:(t + 1) * P], bank, ACT.Copy).then_inc(L["qk_evac"], 1)
                        elif b < 2:
                            act.wait_ge(L["q_zeroed"], B["q_zeroed"] + 1)
                            A_(q_diag[0:HD, pr, 0:DEC], bank[0:HD, :, 0:DEC], ACT.Copy)
                            A_(q_diag[HD:P, pr, DEC:P], bank[HD:P, :, 0:DEC], ACT.Copy).then_inc(L["qk_evac"], 1)
                        else:
                            n = ROWS[t]
                            A_(kT_new[:, pr, t * P:t * P + n], bank[:, :, 0:n], ACT.Copy).then_inc(L["qk_evac"], 1)

                for b in range(IN_BLOCKS[l]):
                    kind = in_kind(b)
                    split_hi(Unit(BASE_IN[l], 2 * b + 4))
                    for t in range(TILES):
                        wait_sum(act, B, "proj_done", BASE_IN[l], b, t)
                        if kind in "qk":
                            if b >= 2:
                                act.wait_ge(L["qk_tr"], B["qk_tr"] + 3 * (b - 2) + t + 1)
                            A_(qk[:, b % 2, t, :], acc(b, t), ACT.Square).then_inc(L["qk_sq"], 1)
                        elif kind == "v":
                            A_(v_new[:, t, (b - 4) * F:(b - 3) * F], acc(b, t), ACT.Copy).then_inc(L["v_copied"], 1)
                        else:
                            if b == 6 and t == 0:
                                act.wait_ge(L["qk_tr"], B["qk_tr"] + 12)
                                act.wait_ge(L["k_stored"], B["k_stored"] + 16 * 2 * TILES)
                            A_(gate[:, t, (b - 6) * F:(b - 5) * F], acc(b, t), ACT.Sigmoid).then_inc(L["g_done"], 1)
                    if 1 <= b <= 4:
                        evacuate_qk(b - 1)
                    split_hi(Unit(BASE_IN[l], 2 * b + 5))
                    if l == 0 and b == 4:
                        act.wait_ge(lam_dots, 2)
                        A_(lamw[:, 2:4], lamw[:, 0:2], ACT.Exp).then_inc(lam_exps, 1)

                def alibi(p):
                    if p >= 2:
                        act.wait_ge(L["max_done"], B["max_done"] + 3 * (p - 2) + 3)
                    A_(bias[:, p % 2, :], dist[:, :], ACT.Copy, scale=2.0 ** -(p + 1)).then_inc(L["bias_ready"], 1)

                def square_head(j, p, t):
                    act.wait_ge(L["o_done"], B["o_done"] + j + 1)
                    if j >= 2:
                        act.wait_ge(L["o_sqd"], B["o_sqd"] + j - 1)
                    A_(o_sq[:, j % 2, :], o[:, t, p * P:(p + 1) * P], ACT.Square, accum_out=ms[0][:, j:j + 1]).then_inc(L["o_sqd"], 1)

                def past_keys(p):
                    act.wait_ge(L["past_tr"], B["past_tr"] + p + 1)
                    A_(kT_past[:, p % 2, :], ps[:, 5, :], ACT.Copy).then_inc(L["past_ev"], 1)

                def exps(j, t):
                    act.wait_ge(L["neg_done"], B["neg_done"] + j + 1)
                    n = KEYS[t]
                    for c in range(2 if t < 2 else 1):
                        s = probs[:, j % 3, c * n:(c + 1) * n]
                        ins = A_(s, s, ACT.Exp, bias=nmx[:, j % 3, c:c + 1], scale=SCALE, accum_out=sm[:, j % 3, c:c + 1])
                    ins.then_inc(L["exp_done"], 1)

                def copy_dT(j, p, t):
                    act.wait_ge(L["dT_done"], B["dT_done"] + j + 1)
                    if j >= 2:
                        act.wait_ge(L["pv_done"], B["pv_done"] + j - 1)
                    bank, q = ps[:, DT_BANK[j % 2], :], (DEC if l == 0 else P)
                    if t < 2:
                        n = KEYS[t] * (1 if l == 0 else 2)
                        A_(dT[:, j % 2, 0:n], bank[:, 0:n], ACT.Copy).then_inc(L["dT_copied"], 1)
                    else:
                        A_(dT[:, j % 2, 0:4 * q], bank[:, 0:4 * q], ACT.Copy)
                        A_(dT[0:DEC, j % 2, 4 * q:5 * q], new_keys_T(j, l), ACT.Copy).then_inc(L["dT_copied"], 1)

                its = list(items())
                past_keys(0)
                if l == 0:
                    act.wait_ge(L["alibi"], B["alibi"] + 16)
                    alibi(0)
                    alibi(1)
                exps(0, 0)
                for j, p, t in its:
                    if j + 1 < len(its):
                        exps(j + 1, its[j + 1][2])
                    if t == 1 and p + 1 < PAIRS:
                        past_keys(p + 1)
                    if j >= 1:
                        copy_dT(*its[j - 1])
                    if l == 0:
                        if t == 0 and 1 <= p < PAIRS - 1:
                            alibi(p + 1)
                        if j >= 3:
                            square_head(*its[j - 3])
                copy_dT(*its[-1])
                if l == 0:
                    for item in its[-3:]:
                        square_head(*item)
                for i in range(2 * TILES):
                    t, half = divmod(i, 2)
                    act.wait_ge(L["o_tr"], B["o_tr"] + i + 1)
                    A_(oT_hi[:, 4 * half:4 * half + 4, t * P:(t + 1) * P], ps[:, i, :].rearrange("p (k n) -> p k n", k=4), ACT.Copy).then_inc(L["o_hi"], 1)
                split_slab(BASE_OUT[l], 2)
                split_hi(Unit(BASE_OUT[l], 6))

                for t in range(TILES):
                    act.wait_ge(L["x_mid"], B["x_mid"] + TILES + t + 1)
                    if t == 0:
                        act.wait_ge(L["k_stored"], B["k_stored"] + 16 * 2 * TILES)
                        act.wait_ge(L["v_stored"], B["v_stored"] + 16 * TILES)
                        if l == 1:
                            act.wait_ge(fox["logf_stored"], 16 * TILES)
                    A_(h2[:, t, :], x[:, t, :], ACT.Square, accum_out=ss[:, t:t + 1]).then_inc(L["sq1"], 1)
                split_hi(Unit(BASE_OUT[l], 7))
                for t in range(TILES):
                    act.wait_ge(L["h_ready1"], B["h_ready1"] + t + 1)
                    A_(h2_hi[:, t, :], h2[:, t, :], ACT.Copy).then_inc(L["h2hi"], 1)
                    for half in range(2):
                        i = 2 * t + half
                        act.wait_ge(L["tr1"], B["tr1"] + i + 1)
                        A_(h2T[:, 4 * half:4 * half + 4, t * P:(t + 1) * P], ps[:, i, :].rearrange("p (k n) -> p k n", k=4), ACT.Copy).then_inc(L["ev1"], 1)
                act.wait_ge(L["logit_sb"], B["logit_sb"] + 1)
                A_(ge, gd, ACT.Exp).then_inc(L["gexp"], 1)

                def silu(order, e, g):
                    wait_matrix(act, l, order, ("g", e), g)
                    if order is not FIRST:
                        act.wait_ge(L["hid_done"], B["hid_done"] + g * 4 + e)
                    A_(act_g[:, :], ps[:, 0, :], ACT.Silu).then_inc(L["silu_done"], 1)

                def hidden_hi(e, g):
                    act.wait_ge(L["hT_done"], B["hT_done"] + g * 4 + e + 1)
                    A_(hidT_hi[:, :, :].rearrange("p k n -> p (k n)"), ps[:, 2, :], ACT.Copy).then_inc(L["hT_hi"], 1)

                def gathered_hi(g):
                    for i in range(2):
                        act.wait_ge(L["gathered"], B["gathered"] + g * 2 + i + 1)
                        A_(xT_hi[:, 4 * i:4 * i + 4, :].rearrange("p k n -> p (k n)"), ps[:, 5 + i, :], ACT.Copy).then_inc(L["x_hi"], 1)

                def moe_round(order, g):
                    last = order is LAST
                    for m, (kind, e) in enumerate(order):
                        ahead = not (last and m >= len(order) - 2 and l == 1)
                        if ahead:
                            split_hi(Unit(BASE_MOE[l], 2 * (m + 4), g))
                        if kind == "g":
                            silu(order, e, g)
                        if (kind, e) in (("g", 1), ("g", 2), ("g", 3)):
                            hidden_hi(e - 1, g)
                        if (kind, e) == ("u", 3) and not last:
                            gathered_hi(g + 1)
                        if (kind, e) == ("d", 2):
                            hidden_hi(3, g)
                        if (kind, e) == ("d", 3):
                            wait_matrix(act, l, order, ("d", 3), g)
                            for i in range(2):
                                A_(y_hi[:, i * F:(i + 1) * F], ps[:, 3 + i, :], ACT.Copy).then_inc(L["y_hi"], 1)
                        if ahead and not (last and m == len(order) - 1):
                            split_hi(Unit(BASE_MOE[l], 2 * (m + 4) + 1, g))

                gathered_hi(0)
                act.wait_ge(L["logit_sb"], B["logit_sb"] + 2)
                A_(e2, dv, ACT.Exp).then_inc(L["gexp"], 1)
                silu(FIRST, 0, 0)
                split_slab(BASE_MOE[l], 2)
                split_slab(BASE_MOE[l], 3)
                with act.Fori(0, GROUPS - 1) as g:
                    moe_round(ORDER, g)
                moe_round(LAST, GROUPS - 1)

                act.wait_ge(OV[l]["flag_ready"], 1)
                flag_v = act.value_load(flag[0:1, 0:1])
                with act.If(flag_v > 0):
                    with act.Fori(0, EXPERTS) as e:
                        for t in range(TILES):
                            act.wait_ge(OV[l]["over_used"], e * 18 + 6 * t + 3)
                            A_(act_g[:, :], ps[:, 0, :], ACT.Silu).then_inc(OV[l]["over_act"], 1)
                            act.wait_ge(OV[l]["over_tr"], e * TILES + t + 1)
                            A_(over_hT[:, :], ps[:, 2, :], ACT.Copy).then_inc(OV[l]["over_ht"], 1)
                            act.wait_ge(OV[l]["over_x"], e * TILES + t + 1)

        @block.tensor
        def _(pe):
            mm, tr = nc.tensor.matmul, nc.tensor.transpose

            def split_mm(out, a_hi, a_lo, b_hi, b_lo, start, stop):
                mm(out, a_hi, b_hi, start=start, stop=False)
                mm(out, a_hi, b_lo, start=False, stop=False)
                return mm(out, a_lo, b_hi, start=False, stop=stop)

            def unit_parts(U, n):
                hi = w_hi[:, U.hslot, :].rearrange("p (k n) -> p k n", n=n)
                lo = w_lo[:, U.slot, :].rearrange("p (k n) -> p k n", n=n)
                return hi, lo

            def transposes(B, src, ready, done, counts=(1, 2, 3)):
                for i in range(2 * TILES):
                    t, half = divmod(i, 2)
                    pe.wait_ge(L[ready], B[ready] + counts[t])
                    for k in range(4):
                        c = (4 * half + k) * P
                        ins = tr(ps[:, i, k * P:(k + 1) * P], src[:, t, c:c + P], ident)
                    ins.then_inc(L[done], 1)

            def project(B, base, b, a_hi, a_lo, low, done, free):
                for half in range(2):
                    U = Unit(base, 2 * b + half)
                    pe.wait_ge(lo_ready, U.n + 1)
                    hi, lo = unit_parts(U, F)
                    for t in range(TILES):
                        if b == 0:
                            pe.wait_ge(L[low], B[low] + 2 * t + half + 1)
                        if half == 0:
                            free(b, t)
                        for k in range(4):
                            kb = 4 * half + k
                            ts = slice(t * P, (t + 1) * P)
                            ins = split_mm(acc(b, t), a_hi[:, kb, ts], a_lo[:, kb, ts], hi[:, k, :], lo[:, k, :],
                                           start=(kb == 0), stop=(kb == KB - 1))
                        if half == 1 and t < TILES - 1:
                            ins.then_inc(L[done], 1)
                    ins.then_inc(units_used, 1)

            pe.wait_ge(const_loaded, 16)
            for l in range(2):
                B = BEFORE[l]
                transposes(B, h, "h_ready0", "tr0")
                if l == 1:
                    pe.wait_ge(fox["wf_lo"], 1)
                    pe.wait_ge(L["lo0"], B["lo0"] + 2 * TILES)
                    for t in range(TILES):
                        for kb in range(KB):
                            ts = slice(t * P, (t + 1) * P)
                            ins = split_mm(ps[:, 7, t * 16:(t + 1) * 16], hT_hi[:, kb, ts], hT_lo[:, kb, ts],
                                           w_f_hi[:, kb, :], w_f_lo[:, kb, :], start=(kb == 0), stop=(kb == KB - 1))
                    ins.then_inc(fox["f_done"], 1)
                    pe.wait_ge(fox["logf_ready"], 1)
                    pe.wait_ge(fox["lp_loaded"], 16)
                    off = ps[0:FOX_HEADS, 7, :]
                    mm(off[:, 0:128], logf[:, 0, :], tri, start=True, stop=True)
                    mm(off[:, 128:256], logf[:, 0, :], ones, start=True, stop=False)
                    mm(off[:, 128:256], logf[:, 1, :], tri, start=False, stop=True)
                    mm(off[:, 256:320], logf[0:DEC, 2, :], tri[0:DEC, 0:DEC], start=True, stop=True)
                    for i in range(PTILES):
                        out = ps[0:FOX_HEADS, 6, i * P:(i + 1) * P]
                        ins = mm(out, logf_past[:, i, :], after, start=True, stop=(i == PTILES - 1))
                        for k in range(i + 1, PTILES):
                            ins = mm(out, logf_past[:, k, :], ones, start=False, stop=(k == PTILES - 1))
                    ins.then_inc(fox["off_done"], 1)

                def free_in(b, t):
                    if b >= 2:
                        if in_kind(b - 2) in "qk":
                            pe.wait_ge(L["qk_n1"], B["qk_n1"] + 3 * (b - 2) + t + 1)
                        else:
                            pe.wait_ge(L["v_copied"], B["v_copied"] + 3 * (b - 6) + t + 1)

                def transpose_qk(b):
                    for t in range(TILES):
                        i = 3 * b + t
                        pe.wait_ge(L["qk_normed"], B["qk_normed"] + i + 1)
                        if i >= 2:
                            pe.wait_ge(L["qk_evac"], B["qk_evac"] + i - 1)
                        elif l == 1:
                            pe.wait_ge(fox["off_lo"], 2)
                        for k in range(4):
                            ins = tr(ps[:, 6 + i % 2, k * P:(k + 1) * P], qk[:, b % 2, t, k * P:(k + 1) * P], ident)
                        ins.then_inc(L["qk_tr"], 1)

                for b in range(IN_BLOCKS[l]):
                    project(B, BASE_IN[l], b, hT_hi, hT_lo, "lo0", "proj_done", free_in)
                    if 1 <= b <= 4:
                        transpose_qk(b - 1)

                its = list(items())

                def past_keys(p):
                    pe.wait_ge(L[f"k_loaded{p % 2}"], B["k_loaded0"] + 16 * (p // 2 + 1))
                    if p == 0:
                        (pe.wait_ge(L["v_copied"], B["v_copied"] + 6) if l == 0 else pe.wait_ge(L["g_done"], B["g_done"] + 6))
                    else:
                        pe.wait_ge(L["past_ev"], B["past_ev"] + p)
                        if l == 1 and p >= 2:
                            pe.wait_ge(L["dT_copied"], B["dT_copied"] + 3 * (p - 2) + 3)
                    for i in range(PTILES):
                        ins = tr(ps[:, 5, i * P:(i + 1) * P], k_past[:, p % 2, i, :], ident)
                    ins.then_inc(L["past_tr"], 1)

                def offsets(out, head, n, width, a, stop=True):
                    if width == P:
                        sel = ident_r[0:FOX_HEADS, head:head + 1].to_broadcast([FOX_HEADS, P])
                    else:
                        sel = pick_heads[:, head // 2, :]
                    mm(out, sel, off_hi[:, a:a + n], start=False, stop=False)
                    return mm(out, sel, off_lo[:, a:a + n], start=False, stop=True)

                def scores(j, p, t):
                    s = 2 * (j % 2)
                    if j >= 2:
                        pe.wait_ge(L["max_done"], B["max_done"] + j - 1)
                    fx = l == 1
                    if t < 2:
                        n = KEYS[t]
                        for c in range(2):
                            out = ps[:, s + c, 0:n]
                            cs = slice(c * HD, (c + 1) * HD)
                            ins = mm(out, qT[cs, p, t * P:(t + 1) * P], kT_new[cs, p, 0:n], start=True, stop=not fx)
                            if fx:
                                ins = offsets(out, 2 * p + c, n, P, 0)
                    else:
                        pe.wait_ge(L["past_ev"], B["past_ev"] + p + 1)
                        ins = mm(ps[:, s, :], q_diag[:, p, :], kT_past[:, p % 2, :], start=True, stop=not fx)
                        if fx:
                            offsets(ps[:, s, :], 2 * p, PAST, DEC, 320)
                        ins = mm(ps[:, s + 1, 0:DEC], q_diag[:, p, :], kT_new[:, p, SEQ:SEQ + DEC], start=True, stop=not fx)
                        if fx:
                            ins = offsets(ps[:, s + 1, 0:DEC], 2 * p, DEC, DEC, 256)
                    ins.then_inc(L["scores_done"], 1)

                def probs_T(j, p, t):
                    if l == 0:
                        pe.wait_ge(L["mixed"], B["mixed"] + j + 1)
                    else:
                        pe.wait_ge(L["exp_done"], B["exp_done"] + j + 1)
                    if j >= 2:
                        pe.wait_ge(L["dT_copied"], B["dT_copied"] + j - 1)
                    pr, bank = probs[:, j % 3, :], ps[:, DT_BANK[j % 2], :]
                    if t < 2:
                        for i in range(KEYS[t] // P * (1 if l == 0 else 2)):
                            ins = tr(bank[:, i * P:(i + 1) * P], pr[:, i * P:(i + 1) * P], ident)
                    elif l == 0:
                        for kb in range(PTILES):
                            mm(bank[:, kb * DEC:(kb + 1) * DEC], pr[:, kb * P:(kb + 1) * P], diag[:, :], start=True, stop=True)
                        ins = mm(new_keys_T(j, l), pr[:, PAST:PAST + DEC], diag[:, :], start=True, stop=True)
                    else:
                        pe.wait_ge(L["past_ev"], B["past_ev"] + min(p + 2, PAIRS))
                        for kb in range(PTILES):
                            tr(bank[:, kb * P:(kb + 1) * P], pr[:, kb * P:(kb + 1) * P], ident)
                        ins = tr(new_keys_T(j, l), pr[:, PAST:PAST + DEC], ident)
                    ins.then_inc(L["dT_done"], 1)

                def values(j, p, t):
                    pe.wait_ge(L["dT_copied"], B["dT_copied"] + j + 1)
                    if j >= 1:
                        pe.wait_ge(L["o_done"], B["o_done"] + j)
                    if t == 2:
                        pe.wait_ge(L[f"v_loaded{p % 2}"], B["v_loaded0"] + 16 * (p // 2 + 1))
                    d = dT[:, j % 2, :]
                    col = p * P
                    members = [(0, P)] if l == 0 else [(0, HD), (HD, HD)]
                    for m, (c0, w) in enumerate(members):
                        out = ps[0:ROWS[t], 6, c0:c0 + w]
                        if t < 2:
                            nb = KEYS[t] // P
                            for kb in range(nb):
                                a = (m * nb + kb) * P
                                ins = mm(out, d[:, a:a + P], v_new[:, kb, col + c0:col + c0 + w], start=(kb == 0), stop=(kb == nb - 1))
                        else:
                            q = DEC if l == 0 else P
                            for kb in range(PTILES):
                                mm(out, d[:, kb * q + m * DEC:kb * q + m * DEC + DEC], v_past[:, p % 2, kb, c0:c0 + w], start=(kb == 0), stop=False)
                            ins = mm(out, d[0:DEC, PTILES * q + m * DEC:PTILES * q + m * DEC + DEC],
                                     v_new[0:DEC, 2, col + c0:col + c0 + w], start=False, stop=True)
                    ins.then_inc(L["pv_done"], 1)

                pe.wait_ge(L["qk_evac"], B["qk_evac"] + 12)
                past_keys(0)
                if l == 1:
                    pe.wait_ge(L["g_done"], B["g_done"] + 6)
                else:
                    pe.wait_ge(L["v_copied"], B["v_copied"] + 6)
                if l == 1:
                    pe.wait_ge(fox["heads_ready"], 1)
                scores(*its[0])
                scores(*its[1])
                for j, p, t in its:
                    if t == 1 and p + 1 < PAIRS:
                        past_keys(p + 1)
                    if j + 2 < len(its):
                        scores(*its[j + 2])
                    probs_T(j, p, t)
                    if j >= 1:
                        values(*its[j - 1])
                values(*its[-1])

                last_items = (3 * PAIRS - 2, 3 * PAIRS - 1, 3 * PAIRS)
                transposes(B, o, "o_normed" if l == 0 else "o_done", "o_tr", counts=last_items)

                def free_out(b, t):
                    pass

                for b in range(OUT_BLOCKS):
                    project(B, BASE_OUT[l], b, oT_hi, oT_lo, "o_lo", "out_done", free_out)

                transposes(B, h2, "h_ready1", "tr1")
                pe.wait_ge(L["ev1"], B["ev1"] + 2 * TILES)
                if l == 0:
                    pe.wait_ge(small_loaded, 16 * SMALL)
                for t in range(TILES):
                    for kb in range(KB):
                        ins = mm(ps[:, 6, t * 20:(t + 1) * 20], h2T[:, kb, t * P:(t + 1) * P], w_router[:, l, kb, :],
                                 start=(kb == 0), stop=(kb == KB - 1))
                ins.then_inc(L["logits"], 1)
                pe.wait_ge(L["onehot"], B["onehot"] + 1)
                ohv = oh
                for t in range(TILES):
                    for s in range(t):
                        mm(ps[:, 7, 4 * t:4 * t + 4], ones, ohv[:, s, :], start=(s == 0), stop=False)
                    mm(ps[:, 7, 4 * t:4 * t + 4], before, ohv[:, t, :], start=(t == 0), stop=True)
                for s in range(TILES):
                    ins = mm(ps[:, 7, 12:16], ones, ohv[:, s, :], start=(s == 0), stop=(s == TILES - 1))
                ins.then_inc(L["ranks"], 1)
                pe.wait_ge(L["h2lo"], B["h2lo"] + TILES)

                def gather(g):
                    pe.wait_ge(L["pick_ready"], B["pick_ready"] + g + 1)
                    for i in range(2):
                        for k in range(4):
                            kb = 4 * i + k
                            for t in range(TILES):
                                for part, src in enumerate((h2_hi, h2_lo)):
                                    ins = mm(ps[:, 5 + i, k * P:(k + 1) * P], src[:, t, kb * P:(kb + 1) * P], pick[:, t, :],
                                             start=(t == 0 and part == 0), stop=(t == TILES - 1 and part == 1))
                        ins.then_inc(L["gathered"], 1)

                def slots(g):
                    for t in range(TILES):
                        mm(ps[:, 7, 384:392], pick[:, t, :], gates_hl[:, t, :], start=(t == 0), stop=(t == TILES - 1))
                    for t in range(TILES):
                        ins = tr(ps[:, 7, t * P:(t + 1) * P], pick[:, t, :].bitcast(F32), ident)
                    ins.then_inc(L["slot_done"], 1)

                def into(m, bank, g):
                    for half in range(2):
                        U = Unit(BASE_MOE[l], 2 * m + half, g)
                        pe.wait_ge(lo_ready, U.n + 1)
                        hi, lo = unit_parts(U, F)
                        for k in range(4):
                            kb = 4 * half + k
                            ins = split_mm(ps[:, bank, :], xT_hi[:, kb, :], xT_lo[:, kb, :], hi[:, k, :], lo[:, k, :],
                                           start=(kb == 0), stop=(kb == KB - 1))
                        ins.then_inc(units_used, 1)

                def down(m, e, g):
                    pe.wait_ge(L["hT_lo"], B["hT_lo"] + g * 4 + e + 1)
                    for half in range(2):
                        U = Unit(BASE_MOE[l], 2 * m + half, g)
                        pe.wait_ge(lo_ready, U.n + 1)
                        hi, lo = unit_parts(U, D)
                        for k in range(2):
                            fb = 2 * half + k
                            for c in range(2):
                                cs = slice(c * F, (c + 1) * F)
                                ins = split_mm(ps[:, 3 + c, :], hidT_hi[:, fb, :], hidT_lo[:, fb, :], hi[:, k, cs], lo[:, k, cs],
                                               start=(e == 0 and fb == 0), stop=(e == 3 and fb == 3))
                        ins.then_inc(units_used, 1)

                def hidden_T(e, g):
                    pe.wait_ge(L["hid_done"], B["hid_done"] + g * 4 + e + 1)
                    if e == 0:
                        pe.wait_ge(L["pickT_taken"], B["pickT_taken"] + g + 1)
                    for k in range(4):
                        ins = tr(ps[:, 2, k * P:(k + 1) * P], hid[:, k * P:(k + 1) * P], ident)
                    ins.then_inc(L["hT_done"], 1)

                def back(g):
                    pe.wait_ge(L["y_lo"], B["y_lo"] + g * 2 + 2)
                    for i in range(2 * TILES):
                        t, c = divmod(i, 2)
                        if i == 5:
                            pe.wait_ge(L["x_added"], B["x_added"] + g * 6 + 1)
                        cs = slice(c * F, (c + 1) * F)
                        mm(ps[:, BACK[i], :], pickT[:, t, :], y_hi[:, cs], start=True, stop=False)
                        mm(ps[:, BACK[i], :], pickT[:, t, :], y_lo[:, cs], start=False, stop=True).then_inc(L["back_done"], 1)

                def moe_round(order, g):
                    last = order is LAST
                    for m, (kind, e) in enumerate(order):
                        if kind == "g":
                            pe.wait_ge(L["silu_done"], B["silu_done"] + g * 4 + e)
                            if e == PER_GROUP:
                                pe.wait_ge(L["x_lo"], B["x_lo"] + g * 2 + 4)
                            into(2 + m, 0, g)
                        elif kind == "u":
                            into(2 + m, 1, g)
                        else:
                            down(2 + m, e, g)
                        if (kind, e) in (("g", 1), ("g", 2), ("g", 3)):
                            hidden_T(e - 1, g)
                        if (kind, e) == ("u", 3) and not last:
                            gather(g + 1)
                            slots(g + 1)
                        if (kind, e) == ("d", 2):
                            hidden_T(3, g)
                    back(g)

                gather(0)
                pe.wait_ge(L["x_lo"], B["x_lo"] + 2)
                into(0, 0, 0)
                pe.wait_ge(L["routed"], B["routed"] + 1)
                slots(0)
                into(1, 1, 0)
                with pe.Fori(0, GROUPS - 1) as g:
                    moe_round(ORDER, g)
                moe_round(LAST, GROUPS - 1)

                pe.wait_ge(OV[l]["flag_ready"], 1)
                flag_v = pe.value_load(flag[0:1, 0:1])
                with pe.If(flag_v > 0):
                    pe.sem_inc(OV[l]["over_used"], 1)
                    with pe.Fori(0, EXPERTS) as e:
                        for t in range(TILES):
                            ts = slice(t * P, (t + 1) * P)
                            wf = over_w[:, :].rearrange("p (k n) -> p k n", n=F)
                            wd = over_w[:, :].rearrange("p (k n) -> p k n", n=D)
                            for j in range(4):
                                pe.wait_ge(OV[l]["over_load"], e * 288 + 16 * (6 * t + j + 1))
                                bank, half = divmod(j, 2)
                                for k in range(4):
                                    kb = 4 * half + k
                                    ins = mm(ps[:, bank, :], h2T[:, kb, ts], wf[:, k, :], start=(kb == 0), stop=(kb == KB - 1))
                                ins.then_inc(OV[l]["over_used"], 1)
                            pe.wait_ge(OV[l]["over_hid"], e * TILES + t + 1)
                            for k in range(4):
                                ins = tr(ps[:, 2, k * P:(k + 1) * P], hid[:, k * P:(k + 1) * P], ident)
                            ins.then_inc(OV[l]["over_tr"], 1)
                            pe.wait_ge(OV[l]["over_ht"], e * TILES + t + 1)
                            for j in range(2):
                                pe.wait_ge(OV[l]["over_load"], e * 288 + 16 * (6 * t + 4 + j + 1))
                                for k in range(2):
                                    fb = 2 * j + k
                                    for c in range(2):
                                        ins = mm(ps[:, 3 + c, :], over_hT[:, fb * P:(fb + 1) * P], wd[:, k, c * F:(c + 1) * F],
                                                 start=(fb == 0), stop=(fb == 3))
                                ins.then_inc(OV[l]["over_used"], 1)
                            pe.wait_ge(OV[l]["over_x"], e * TILES + t + 1)

        @block.vector
        def _(dve):
            v = nc.vector

            def split_lo(U):
                dve.wait_ge(hi_ready, U.n + 1)
                v.tensor_tensor(w_lo[:, U.slot, :], w_raw[:, U.slot, :], w_hi[:, U.hslot, :].bitcast(F32), ALU.subtract).then_inc(lo_ready, 1)

            def split_slab(base, k, g=0):
                for half in range(2):
                    split_lo(Unit(base, 2 * k + half, g))

            def norm(B, rstd_name, which, l, dst, done):
                for t in range(TILES):
                    dve.wait_ge(L[rstd_name], B[rstd_name] + t + 1)
                    v.scalar_tensor_tensor(dst[:, t, :], x[:, t, :], rstd[:, t:t + 1], gain[:, which, :], ALU.mult, ALU.mult).then_inc(L[done], 1)

            v.memset(x[DEC:P, 2, :], 0.0).then_inc(x_padded, 1)
            for l in range(2):
                B = BEFORE[l]
                dve.wait_ge(gain_loaded[l][0], 16)
                norm(B, "rstd0", 0, l, h, "h_ready0")
                if l == 0:
                    split_slab(0, 0)
                else:
                    split_lo(Unit(BASE_IN[1], 3))
                for i in range(2 * TILES):
                    t, half = divmod(i, 2)
                    dve.wait_ge(L["hi0"], B["hi0"] + i + 1)
                    a, b_ = slice(4 * half, 4 * half + 4), slice(t * P, (t + 1) * P)
                    v.tensor_tensor(hT_lo[:, a, b_], ps[:, i, :].rearrange("p (k n) -> p k n", k=4), hT_hi[:, a, b_].bitcast(F32),
                                    ALU.subtract).then_inc(L["lo0"], 1)
                if l == 0:
                    split_slab(0, 1)
                if l == 1:
                    v.tensor_copy(pick_heads[:, :, :].rearrange("h p (c n) -> h (p c) n", c=2),
                                  ident[0:FOX_HEADS, 0:FOX_HEADS].unsqueeze(2).to_broadcast([FOX_HEADS, FOX_HEADS, DEC])).then_inc(fox["heads_ready"], 1)
                    dve.wait_ge(fox["wf_hi"], 1)
                    v.tensor_tensor(w_f_lo[:, :, :], w_f[:, :, :], w_f_hi[:, :, :].bitcast(F32), ALU.subtract).then_inc(fox["wf_lo"], 1)
                    dve.wait_ge(fox["f_done"], 1)
                    z, az, e, s, s2, q, m0 = (lf[:, i, :] for i in range(7))
                    z3 = z.rearrange("p (t h) -> p t h", t=3)
                    link(dve, "dve", v.tensor_tensor(z3, ps[:, 7, 0:48].rearrange("p (t h) -> p t h", t=3),
                                                     b_forget[:, :].unsqueeze(1).to_broadcast([P, 3, 16]), ALU.add))
                    link(dve, "dve", v.tensor_scalar(m0, z, -1.0, None, ALU.mult))
                    v.tensor_tensor(az, z, m0, ALU.max).then_inc(fox["f_z"], 1)
                    dve.wait_ge(fox["f_exp"], 1)
                    link(dve, "dve", v.tensor_scalar(m0, z, 0.0, None, ALU.min))
                    link(dve, "dve", v.tensor_scalar(q, e, 2.0, None, ALU.add))
                    link(dve, "dve", v.reciprocal(s2, q))
                    link(dve, "dve", v.tensor_tensor(s, e, s2, ALU.mult))
                    link(dve, "dve", v.tensor_tensor(s2, s, s, ALU.mult))
                    link(dve, "dve", v.tensor_scalar(q, s2, 1.0 / 17, 1.0 / 15, ALU.mult, ALU.add))
                    for n in (13, 11, 9, 7, 5, 3, 1):
                        link(dve, "dve", v.tensor_tensor(q, q, s2, ALU.mult))
                        link(dve, "dve", v.tensor_scalar(q, q, 1.0 / n, None, ALU.add))
                    link(dve, "dve", v.tensor_tensor(q, q, s, ALU.mult))
                    v.scalar_tensor_tensor(logf[:, :, :].rearrange("p t h -> p (t h)"), q, -2.0, m0, ALU.mult, ALU.add).then_inc(fox["logf_ready"], 1)
                    dve.wait_ge(fox["off_hi"], 1)
                    v.scalar_tensor_tensor(off_lo[:, 0:320], ps[0:FOX_HEADS, 7, 0:320], -1.0 / SCALE, off_hi[:, 0:320].bitcast(F32),
                                           ALU.mult, ALU.subtract).then_inc(fox["off_lo"], 1)
                    dve.wait_ge(fox["off_hi"], 2)
                    v.scalar_tensor_tensor(off_lo[:, 320:832], ps[0:FOX_HEADS, 6, 0:512], 1.0 / SCALE, off_hi[:, 320:832].bitcast(F32),
                                           ALU.mult, ALU.subtract).then_inc(fox["off_lo"], 1)

                for b in range(IN_BLOCKS[l]):
                    kind = in_kind(b)
                    split_lo(Unit(BASE_IN[l], 2 * b + 4))
                    if kind in "vg":
                        split_lo(Unit(BASE_IN[l], 2 * b + 5))
                    if l == 0 and b == 0:
                        dve.wait_ge(qk_gains_loaded, 16 * 4)
                    if kind in "qk":
                        gn = qk_gain[:, 2 * l + b // 2, :].unsqueeze(1).to_broadcast([P, 8, HD])
                        for t in range(TILES):
                            dve.wait_ge(L["qk_sq"], B["qk_sq"] + 3 * b + t + 1)
                            v.tensor_reduce(ms[b % 2][:, 8 * t:8 * t + 8], qk[:, b % 2, t, :].rearrange("p (n d) -> p n d", d=HD), AX, ALU.add).then_inc(L["qk_ms"], 1)
                        split_lo(Unit(BASE_IN[l], 2 * b + 5))
                        dve.wait_ge(L["qk_r"], B["qk_r"] + b + 1)
                        for t in range(TILES):
                            v.tensor_tensor(qk[:, b % 2, t, :].rearrange("p (n d) -> p n d", d=HD), acc(b, t).rearrange("p (n d) -> p n d", d=HD),
                                            rr[b % 2][:, 8 * t:8 * t + 8].unsqueeze(2).to_broadcast([P, 8, HD]), ALU.mult).then_inc(L["qk_n1"], 1)
                        for t in range(TILES):
                            dve.wait_ge(L["qk_n1"], B["qk_n1"] + 3 * b + t + 1)
                            vw = qk[:, b % 2, t, :].rearrange("p (n d) -> p n d", d=HD)
                            v.tensor_tensor(vw, vw, gn, ALU.mult).then_inc(L["qk_normed"], 1)

                    if l == 0 and b == 4:
                        dve.wait_ge(lam_loaded, 16 * 5)
                        for i in range(2):
                            v.tensor_tensor_reduce(lamv[:, 2 * i, :], lamv[:, 2 * i, :], lamv[:, 2 * i + 1, :], 1.0, 0.0,
                                                   ALU.mult, ALU.add, lamw[:, i:i + 1]).then_inc(lam_dots, 1)
                        dve.wait_ge(lam_exps, 1)
                        link(dve, "dve", v.tensor_tensor(lamw[:, 4:5], lamw[:, 3:4], lamw[:, 2:3], ALU.subtract))
                        link(dve, "dve", v.tensor_scalar(lamw[:, 5:6], lamw[:, 4:5], -LAMBDA_INIT, None, ALU.add))
                        dve.wait_ge(const_loaded, 16)
                        link(dve, "dve", v.tensor_copy(lamw[0:HD, 6:7], ones[0:HD, 0:1]))
                        link(dve, "dve", v.tensor_copy(lamw[HD:P, 6:7], lamw[HD:P, 5:6]))
                        link(dve, "dve", v.tensor_tensor(ident2[:, :], ident[:, 0:HD], ident[:, HD:P], ALU.add))
                        link(dve, "dve", v.tensor_copy(ident_r[:, :], ident[:, 0:FOX_HEADS]))

                its = list(items())
                v.memset(o[DEC:P, 2, :], 0.0).then_inc(L["o_zeroed"], 1)

                def row_max(j, p, t):
                    dve.wait_ge(L["scores_done"], B["scores_done"] + j + 1)
                    if l == 0:
                        dve.wait_ge(L["bias_ready"], B["bias_ready"] + p + 1)
                    else:
                        dve.wait_ge(L["alibi"], B["alibi"] + 16)
                    if j >= 3:
                        dve.wait_ge(L["dT_done"], B["dT_done"] + j - 2)
                    n, a = KEYS[t], BCOL[t]
                    s = 2 * (j % 2)
                    flat = ps[:, s:s + 2, :].rearrange("p b n -> p (b n)")
                    members = 2 if t < 2 else 1
                    for c in range(members):
                        src = flat[:, 0:n] if t == 2 else ps[:, s + c, 0:n]
                        ins = v.tensor_tensor_reduce(probs[:, j % 3, c * n:(c + 1) * n], src,
                                                     bias[:, (p % 2 if l == 0 else 1), a:a + n], 1.0, -3e38, ALU.add, ALU.max,
                                                     mx[:, j % 3, c:c + 1])
                    ins.then_inc(L["max_done"], 1)
                    dve.wait_ge(L["max_done"], B["max_done"] + j + 1)
                    v.tensor_scalar(nmx[:, j % 3, 0:members], mx[:, j % 3, 0:members], -SCALE, None, ALU.mult).then_inc(L["neg_done"], 1)

                def mix(j, p, t):
                    dve.wait_ge(L["exp_done"], B["exp_done"] + j + 1)
                    n = 2 if t < 2 else 1
                    r, sums = rs[:, j % 3, 0:n], sm[:, j % 3, 0:n]
                    if l == 1:
                        inv = v.reciprocal(r, sums)
                        if t == 2:
                            link(dve, "dve", inv)
                            inv = v.tensor_copy(rs[0:DEC, j % 3, 1:2], rs[DEC:P, j % 3, 0:1])
                        inv.then_inc(L["mixed"], 1)
                        return
                    link(dve, "dve", v.reciprocal(r, sums))
                    if t < 2:
                        w = KEYS[t]
                        link(dve, "dve", v.scalar_tensor_tensor(r[:, 1:2], r[:, 1:2], sums[:, 0:1], lamw[:, 5:6], ALU.mult, ALU.mult))
                        v.scalar_tensor_tensor(probs[:, j % 3, 0:w], probs[:, j % 3, w:2 * w], r[:, 1:2], probs[:, j % 3, 0:w],
                                               ALU.mult, ALU.add).then_inc(L["mixed"], 1)
                    else:
                        link(dve, "dve", v.tensor_tensor(r, r, lamw[:, 6:7], ALU.mult))
                        v.tensor_scalar(diag[:, :], ident2[:, :], r, None, ALU.mult).then_inc(L["mixed"], 1)

                def take_o(j, p, t):
                    dve.wait_ge(L["pv_done"], B["pv_done"] + j + 1)
                    n = ROWS[t]
                    cs = slice(p * P, (p + 1) * P)
                    if l == 0 and t < 2:
                        v.tensor_scalar(o[:, t, cs], ps[:, 6, 0:P], rs[:, j % 3, 0:1], None, ALU.mult).then_inc(L["o_done"], 1)
                    elif l == 0:
                        v.tensor_copy(o[0:n, t, cs], ps[0:n, 6, 0:P]).then_inc(L["o_done"], 1)
                    else:
                        dve.wait_ge(L["mixed"], B["mixed"] + j + 1)
                        for c in range(2):
                            hs = slice(p * P + c * HD, p * P + (c + 1) * HD)
                            ins = v.scalar_tensor_tensor(o[0:n, t, hs], ps[0:n, 6, c * HD:(c + 1) * HD], rs[0:n, j % 3, c:c + 1],
                                                         gate[0:n, t, hs], ALU.mult, ALU.mult)
                        ins.then_inc(L["o_done"], 1)

                def norm_head(j, p, t):
                    dve.wait_ge(L["o_r"], B["o_r"] + j + 1)
                    vw = o[:, t, p * P:(p + 1) * P]
                    v.scalar_tensor_tensor(vw, vw, rr[0][:, j:j + 1], subln[:, :], ALU.mult, ALU.mult).then_inc(L["o_normed"], 1)

                if l == 1:
                    dve.wait_ge(L["g_done"], B["g_done"] + 6)
                row_max(*its[0])
                row_max(*its[1])
                dve.wait_ge(L["o_zeroed"], B["o_zeroed"] + 1)
                for j, p, t in its:
                    if j >= 2:
                        take_o(*its[j - 2])
                    mix(j, p, t)
                    if j + 2 < len(its):
                        row_max(*its[j + 2])
                    if l == 0 and j >= 7:
                        norm_head(*its[j - 7])
                take_o(*its[-2])
                take_o(*its[-1])
                if l == 0:
                    for item in its[-7:]:
                        norm_head(*item)
                for i in range(2 * TILES):
                    t, half = divmod(i, 2)
                    dve.wait_ge(L["o_hi"], B["o_hi"] + i + 1)
                    a, b_ = slice(4 * half, 4 * half + 4), slice(t * P, (t + 1) * P)
                    v.tensor_tensor(oT_lo[:, a, b_], ps[:, i, :].rearrange("p (k n) -> p k n", k=4), oT_hi[:, a, b_].bitcast(F32),
                                    ALU.subtract).then_inc(L["o_lo"], 1)
                for b in range(OUT_BLOCKS):
                    if b == 0:
                        split_slab(BASE_OUT[l], 2)
                    else:
                        split_lo(Unit(BASE_OUT[l], 6))
                    for t in range(TILES):
                        wait_sum(dve, B, "out_done", BASE_OUT[l], b, t)
                        xs = x[:, t, b * F:(b + 1) * F]
                        v.tensor_tensor(xs, xs, acc(b, t), ALU.add).then_inc(L["x_mid"], 1)

                dve.wait_ge(gain_loaded[l][1], 16)
                if l == 0:
                    dve.wait_ge(small_loaded, 16 * SMALL)
                norm(B, "rstd1", 1, l, h2, "h_ready1")
                split_lo(Unit(BASE_OUT[l], 7))
                for t in range(TILES):
                    dve.wait_ge(L["h2hi"], B["h2hi"] + t + 1)
                    v.tensor_tensor(h2_lo[:, t, :], h2[:, t, :], h2_hi[:, t, :].bitcast(F32), ALU.subtract).then_inc(L["h2lo"], 1)
                K = lambda ins: link(dve, "dve", ins)
                b4 = lambda ap: ap.unsqueeze(2).to_broadcast([P, 3, 4])
                prio3 = prio.unsqueeze(1).to_broadcast([P, 3, 4])

                def first_of(dst, vals, top_):
                    K(v.tensor_tensor(t4, vals, b4(top_), ALU.is_equal))
                    K(v.tensor_tensor(t4, t4, prio3, ALU.mult))
                    K(v.tensor_reduce(dv, t4, AX, ALU.max))
                    K(v.tensor_tensor(dst, t4, b4(dv), ALU.is_equal))

                dve.wait_ge(L["logits"], B["logits"] + 1)
                K(v.tensor_tensor(lg, ps[:, 6, 0:60].rearrange("p (t n) -> p t n", t=3), b_router[:, l, :].unsqueeze(1).to_broadcast([P, 3, 20]), ALU.add))
                gl = lg[:, :, 0:4]
                K(v.tensor_reduce(gmx, gl, AX, ALU.max))
                v.tensor_tensor(gd, gl, b4(gmx), ALU.subtract).then_inc(L["logit_sb"], 1)
                first_of(oh, gl, gmx)
                v.tensor_tensor(oh, oh, b4(valid), ALU.mult).then_inc(L["onehot"], 1)
                dve.wait_ge(L["onehot"], B["onehot"] + 1)
                dve.wait_ge(L["ranks"], B["ranks"] + 1)
                K(v.tensor_tensor(t4, ps[:, 7, 0:12].rearrange("p (t g) -> p t g", t=3), oh, ALU.mult))
                K(v.tensor_tensor(t4b, t4, oh, ALU.add))
                K(v.tensor_scalar(pos, t4b, -1.0, None, ALU.add))

                def build_pick(g):
                    K_ = v.tensor_copy(pos_g[:, :], pos[:, :, bass.ds(g, 1)].rearrange("p t g -> p (t g)"))
                    K_.then_inc(L["pos_copied"], 1)
                    dve.wait_ge(L["pos_copied"], B["pos_copied"] + g + 1)
                    for t in range(TILES):
                        ins = v.tensor_scalar(pick[:, t, :], iota, pos_g[:, t:t + 1], None, ALU.is_equal)
                    ins.then_inc(L["pick_ready"], 1)

                build_pick(0)
                K(v.tensor_reduce(rank, t4, AX, ALU.add))
                K(v.tensor_reduce(total, ps[:, 7, 12:16], AX, ALU.max))
                v.tensor_scalar(flag[0:1, 0:1], total[0:1, :], float(CAP), None, ALU.is_gt).then_inc(OV[l]["flag_ready"], 1)
                K(v.tensor_scalar(over, rank, float(CAP), None, ALU.is_ge))
                for gi in range(GROUPS):
                    K(v.tensor_tensor(t16[:, 12 * gi:12 * gi + 12].rearrange("p (t e) -> p t e", t=3), lg[:, :, 4 + 4 * gi:8 + 4 * gi],
                                      oh[:, :, gi:gi + 1].to_broadcast([P, 3, 4]), ALU.mult))
                K(v.tensor_tensor(t16[:, 0:24], t16[:, 0:24], t16[:, 24:48], ALU.add))
                K(v.tensor_tensor(ig, t16[:, 0:12].rearrange("p (t e) -> p t e", t=3), t16[:, 12:24].rearrange("p (t e) -> p t e", t=3), ALU.add))
                K(v.tensor_reduce(v1, ig, AX, ALU.max))
                first_of(oh1, ig, v1)
                K(v.scalar_tensor_tensor(ig2, oh1, -1e30, ig, ALU.mult, ALU.add))
                K(v.tensor_reduce(v2, ig2, AX, ALU.max))
                first_of(oh2, ig2, v2)
                v.tensor_tensor(dv, v2, v1, ALU.subtract).then_inc(L["logit_sb"], 1)

                def gate_weights():
                    dve.wait_ge(L["gexp"], B["gexp"] + 1)
                    K(v.tensor_reduce(gsum, ge, AX, ALU.add))
                    K(v.reciprocal(ptop, gsum))
                    dve.wait_ge(L["gexp"], B["gexp"] + 2)
                    K(v.tensor_scalar(w1, e2, 1.0, None, ALU.add))
                    K(v.reciprocal(w1, w1))
                    K(v.tensor_tensor(w1, w1, ptop, ALU.mult))
                    K(v.tensor_tensor(w2, w1, e2, ALU.mult))
                    K(v.tensor_tensor(t4, oh1, b4(w1), ALU.mult))
                    K(v.tensor_tensor(t4b, oh2, b4(w2), ALU.mult))
                    K(v.tensor_tensor(gate4, t4, t4b, ALU.add))
                    K(v.tensor_copy(gates_hl[:, :, 0:4], gate4))
                    v.tensor_tensor(gates_hl[:, :, 4:8], gate4, gates_hl[:, :, 0:4].bitcast(F32), ALU.subtract).then_inc(L["routed"], 1)

                def hidden(order, e, g):
                    wait_matrix(dve, l, order, ("u", e), g)
                    dve.wait_ge(L["silu_done"], B["silu_done"] + g * 4 + e + 1)
                    dve.wait_ge(L["slot_gated"], B["slot_gated"] + g + (2 if e == PER_GROUP else 1))
                    ge_ = slot_gate[:, e % PER_GROUP:e % PER_GROUP + 1]
                    v.scalar_tensor_tensor(hid[:, :], act_g[:, :], ge_, ps[:, 1, :], ALU.mult, ALU.mult).then_inc(L["hid_done"], 1)

                def hidden_lo(e, g):
                    dve.wait_ge(L["hT_hi"], B["hT_hi"] + g * 4 + e + 1)
                    v.tensor_tensor(hidT_lo[:, :, :].rearrange("p k n -> p (k n)"), ps[:, 2, :],
                                    hidT_hi[:, :, :].rearrange("p k n -> p (k n)").bitcast(F32), ALU.subtract).then_inc(L["hT_lo"], 1)

                def gathered_lo(g):
                    for i in range(2):
                        dve.wait_ge(L["x_hi"], B["x_hi"] + g * 2 + i + 1)
                        xs = slice(4 * i, 4 * i + 4)
                        v.tensor_tensor(xT_lo[:, xs, :].rearrange("p k n -> p (k n)"), ps[:, 5 + i, :],
                                        xT_hi[:, xs, :].rearrange("p k n -> p (k n)").bitcast(F32), ALU.subtract).then_inc(L["x_lo"], 1)

                def take_gates(g, first=False):
                    dve.wait_ge(L["slot_done"], B["slot_done"] + g + 1)
                    if not first:
                        dve.wait_ge(L["hid_done"], B["hid_done"] + g * 4)
                    v.tensor_reduce(slot_gate[:, :], ps[:, 7, 384:392].rearrange("p (a e) -> p e a", a=2), AX, ALU.add).then_inc(L["slot_gated"], 1)

                def add_back(g):
                    for i in range(2 * TILES):
                        t, c = divmod(i, 2)
                        dve.wait_ge(L["back_done"], B["back_done"] + g * 6 + i + 1)
                        xs = x[:, t, c * F:(c + 1) * F]
                        v.tensor_tensor(xs, xs, ps[:, BACK[i], :], ALU.add).then_inc(L["x_added"], 1)

                def take_pickT():
                    v.tensor_copy(pickT[:, :, :].rearrange("p t n -> p (t n)"), ps[:, 7, 0:384]).then_inc(L["pickT_taken"], 1)

                def moe_round(order, g):
                    last = order is LAST
                    for m, (kind, e) in enumerate(order):
                        ahead = not (last and m >= len(order) - 2 and l == 1)
                        if ahead:
                            split_lo(Unit(BASE_MOE[l], 2 * (m + 4), g))
                        if kind == "u" and e < PER_GROUP:
                            hidden(order, e, g)
                        if (kind, e) in (("g", 1), ("g", 2), ("g", 3)):
                            hidden_lo(e - 1, g)
                        if (kind, e) == ("u", 1) and not last:
                            build_pick(g + 1)
                        if (kind, e) == ("u", 3) and not last:
                            gathered_lo(g + 1)
                            take_gates(g + 1)
                        if (kind, e) == ("d", 2):
                            hidden_lo(3, g)
                        if (kind, e) == ("d", 3):
                            for i in range(2):
                                dve.wait_ge(L["y_hi"], B["y_hi"] + g * 2 + i + 1)
                                cs = slice(i * F, (i + 1) * F)
                                v.tensor_tensor(y_lo[:, cs], ps[:, 3 + i, :], y_hi[:, cs].bitcast(F32), ALU.subtract).then_inc(L["y_lo"], 1)
                        if (kind, e) == ("u", PER_GROUP):
                            hidden(order, e, g)
                            add_back(g)
                            take_pickT()
                        if ahead and not (last and m == len(order) - 1):
                            split_lo(Unit(BASE_MOE[l], 2 * (m + 4) + 1, g))
                    if last:
                        add_back(g)

                gathered_lo(0)
                gate_weights()
                take_gates(0, first=True)
                take_pickT()
                split_slab(BASE_MOE[l], 2)
                hidden(FIRST, 0, 0)
                split_slab(BASE_MOE[l], 3)
                with dve.Fori(0, GROUPS - 1) as g:
                    moe_round(ORDER, g)
                moe_round(LAST, GROUPS - 1)

                dve.wait_ge(OV[l]["flag_ready"], 1)
                flag_v = dve.value_load(flag[0:1, 0:1])
                kept = chain["dve"]
                with dve.If(flag_v > 0):
                    v.tensor_tensor(t4, gate4, b4(over), ALU.mult).then_inc(OV[l]["over_done"], 1)
                    dve.wait_ge(OV[l]["over_done"], 1)
                    for gi in range(GROUPS):
                        ins = v.tensor_tensor(over_gate[:, :, 4 * gi:4 * gi + 4], t4, oh[:, :, gi:gi + 1].to_broadcast([P, 3, 4]), ALU.mult)
                    ins.then_inc(OV[l]["over_done"], 1)
                    with dve.Fori(0, EXPERTS) as e:
                        dve.wait_ge(OV[l]["over_done"], e + 2)
                        v.tensor_copy(over_col[:, :], over_gate[:, :, bass.ds(e, 1)].rearrange("p t e -> p (t e)")).then_inc(OV[l]["over_done"], 1)
                        dve.wait_ge(OV[l]["over_done"], e + 3)
                        for t in range(TILES):
                            dve.wait_ge(OV[l]["over_used"], e * 18 + 6 * t + 5)
                            dve.wait_ge(OV[l]["over_act"], e * TILES + t + 1)
                            v.scalar_tensor_tensor(hid[:, :], act_g[:, :], over_col[:, t:t + 1], ps[:, 1, :], ALU.mult, ALU.mult).then_inc(OV[l]["over_hid"], 1)
                            dve.wait_ge(OV[l]["over_used"], e * 18 + 6 * t + 7)
                            for c in range(2):
                                xs = x[:, t, c * F:(c + 1) * F]
                                ins = v.tensor_tensor(xs, xs, ps[:, 3 + c, :], ALU.add)
                            ins.then_inc(OV[l]["over_x"], 1)
                assert chain["dve"] == kept


_OUT_SHAPES = [
    ("y_prompt", (1, SEQ, D)), ("y_sample", (1, DEC, D)),
    ("new_diff_k_prompt", (1, 1, SEQ, 8, 128)), ("new_diff_v_prompt", (1, 1, SEQ, 8, 128)),
    ("new_fox_k_prompt", (1, 1, SEQ, 16, 64)), ("new_fox_v_prompt", (1, 1, SEQ, 16, 64)),
    ("new_fox_logf_prompt", (1, 1, SEQ, 16)),
    ("new_diff_k_sample", (1, 1, DEC, 8, 128)), ("new_diff_v_sample", (1, 1, DEC, 8, 128)),
    ("new_fox_k_sample", (1, 1, DEC, 16, 64)), ("new_fox_v_sample", (1, 1, DEC, 16, 64)),
    ("new_fox_logf_sample", (1, 1, DEC, 16)),
]


def kernel(**inputs):
    import concourse.bacc as _bacc
    from concourse.bass_utils import run_bass_kernel_spmd as _run

    nc = _bacc.Bacc("TRN2", target_bir_lowering=False, num_devices=1)
    arrays, aps = {}, {}
    host = {name: np.ascontiguousarray(a) for name, a in inputs.items()}
    host["c_consts"], host["c_dist"], host["c_mask"] = constants()
    for name, a in host.items():
        arrays[f"in_{name}"] = a
        aps[name] = nc.dram_tensor(f"in_{name}", a.shape, mybir.dt.from_np(a.dtype), kind="ExternalInput").ap()
    for name, shape in _OUT_SHAPES:
        aps[name] = nc.dram_tensor(f"out_{name}", shape, F32, kind="ExternalOutput").ap()
    build(nc, aps)
    r = _run(nc, [arrays], core_ids=[0])
    return tuple(r.results[0][f"out_{name}"] for name, _ in _OUT_SHAPES)
```

```python
from contextlib import ExitStack
import math

import numpy as np
import concourse.bass as bass
from concourse import mybir

F32 = mybir.dt.float32
F32R = mybir.dt.float32r
I32 = mybir.dt.int32
ALU = mybir.AluOpType
ACT = mybir.ActivationFunctionType
AX = mybir.AxisListType.X

P = 128
D = 1024
SEQ, DEC, PAST = 256, 64, 512
TILES = 3
TOK = TILES * P
KB = D // P
HD = 64
PAIRS = D // P
FOX_HEADS = 16
GROUPS, PER_GROUP, EXPERTS = 4, 4, 16
F = 512
EPS = 1e-6
SCALE = HD ** -0.5
CHUNK = 64
CAP = 128
LAMBDA_INIT = 0.8 - 0.6 * math.exp(0.0)
ROWS = [128, 128, 64]
PTILES = PAST // P
SMALL = 9

RAW, HI = 6, 4
UNIT = 2048
PER_LOOP = 2 * 3 * PER_GROUP
IN_BLOCKS = [6, 8]
OUT_BLOCKS = D // F
BASE_IN, BASE_OUT, BASE_MOE = [0, 0], [0, 0], [0, 0]
_n = 0
for _l in range(2):
    BASE_IN[_l] = _n
    BASE_OUT[_l] = BASE_IN[_l] + 2 * IN_BLOCKS[_l]
    BASE_MOE[_l] = BASE_OUT[_l] + 2 * OUT_BLOCKS
    _n = BASE_MOE[_l] + GROUPS * PER_LOOP
UNITS = _n

FIRST = [("g", 0), ("u", 0)]
ORDER = [("g", 1), ("u", 1), ("d", 0), ("g", 2), ("u", 2), ("d", 1), ("g", 3), ("u", 3), ("d", 2),
         ("g", 4), ("d", 3), ("u", 4)]
DT_BANK = [4, 7]
BACK = [5, 6, 3, 4, 2, 5]
LAST = [m for m in ORDER if m[1] < PER_GROUP]

C_ID, C_IOTA, C_TRI, C_BEFORE, C_AFTER, C_ONE = (i * P for i in range(6))
C_VALID = 6 * P
C_PRIO = C_VALID + TILES
C_WIDTH = C_PRIO + 4 + 1
KEYS = [128, 256, 576]
BCOL = [0, 128, 384]
BIAS = 960


def constants():
    c = np.zeros((P, C_WIDTH), np.float32)
    i = np.arange(P)
    c[:, C_ID:C_ID + P] = np.eye(P)
    c[:, C_IOTA:C_IOTA + P] = np.where(i < CAP, i, -7)[None]
    c[:, C_TRI:C_TRI + P] = i[:, None] <= i[None]
    c[:, C_BEFORE:C_BEFORE + P] = i[:, None] < i[None]
    c[:, C_AFTER:C_AFTER + P] = i[:, None] > i[None]
    c[:, C_ONE:C_ONE + P] = 1
    c[:, C_VALID:C_VALID + TILES] = 1
    c[DEC:, C_VALID + 2] = 0
    c[:, C_PRIO:C_PRIO + 4] = [4, 3, 2, 1]
    dist = np.zeros((P, BIAS), np.float32)
    mask = np.zeros((P, BIAS), np.float32)
    for t, (keys, at, q0) in enumerate(zip(KEYS, BCOL, (0, P, PAST))):
        q = q0 + (i if t < 2 else i % DEC)[:, None]
        k = np.arange(keys)[None]
        dist[:, at:at + keys] = np.where(k // CHUNK <= q // CHUNK, -np.abs(q - k) / SCALE, -1e34)
        mask[:, at:at + keys] = np.where(k <= q, 0, -1e30 / SCALE)
    return c, dist, mask


class Unit:

    def __init__(self, base, i, g=0):
        n = base + i
        self.slot, self.hslot, self.static = n % RAW, n % HI, n
        self.n = g * PER_LOOP + n
        self.arrivals = g * (16 * PER_LOOP // RAW) + 16 * (n // RAW + 1)


def build(nc, A):
    with ExitStack() as ctx:
        S = lambda name: ctx.enter_context(nc.semaphore(name))

        start = (nc.sbuf_base + 63) // 32 * 32
        at = [start]

        def sb(name, shape, dt=F32, offset=None):
            size = (int(np.prod(shape[1:])) * 4 + 31) // 32 * 32
            if offset is None:
                offset = at[0]
                at[0] += size
            return nc.alloc_sbuf_tensor_at(name, shape, dt, offset=offset)

        ring_at = at[0]
        w_raw = sb("w_raw", [P, RAW, UNIT])
        w_lo = sb("w_lo", [P, RAW, UNIT], F32R, offset=ring_at)
        w_hi = sb("w_hi", [P, HI, UNIT], F32R)
        x = sb("x", [P, TILES, D])
        cst = sb("cst", [P, C_WIDTH])
        ident = cst[:, C_ID:C_ID + P]
        iota = cst[:, C_IOTA:C_IOTA + P]
        tri = cst[:, C_TRI:C_TRI + P]
        before = cst[:, C_BEFORE:C_BEFORE + P]
        after = cst[:, C_AFTER:C_AFTER + P]
        ones = cst[:, C_ONE:C_ONE + P]
        valid = cst[:, C_VALID:C_VALID + TILES]
        prio = cst[:, C_PRIO:C_PRIO + 4]
        neghalf = sb("neghalf", [P, 24])
        gain_at = at[0]
        gain = sb("gain", [P, 2, D])
        qk_gain = sb("qk_gain", [P, 4, HD])
        own_at = at[0]
        subln = sb("subln", [P, P])
        lamv = sb("lamv", [P, 4, HD])
        lamw = sb("lamw", [P, 8])
        ident2 = sb("ident2", [P, HD])
        diag = sb("diag", [P, DEC])
        o_sq = sb("o_sq", [P, 2, P])
        dist = sb("dist", [P, BIAS])
        own_end = at[0]
        at[0] = own_at
        pick_heads = sb("pick_heads", [FOX_HEADS, PAIRS, P], F32R)
        w_f = sb("w_f", [P, KB, FOX_HEADS])
        w_f_hi = sb("w_f_hi", [P, KB, FOX_HEADS], F32R)
        w_f_lo = sb("w_f_lo", [P, KB, FOX_HEADS], F32R)
        lf = sb("lf", [P, 7, TILES * FOX_HEADS])
        logf = sb("logf", [P, TILES, FOX_HEADS])
        logf_past = sb("logf_past", [P, PTILES, FOX_HEADS])
        at[0] = max(at[0], own_end)
        w_router = sb("w_router", [P, 2, KB, 20])
        b_router = sb("b_router", [P, 2, 20])
        b_forget = sb("b_forget", [P, FOX_HEADS])
        ident_r = sb("ident_r", [P, FOX_HEADS], F32R)
        stat = sb("stat", [P, 160])
        ss, mean, rstd = stat[:, 0:3], stat[:, 3:6], stat[:, 6:9]
        mx, nmx, sm, rs = (stat[:, a:a + 6].rearrange("p (j c) -> p j c", j=3) for a in (12, 18, 24, 30))
        ms = [stat[:, 40 + 24 * i:64 + 24 * i] for i in range(2)]
        rr = [stat[:, 88 + 24 * i:112 + 24 * i] for i in range(2)]
        flag = sb("flag", [1, 8], I32)
        region = at[0]

        hT_hi = sb("hT_hi", [P, KB, TOK], F32R, offset=region)
        hT_lo = sb("hT_lo", [P, KB, TOK], F32R, offset=region + 12288)
        oT_hi = sb("oT_hi", [P, KB, TOK], F32R, offset=region)
        oT_lo = sb("oT_lo", [P, KB, TOK], F32R, offset=region + 12288)
        bias = sb("bias", [P, 2, BIAS], offset=region + 3840)
        probs = sb("probs", [P, 3, 576], offset=region + 11520)
        dT = sb("dT", [P, 2, 640], offset=region + 18432)
        assert 18432 + 5120 <= 24576
        at[0] = region + 24576
        h_at = at[0]
        h = sb("h", [P, TILES, D])
        o = sb("o", [P, TILES, D], offset=h_at)
        low_rows = sb("low_rows", [DEC, 2, F], offset=h_at + 8 * D)
        k_past = sb("k_past", [P, 2, PTILES, P])
        v_past = sb("v_past", [P, 2, PTILES, P])
        kT_past = sb("kT_past", [P, 2, PAST])
        qT = sb("qT", [P, PAIRS, SEQ])
        low_out = sb("low_out", [DEC, 2, F], offset=at[0])
        q_diag = sb("q_diag", [P, PAIRS, P])
        kT_new = sb("kT_new", [P, PAIRS, SEQ + DEC])
        v_new = sb("v_new", [P, TILES, D])
        qk_at = at[0]
        qk = sb("qk", [P, 2, TILES, F])
        gate = sb("gate", [P, TILES, D], offset=qk_at)
        off_hi = sb("off_hi", [FOX_HEADS, 832], F32R, offset=gain_at)
        off_lo = sb("off_lo", [FOX_HEADS, 832], F32R, offset=gain_at + 4 * D)
        top = at[0]

        at[0] = region
        xT_hi = sb("xT_hi", [P, KB, P], F32R)
        xT_lo = sb("xT_lo", [P, KB, P], F32R)
        pick = sb("pick", [P, TILES, P], F32R)
        pickT = sb("pickT", [P, TILES, P], F32R)
        act_g = sb("act_g", [P, F])
        hid = sb("hid", [P, F])
        hidT_hi = sb("hidT_hi", [P, 4, P], F32R)
        hidT_lo = sb("hidT_lo", [P, 4, P], F32R)
        r_ = sb("router", [P, 640])
        gates_hl = sb("gates_hl", [P, TILES, 8], F32R)
        slot_gate = sb("slot_gate", [P, 4])
        pos_g = sb("pos_g", [P, TILES])
        over_gate = sb("over_gate", [P, TILES, EXPERTS])
        over_col = sb("over_col", [P, TILES])
        assert at[0] <= h_at
        at[0] = h_at
        h2 = sb("h2", [P, TILES, D])
        h2_hi = sb("h2_hi", [P, TILES, D], F32R)
        h2_lo = sb("h2_lo", [P, TILES, D], F32R)
        h2T = sb("h2T", [P, KB, TOK])
        slots_at = at[0]
        x_slots = sb("x_slots", [P, D])
        at[0] = slots_at
        hidT_last_hi = sb("hidT_last_hi", [P, 4, P], F32R)
        hidT_last_lo = sb("hidT_last_lo", [P, 4, P], F32R)
        y_hi = sb("y_hi", [P, D], F32R)
        y_lo = sb("y_lo", [P, D], F32R)
        over_w = sb("over_w", [P, UNIT])
        over_hT = sb("over_hT", [P, F])
        top = max(top, at[0])
        assert top <= nc.sbuf_usable_end, (top, nc.sbuf_usable_end)
        rcol = [0]

        def rt(*shape):
            n = int(np.prod(shape))
            ap = r_[:, rcol[0]:rcol[0] + n]
            rcol[0] += n
            if len(shape) == 2:
                ap = ap.rearrange("p (a b) -> p a b", a=shape[0])
            return ap

        lg = rt(3, 20)
        gmx, gsum, ptop, v1, v2, dv, e2, w1, w2, rank, over = (rt(3) for _ in range(11))
        gd, ge, oh, ig, oh1, oh2, ig2, t4, gate4, t4b = (rt(3, 4) for _ in range(10))
        pos = rt(3, 4)
        total = rt(1)
        t16 = rt(48)

        ps = ctx.enter_context(nc.psum_tensor("ps", [P, 8, 512], F32))

        raw_ready = [S(f"raw_ready{i}") for i in range(RAW)]
        hi_ready, lo_ready, units_used = S("hi_ready"), S("lo_ready"), S("units_used")
        ident_loaded, const_loaded, small_loaded = S("ident_loaded"), S("const_loaded"), S("small_loaded")
        x_loaded = [S(f"x_loaded{t}") for t in range(TILES)]
        qk_gains_loaded, lam_loaded = S("qk_gains_loaded"), S("lam_loaded")
        gain_loaded = [[S(f"gain_loaded{l}{i}") for i in range(2)] for l in range(2)]
        x_padded, halves_ready = S("x_padded"), S("halves_ready")
        lam_dots, lam_exps = S("lam_dots"), S("lam_exps")
        dve_chain, pool_chain = S("dve_chain"), S("pool_chain")
        chain = {"dve": 0, "pool": 0}

        def link(eng, which, ins):
            chain[which] += 1
            s = dve_chain if which == "dve" else pool_chain
            ins.then_inc(s, 1)
            eng.wait_ge(s, chain[which])

        per_layer = dict(
            sq0=3, rstd0=3, h_ready0=3, tr0=6, hi0=6, lo0=6, proj_done=12, low_moved=6, low_added=6, qk_sq=12, qk_ms=12, qk_r=4, qk_n1=12,
            qk_normed=12, qk_tr=12, qk_evac=12, v_copied=6, g_done=0, k_stored=16 * 2 * TILES, v_stored=16 * TILES,
            k_loaded0=64, k_loaded1=64, v_loaded0=64, v_loaded1=64,
            q_zeroed=1, bias_ready=8, alibi=16, past_tr=8, past_ev=8, scores_done=24, max_done=24, neg_done=24, exp_done=24,
            mixed=24, dT_done=24, dT_copied=24, pv_done=24, o_done=24, o_zeroed=1, o_sqd=24, o_r=24, o_normed=24, o_tr=6,
            o_hi=6, o_lo=6, out_done=4, low_out_moved=2, x_mid=6,
            sq1=3, rstd1=3, h_ready1=3, tr1=6, ev1=6, h2hi=3, h2lo=3, logits=1, logit_sb=2, gexp=2, onehot=1, ranks=2,
            routed=1, pos_copied=4, pickT_taken=4, pick_ready=4, gathered=8, slots_copied=8, slots_tr=8, slot_done=4, slot_gated=4, x_hi=8, x_lo=8, silu_done=16, hid_done=16,
            hT_done=16, hT_hi=16, hT_lo=16, y_hi=8, y_lo=8, back_done=24, x_added=24)
        L = {name: S(name) for name in per_layer}
        BEFORE = [{name: l * n for name, n in per_layer.items()} for l in range(2)]
        OV = [{name: S(f"{name}{l}") for name in ("flag_ready", "over_load", "over_used", "over_act", "over_hid", "over_tr",
                                                  "over_ht", "over_done", "over_x")} for l in range(2)]
        fox = {name: S(f"fox_{name}") for name in ("wf_loaded", "lp_loaded", "wf_hi", "wf_lo", "f_done", "f_z", "f_exp",
                                                   "logf_ready", "logf_stored", "heads_ready", "off_done", "off_hi", "off_lo")}
        stores_done = S("stores_done")

        W_IN = [A["diff_w_in"][0], A["fox_w_in"][0]]
        W_OUT = [A["diff_w_out"][0], A["fox_w_out"][0]]
        K_CACHE = [A["cache_diff_k"].rearrange("a b s h d -> (a b s) (h d)"), A["cache_fox_k"].rearrange("a b s h d -> (a b s) (h d)")]
        V_CACHE = [A["cache_diff_v"].rearrange("a b s h d -> (a b s) (h d)"), A["cache_fox_v"].rearrange("a b s h d -> (a b s) (h d)")]
        K_OUT = [[A[n].rearrange("a b s h d -> (a b s) (h d)") for n in ("new_diff_k_prompt", "new_diff_k_sample")],
                 [A[n].rearrange("a b s h d -> (a b s) (h d)") for n in ("new_fox_k_prompt", "new_fox_k_sample")]]
        V_OUT = [[A[n].rearrange("a b s h d -> (a b s) (h d)") for n in ("new_diff_v_prompt", "new_diff_v_sample")],
                 [A[n].rearrange("a b s h d -> (a b s) (h d)") for n in ("new_fox_v_prompt", "new_fox_v_sample")]]
        x_p = A["x_prompt"][0]
        x_s = A["x_sample"][0]

        def token_rows(prompt, sample, t):
            return prompt[t * P:(t + 1) * P, :] if t < 2 else sample[0:DEC, :]

        def items():
            for j in range(3 * PAIRS):
                yield j, j // 3, j % 3

        def new_keys_T(j, l):
            if l == 0:
                return ps[0:DEC, DT_BANK[j % 2], 4 * DEC:5 * DEC]
            return ps[0:DEC, 5, 0:P]

        def hi_part(dst, i):
            t, half = divmod(i, 2)
            n, ks = ROWS[t], slice(4 * half, 4 * half + 4)
            return dst[:, ks, t * P:t * P + n], ps[:, i, :].rearrange("p (k n) -> p k n", k=4)[:, :, 0:n]

        def lo_part(dst_hi, dst_lo, i):
            t, half = divmod(i, 2)
            ks = slice(4 * half, 4 * half + 4)
            if t < 2:
                return dst_lo[:, ks, t * P:(t + 1) * P]
            return dst_hi[:, ks, 2 * P + DEC:3 * P]

        def in_kind(b):
            return "qqkkvvgg"[b]

        def acc(b, t):
            return ps[:, 3 * (b % 2) + t, :]

        def src_proj(w, b, half):
            return w[half * 512:(half + 1) * 512, b * F:(b + 1) * F].rearrange("(k p) n -> p k n", p=P)

        def src_moe(l, e, kind, half):
            name = {"g": "moe_w_gate", "u": "moe_w_up", "d": "moe_w_down"}[kind]
            w = A[name][l]
            w = w[bass.ds(e, 1), :, :]
            n = 512 if kind != "d" else 256
            return w[:, half * n:(half + 1) * n, :].rearrange("e (k p) n -> p (e k) n", p=P)

        def wait_sum(eng, B, name, base, b, t):
            if t < TILES - 1:
                eng.wait_ge(L[name], B[name] + 2 * b + t + 1)
            else:
                eng.wait_ge(units_used, Unit(base, 2 * b + 1).n + 1)

        def wait_matrix(eng, l, order, what, g):
            m0 = 0 if order is FIRST else 2
            eng.wait_ge(units_used, Unit(BASE_MOE[l], 2 * (m0 + order.index(what)) + 1, g).n + 1)

        def raw_view(slot, kind):
            return w_raw[:, slot, :].rearrange("p (k n) -> p k n", n=F if kind != "d" else D)

        block = ctx.enter_context(nc.Block())

        @block.sync
        def _(sp):
            for t in range(TILES):
                sp.dma_start(x[0:ROWS[t], t, :], token_rows(x_p, x_s, t)).then_inc(x_loaded[t], 16)
            sp.dma_start(gain[:, 0, :], A["norm_mix"][0, :].partition_broadcast(P)).then_inc(gain_loaded[0][0], 16)
            sp.dma_start(ident, A["c_consts"][:, C_ID:C_ID + P]).then_inc(ident_loaded, 16)

            def load_unit(U, kind, src):
                if U.static >= RAW:
                    sp.wait_ge(units_used, U.n - RAW + 1)
                sp.dma_start(raw_view(U.slot, kind), src).then_inc(raw_ready[U.slot], 16)

            def load_matrices(l, order, m0, g):
                for m, (kind, e) in enumerate(order):
                    for half in range(2):
                        load_unit(Unit(BASE_MOE[l], 2 * (m0 + m) + half, g), kind, src_moe(l, g * PER_GROUP + e, kind, half))

            for l in range(2):
                for b in range(2 * l, IN_BLOCKS[l]):
                    if l == 0 and b == 1:
                        sp.dma_start(cst[:, C_ID + P:], A["c_consts"][:, C_ID + P:]).then_inc(const_loaded, 16)
                    for half in range(2):
                        load_unit(Unit(BASE_IN[l], 2 * b + half), "p", src_proj(W_IN[l], b, half))
                for b in range(OUT_BLOCKS):
                    for half in range(2):
                        load_unit(Unit(BASE_OUT[l], 2 * b + half), "p", src_proj(W_OUT[l], b, half))
                load_matrices(l, FIRST, 0, 0)
                with sp.Fori(0, GROUPS - 1) as g:
                    load_matrices(l, ORDER, 2, g)
                load_matrices(l, LAST, 2, GROUPS - 1)
                if l == 0:
                    for b in range(2):
                        for half in range(2):
                            load_unit(Unit(BASE_IN[1], 2 * b + half), "p", src_proj(W_IN[1], b, half))
                sp.wait_ge(OV[l]["flag_ready"], 1)
                flag_v = sp.value_load(flag[0:1, 0:1])
                with sp.If(flag_v > 0):
                    with sp.Fori(0, EXPERTS) as e:
                        for t in range(TILES):
                            for j, (kind, half) in enumerate([("g", 0), ("g", 1), ("u", 0), ("u", 1), ("d", 0), ("d", 1)]):
                                sp.wait_ge(OV[l]["over_used"], e * 18 + 6 * t + j + 1)
                                sp.dma_start(over_w[:, :].rearrange("p (k n) -> p k n", n=F if kind != "d" else D),
                                             src_moe(l, e, kind, half)).then_inc(OV[l]["over_load"], 16)
                    sp.wait_ge(OV[l]["over_x"], EXPERTS * TILES)
            for t in range(TILES):
                sp.wait_ge(L["x_added"], 2 * 6 * GROUPS - 6 + 2 * t + 2)
                sp.dma_start(token_rows(A["y_prompt"][0], A["y_sample"][0], t), x[0:ROWS[t], t, :]).then_inc(stores_done, 16)
            sp.wait_ge(stores_done, 16 * TILES)

        @block.gpsimd
        def _(pool):
            pool.memset(neghalf[:, :], -0.5).then_inc(halves_ready, 1)
            pool.memset(stat[:, 40:136], 1.0).then_inc(halves_ready, 1)
            pool.wait_ge(halves_ready, 2)
            qk_gains = [
                (qk_gain[:, 0, :], A["diff_q_norm"][0, :].partition_broadcast(P)),
                (qk_gain[:, 1, :], A["diff_k_norm"][0, :].partition_broadcast(P)),
                (qk_gain[:, 2, :], A["fox_q_norm"][0, :].partition_broadcast(P)),
                (qk_gain[:, 3, :], A["fox_k_norm"][0, :].partition_broadcast(P)),
            ]
            head_vectors = [
                (subln[:, :], A["diff_subln"][0, :].partition_broadcast(P)),
                (lamv[:, 0, :], A["diff_lambda_q1"][0, :].partition_broadcast(P)),
                (lamv[:, 1, :], A["diff_lambda_k1"][0, :].partition_broadcast(P)),
                (lamv[:, 2, :], A["diff_lambda_q2"][0, :].partition_broadcast(P)),
                (lamv[:, 3, :], A["diff_lambda_k2"][0, :].partition_broadcast(P)),
            ]
            small = [(b_forget[:, :], A["fox_b_f"][0, :].partition_broadcast(P))]
            for l in range(2):
                small += [
                    (w_router[:, l, :, 0:4], A["moe_w_group"][l].rearrange("(k p) n -> p k n", p=P)),
                    (w_router[:, l, :, 4:20], A["moe_w_expert"][l].rearrange("(k p) n -> p k n", p=P)),
                    (b_router[:, l, 0:4], A["moe_b_group"][l, :].partition_broadcast(P)),
                    (b_router[:, l, 4:20], A["moe_b_expert"][l, :].partition_broadcast(P)),
                ]
            assert len(small) == SMALL

            def rms(B, squares, done):
                for t in range(TILES):
                    ts = slice(t, t + 1)
                    pool.wait_ge(L[squares], B[squares] + t + 1)
                    link(pool, "pool", pool.tensor_scalar(mean[:, ts], ss[:, ts], 1.0 / D, EPS, ALU.mult, ALU.add))
                    pool.tensor_tensor(rstd[:, ts], mean[:, ts], neghalf[:, 0:1], ALU.pow).then_inc(L[done], 1)

            for l in range(2):
                B = BEFORE[l]
                if l == 0:
                    for dst, src in qk_gains:
                        pool.dma_start(dst, src).then_inc(qk_gains_loaded, 16)
                rms(B, "sq0", "rstd0")
                pool.memset(q_diag[:, :, :], 0.0).then_inc(L["q_zeroed"], 1)
                if l == 1:
                    pool.dma_start(w_f[:, :, :], W_IN[1][:, 4 * D:4 * D + FOX_HEADS].rearrange("(k p) n -> p k n", p=P)).then_inc(fox["wf_loaded"], 16)
                    pool.dma_start(logf_past[:, :, :], A["cache_fox_logf"].rearrange("a b (i p) h -> p (a b i) h", p=P)).then_inc(fox["lp_loaded"], 16)

                def load_keys(p):
                    cols = slice(p * P, (p + 1) * P)
                    if p >= 2:
                        pool.wait_ge(L["past_tr"], B["past_tr"] + p - 1)
                    pool.dma_start(k_past[:, p % 2, :, :], K_CACHE[l][:, cols].rearrange("(i p) n -> p i n", p=P)).then_inc(L[f"k_loaded{p % 2}"], 16)

                def load_values(p):
                    cols = slice(p * P, (p + 1) * P)
                    if p >= 2:
                        pool.wait_ge(L["pv_done"], B["pv_done"] + 3 * (p - 2) + 3)
                    pool.dma_start(v_past[:, p % 2, :, :], V_CACHE[l][:, cols].rearrange("(i p) n -> p i n", p=P)).then_inc(L[f"v_loaded{p % 2}"], 16)

                for p in range(2):
                    load_keys(p)
                    load_values(p)
                if l == 0:
                    for dst, src in head_vectors:
                        pool.dma_start(dst, src).then_inc(lam_loaded, 16)
                    pool.dma_start(dist[:, :], A["c_dist"]).then_inc(L["alibi"], 16)
                    pool.dma_start(gain[:, 1, :], A["norm_ffn"][0, :].partition_broadcast(P)).then_inc(gain_loaded[0][1], 16)
                    pool.wait_ge(L["h_ready0"], B["h_ready0"] + TILES)
                    pool.dma_start(gain[:, 0, :], A["norm_mix"][1, :].partition_broadcast(P)).then_inc(gain_loaded[1][0], 16)
                pool.wait_ge(L["tr0"], B["tr0"] + 2 * TILES)
                pool.wait_ge(L["q_zeroed"], B["q_zeroed"] + 1)
                pool.memset(o[DEC:P, 2, :], 0.0).then_inc(L["o_zeroed"], 1)
                pool.wait_ge(L["o_zeroed"], B["o_zeroed"] + 1)
                for b in range(4):
                    pool.wait_ge(L["qk_ms"], B["qk_ms"] + 3 * b + 3)
                    link(pool, "pool", pool.tensor_scalar(ms[b % 2], ms[b % 2], 1.0 / HD, EPS, ALU.mult, ALU.add))
                    pool.tensor_tensor(rr[b % 2], ms[b % 2], neghalf[:, :], ALU.pow).then_inc(L["qk_r"], 1)
                    if b >= 2:
                        for t in range(TILES):
                            pool.wait_ge(L["qk_normed"], B["qk_normed"] + 3 * b + t + 1)
                            out = token_rows(K_OUT[l][0], K_OUT[l][1], t)[:, (b - 2) * F:(b - 1) * F]
                            pool.dma_start(out, qk[0:ROWS[t], b % 2, t, :]).then_inc(L["k_stored"], 16)
                if l == 0:
                    for dst, src in small:
                        pool.dma_start(dst, src).then_inc(small_loaded, 16)
                if l == 1:
                    pool.wait_ge(fox["logf_ready"], 1)
                    for t in range(TILES):
                        prompt, sample = (A[n].rearrange("a b s h -> (a b s) h") for n in ("new_fox_logf_prompt", "new_fox_logf_sample"))
                        pool.dma_start(token_rows(prompt, sample, t), logf[0:ROWS[t], t, :]).then_inc(fox["logf_stored"], 16)
                for t in range(TILES):
                    pool.wait_ge(L["v_copied"], B["v_copied"] + 3 + t + 1)
                    pool.dma_start(token_rows(V_OUT[l][0], V_OUT[l][1], t), v_new[0:ROWS[t], t, :]).then_inc(L["v_stored"], 16)
                if l == 1:
                    pool.wait_ge(units_used, Unit(BASE_OUT[l], 0).n)
                    pool.dma_start(bias[:, 1, :], A["c_mask"]).then_inc(L["alibi"], 16)

                def head_rms(c0, c1):
                    m, r = ms[0][:, c0:c1], rr[0][:, c0:c1]
                    k = (1.0 - LAMBDA_INIT) ** 2
                    pool.wait_ge(L["o_sqd"], B["o_sqd"] + c1)
                    link(pool, "pool", pool.tensor_scalar(m, m, 1.0 / (P * k), EPS / k, ALU.mult, ALU.add))
                    pool.tensor_tensor(r, m, neghalf[:, 0:c1 - c0], ALU.pow).then_inc(L["o_r"], c1 - c0)

                load_keys(2)
                load_keys(3)
                for p in range(2, PAIRS):
                    if p + 2 < PAIRS:
                        load_keys(p + 2)
                    load_values(p)
                    if l == 0:
                        head_rms(3 * (p - 2), 3 * (p - 1))
                if l == 0:
                    head_rms(3 * (PAIRS - 2), 3 * (PAIRS - 1))
                    for i in range(3 * (PAIRS - 1), 3 * PAIRS):
                        head_rms(i, i + 1)
                else:
                    pool.wait_ge(L["scores_done"], B["scores_done"] + 3 * PAIRS)
                    pool.dma_start(gain[:, 1, :], A["norm_ffn"][1, :].partition_broadcast(P)).then_inc(gain_loaded[1][1], 16)
                rms(B, "sq1", "rstd1")
                pool.wait_ge(L["k_stored"], B["k_stored"] + 16 * 2 * TILES)
                pool.wait_ge(L["v_stored"], B["v_stored"] + 16 * TILES)
                if l == 1:
                    pool.wait_ge(fox["logf_stored"], 16 * TILES)
                pool.wait_ge(OV[l]["flag_ready"], 1)
                flag_v = pool.value_load(flag[0:1, 0:1])
                with pool.If(flag_v > 0):
                    pool.wait_ge(OV[l]["over_x"], EXPERTS * TILES)

        @block.scalar
        def _(act):
            A_ = nc.scalar.activation

            def split_hi(U):
                act.wait_ge(raw_ready[U.slot], U.arrivals)
                if U.static >= HI:
                    act.wait_ge(units_used, U.n - HI + 1)
                A_(w_hi[:, U.hslot, :], w_raw[:, U.slot, :], ACT.Copy).then_inc(hi_ready, 1)

            def split_slab(base, k, g=0):
                for half in range(2):
                    split_hi(Unit(base, 2 * k + half, g))

            for l in range(2):
                B = BEFORE[l]
                for t in range(TILES):
                    if l == 0:
                        act.wait_ge(x_loaded[t], 16)
                        if t == 2:
                            act.wait_ge(x_padded, 1)
                    else:
                        act.wait_ge(L["x_added"], 6 * GROUPS - 6 + 2 * t + 2)
                    A_(h[:, t, :], x[:, t, :], ACT.Square, accum_out=ss[:, t:t + 1]).then_inc(L["sq0"], 1)
                for i in range(2 * TILES):
                    if l == 0 and i in (2, 4):
                        split_hi(Unit(0, i // 2 - 1))
                    t, half = divmod(i, 2)
                    act.wait_ge(L["tr0"], B["tr0"] + i + 1)
                    dst, src = hi_part(hT_hi, i)
                    A_(dst, src, ACT.Copy).then_inc(L["hi0"], 1)
                split_slab(BASE_IN[l], 1)
                if l == 1:
                    act.wait_ge(fox["wf_loaded"], 16)
                    A_(w_f_hi[:, :, :], w_f[:, :, :], ACT.Copy).then_inc(fox["wf_hi"], 1)

                def evacuate_qk(b):
                    for t in range(TILES):
                        i = 3 * b + t
                        act.wait_ge(L["qk_tr"], B["qk_tr"] + i + 1)
                        bank = ps[:, 6 + i % 2, :].rearrange("p (k n) -> p k n", k=4)
                        pr = slice(4 * (b % 2), 4 * (b % 2) + 4)
                        if b < 2 and t < 2:
                            A_(qT[:, pr, t * P:(t + 1) * P], bank, ACT.Copy).then_inc(L["qk_evac"], 1)
                        elif b < 2:
                            act.wait_ge(L["q_zeroed"], B["q_zeroed"] + 1)
                            A_(q_diag[0:HD, pr, 0:DEC], bank[0:HD, :, 0:DEC], ACT.Copy)
                            A_(q_diag[HD:P, pr, DEC:P], bank[HD:P, :, 0:DEC], ACT.Copy).then_inc(L["qk_evac"], 1)
                        else:
                            n = ROWS[t]
                            A_(kT_new[:, pr, t * P:t * P + n], bank[:, :, 0:n], ACT.Copy).then_inc(L["qk_evac"], 1)

                def alibi(p):
                    if p >= 2:
                        act.wait_ge(L["max_done"], B["max_done"] + 3 * (p - 2) + 3)
                    A_(bias[:, p % 2, :], dist[:, :], ACT.Copy, scale=2.0 ** -(p + 1)).then_inc(L["bias_ready"], 1)

                for b in range(IN_BLOCKS[l]):
                    kind = in_kind(b)
                    split_hi(Unit(BASE_IN[l], 2 * b + 4))
                    for t in range(TILES):
                        wait_sum(act, B, "proj_done", BASE_IN[l], b, t)
                        n, src = ROWS[t], acc(b, t)
                        if t == 2:
                            if b == 0:
                                act.wait_ge(L["tr0"], B["tr0"] + 2 * TILES)
                            elif 2 <= b <= 5:
                                act.wait_ge(L["qk_n1"], B["qk_n1"] + 3 * (b - 2) + 3)
                            elif b >= 6:
                                act.wait_ge(L["v_copied"], B["v_copied"] + 3 * (b - 6) + 3)
                            if l == 0 and b == IN_BLOCKS[l] - 1:
                                act.wait_ge(L["alibi"], B["alibi"] + 16)
                                alibi(0)
                            A_(low_rows[:, b % 2, :], acc(b, t)[DEC:P, :], ACT.Copy).then_inc(L["low_moved"], 1)
                            if l == 1 and b == 1:
                                act.wait_ge(fox["off_done"], 1)
                                A_(off_hi[:, 0:320], ps[0:FOX_HEADS, 7, 0:320], ACT.Copy, scale=-1.0 / SCALE).then_inc(fox["off_hi"], 1)
                                A_(off_hi[:, 320:832], ps[0:FOX_HEADS, 6, 0:512], ACT.Copy, scale=1.0 / SCALE).then_inc(fox["off_hi"], 1)
                            if 1 <= b <= 4:
                                evacuate_qk(b - 1)
                            act.wait_ge(L["low_added"], B["low_added"] + b + 1)
                            src = low_rows[:, b % 2, :]
                        if kind in "qk":
                            if b >= 2:
                                act.wait_ge(L["qk_tr"], B["qk_tr"] + 3 * (b - 2) + t + 1)
                            A_(qk[0:n, b % 2, t, :], src[0:n, :], ACT.Square).then_inc(L["qk_sq"], 1)
                        elif kind == "v":
                            A_(v_new[0:n, t, (b - 4) * F:(b - 3) * F], src[0:n, :], ACT.Copy).then_inc(L["v_copied"], 1)
                        else:
                            if b == 6 and t == 0:
                                act.wait_ge(L["qk_tr"], B["qk_tr"] + 12)
                                act.wait_ge(L["k_stored"], B["k_stored"] + 16 * 2 * TILES)
                            A_(gate[0:n, t, (b - 6) * F:(b - 5) * F], src[0:n, :], ACT.Sigmoid).then_inc(L["g_done"], 1)
                    if b < IN_BLOCKS[l] - 1:
                        split_hi(Unit(BASE_IN[l], 2 * b + 5))
                    if l == 1 and b == 0:
                        act.wait_ge(fox["f_z"], 1)
                        A_(lf[:, 2, :], lf[:, 1, :], ACT.Exp, scale=-1.0).then_inc(fox["f_exp"], 1)
                    if l == 0 and b == 4:
                        act.wait_ge(lam_dots, 2)
                        A_(lamw[:, 2:4], lamw[:, 0:2], ACT.Exp).then_inc(lam_exps, 1)

                def square_head(j, p, t):
                    act.wait_ge(L["o_done"], B["o_done"] + j + 1)
                    if j >= 2:
                        act.wait_ge(L["o_sqd"], B["o_sqd"] + j - 1)
                    A_(o_sq[:, j % 2, :], o[:, t, p * P:(p + 1) * P], ACT.Square, accum_out=ms[0][:, j:j + 1]).then_inc(L["o_sqd"], 1)

                def past_keys(p):
                    act.wait_ge(L["past_tr"], B["past_tr"] + p + 1)
                    A_(kT_past[:, p % 2, :], ps[:, 5, :], ACT.Copy).then_inc(L["past_ev"], 1)

                def exps(j, t):
                    act.wait_ge(L["neg_done"], B["neg_done"] + j + 1)
                    n = KEYS[t]
                    for c in range(2 if t < 2 else 1):
                        s = probs[:, j % 3, c * n:(c + 1) * n]
                        ins = A_(s, s, ACT.Exp, bias=nmx[:, j % 3, c:c + 1], scale=SCALE, accum_out=sm[:, j % 3, c:c + 1])
                    ins.then_inc(L["exp_done"], 1)

                def copy_dT(j, p, t):
                    act.wait_ge(L["dT_done"], B["dT_done"] + j + 1)
                    if j >= 2:
                        act.wait_ge(L["pv_done"], B["pv_done"] + j - 1)
                    bank, q = ps[:, DT_BANK[j % 2], :], (DEC if l == 0 else P)
                    if t < 2:
                        n = KEYS[t] * (1 if l == 0 else 2)
                        A_(dT[:, j % 2, 0:n], bank[:, 0:n], ACT.Copy).then_inc(L["dT_copied"], 1)
                    else:
                        A_(dT[:, j % 2, 0:4 * q], bank[:, 0:4 * q], ACT.Copy)
                        A_(dT[0:DEC, j % 2, 4 * q:5 * q], new_keys_T(j, l), ACT.Copy).then_inc(L["dT_copied"], 1)

                its = list(items())
                past_keys(0)
                exps(0, 0)
                if l == 0:
                    alibi(1)
                for j, p, t in its:
                    if j + 1 < len(its):
                        exps(j + 1, its[j + 1][2])
                    if t == 1 and p + 1 < PAIRS:
                        past_keys(p + 1)
                    if j >= 1:
                        copy_dT(*its[j - 1])
                    if l == 0:
                        if t == 0 and 1 <= p < PAIRS - 1:
                            alibi(p + 1)
                        if j >= 3:
                            square_head(*its[j - 3])
                copy_dT(*its[-1])
                if l == 0:
                    for item in its[-3:]:
                        square_head(*item)
                for i in range(2 * TILES):
                    t, half = divmod(i, 2)
                    act.wait_ge(L["o_tr"], B["o_tr"] + i + 1)
                    dst, src = hi_part(oT_hi, i)
                    A_(dst, src, ACT.Copy).then_inc(L["o_hi"], 1)
                def move_out(b):
                    wait_sum(act, B, "out_done", BASE_OUT[l], b, 2)
                    A_(low_out[:, b, :], acc(b, 2)[DEC:P, :], ACT.Copy).then_inc(L["low_out_moved"], 1)

                split_hi(Unit(BASE_OUT[l], 3))
                split_hi(Unit(BASE_OUT[l], 4))
                move_out(0)
                split_hi(Unit(BASE_OUT[l], 5))
                split_hi(Unit(BASE_OUT[l], 6))

                for t in range(TILES):
                    if t == 2:
                        move_out(1)
                    act.wait_ge(L["x_mid"], B["x_mid"] + TILES + t + 1)
                    if t == 0:
                        act.wait_ge(L["k_stored"], B["k_stored"] + 16 * 2 * TILES)
                        act.wait_ge(L["v_stored"], B["v_stored"] + 16 * TILES)
                        if l == 1:
                            act.wait_ge(fox["logf_stored"], 16 * TILES)
                    A_(h2[:, t, :], x[:, t, :], ACT.Square, accum_out=ss[:, t:t + 1]).then_inc(L["sq1"], 1)
                for t in range(TILES):
                    for half in range(2):
                        i = 2 * t + half
                        act.wait_ge(L["tr1"], B["tr1"] + i + 1)
                        A_(h2T[:, 4 * half:4 * half + 4, t * P:(t + 1) * P], ps[:, i, :].rearrange("p (k n) -> p k n", k=4), ACT.Copy).then_inc(L["ev1"], 1)
                for t in range(TILES):
                    A_(h2_hi[:, t, :], h2[:, t, :], ACT.Copy).then_inc(L["h2hi"], 1)
                split_hi(Unit(BASE_OUT[l], 7))
                act.wait_ge(L["logit_sb"], B["logit_sb"] + 1)
                A_(ge, gd, ACT.Exp).then_inc(L["gexp"], 1)

                def silu(order, e, g):
                    wait_matrix(act, l, order, ("g", e), g)
                    if order is not FIRST:
                        act.wait_ge(L["hid_done"], B["hid_done"] + g * 4 + e)
                    A_(act_g[:, :], ps[:, 0, :], ACT.Silu).then_inc(L["silu_done"], 1)

                def hidden_hi(e, g, dst=hidT_hi):
                    act.wait_ge(L["hT_done"], B["hT_done"] + g * 4 + e + 1)
                    A_(dst[:, :, :].rearrange("p k n -> p (k n)"), ps[:, 2, :], ACT.Copy).then_inc(L["hT_hi"], 1)

                def copy_gathered(g):
                    for i in range(2):
                        act.wait_ge(L["gathered"], B["gathered"] + g * 2 + i + 1)
                        A_(x_slots[:, i * F:(i + 1) * F], ps[:, 5 + i, :], ACT.Copy).then_inc(L["slots_copied"], 1)

                def gathered_hi(g):
                    for i in range(2):
                        act.wait_ge(L["slots_tr"], B["slots_tr"] + g * 2 + i + 1)
                        A_(xT_hi[:, 4 * i:4 * i + 4, :].rearrange("p k n -> p (k n)"), ps[:, 5 + i, :], ACT.Copy).then_inc(L["x_hi"], 1)

                def moe_round(order, g):
                    last = order is LAST
                    for m, (kind, e) in enumerate(order):
                        ahead = not (last and m >= len(order) - 2 and l == 1)
                        late = last and m >= len(order) - 2
                        if ahead and not late:
                            split_hi(Unit(BASE_MOE[l], 2 * (m + 4), g))
                        if kind == "g":
                            silu(order, e, g)
                        if (kind, e) in (("g", 1), ("g", 2), ("g", 3)):
                            hidden_hi(e - 1, g)
                        if (kind, e) == ("g", 3) and not last:
                            copy_gathered(g + 1)
                        if (kind, e) == ("u", 3) and not last:
                            gathered_hi(g + 1)
                        if (kind, e) == ("d", 2):
                            hidden_hi(3, g, hidT_last_hi if last else hidT_hi)
                        if (kind, e) == ("d", 3):
                            wait_matrix(act, l, order, ("d", 3), g)
                            for i in range(2):
                                A_(y_hi[:, i * F:(i + 1) * F], ps[:, 3 + i, :], ACT.Copy).then_inc(L["y_hi"], 1)
                        if last and m == len(order) - 2:
                            split_hi(Unit(BASE_MOE[l], 2 * (m + 3) + 1, g))
                        if ahead and not (last and m == len(order) - 1):
                            if late:
                                split_hi(Unit(BASE_MOE[l], 2 * (m + 4), g))
                            if not (last and m == len(order) - 3):
                                split_hi(Unit(BASE_MOE[l], 2 * (m + 4) + 1, g))

                copy_gathered(0)
                gathered_hi(0)
                act.wait_ge(L["logit_sb"], B["logit_sb"] + 2)
                A_(e2, dv, ACT.Exp).then_inc(L["gexp"], 1)
                silu(FIRST, 0, 0)
                split_slab(BASE_MOE[l], 2)
                split_slab(BASE_MOE[l], 3)
                with act.Fori(0, GROUPS - 1) as g:
                    moe_round(ORDER, g)
                moe_round(LAST, GROUPS - 1)

                act.wait_ge(OV[l]["flag_ready"], 1)
                flag_v = act.value_load(flag[0:1, 0:1])
                with act.If(flag_v > 0):
                    with act.Fori(0, EXPERTS) as e:
                        for t in range(TILES):
                            act.wait_ge(OV[l]["over_used"], e * 18 + 6 * t + 3)
                            A_(act_g[:, :], ps[:, 0, :], ACT.Silu).then_inc(OV[l]["over_act"], 1)
                            act.wait_ge(OV[l]["over_tr"], e * TILES + t + 1)
                            A_(over_hT[:, :], ps[:, 2, :], ACT.Copy).then_inc(OV[l]["over_ht"], 1)
                            act.wait_ge(OV[l]["over_x"], e * TILES + t + 1)

        @block.tensor
        def _(pe):
            mm, tr = nc.tensor.matmul, nc.tensor.transpose

            def split_mm(out, a_hi, a_lo, b_hi, b_lo, start, stop):
                mm(out, a_hi, b_hi, start=start, stop=False)
                mm(out, a_hi, b_lo, start=False, stop=False)
                return mm(out, a_lo, b_hi, start=False, stop=stop)

            def stay_busy(bank, n):
                for _ in range(n):
                    mm(ps[:, bank, 0:256], ident, cst[:, 0:256], start=True, stop=True)

            def unit_parts(U, n):
                hi = w_hi[:, U.hslot, :].rearrange("p (k n) -> p k n", n=n)
                lo = w_lo[:, U.slot, :].rearrange("p (k n) -> p k n", n=n)
                return hi, lo

            def transposes(B, src, ready, done, counts=(1, 2, 3), tiles=range(TILES)):
                for i in range(2 * tiles[0], 2 * tiles[-1] + 2):
                    t, half = divmod(i, 2)
                    pe.wait_ge(L[ready], B[ready] + counts[t])
                    for k in range(4):
                        c = (4 * half + k) * P
                        ins = tr(ps[:, i, k * P:(k + 1) * P], src[:, t, c:c + P], ident)
                    ins.then_inc(L[done], 1)

            def project(B, base, b, a_hi, a_lo, low, done, free, last_transposes):
                for half in range(2):
                    U = Unit(base, 2 * b + half)
                    pe.wait_ge(lo_ready, U.n + 1)
                    hi, lo = unit_parts(U, F)
                    for t in range(TILES):
                        if b == 0 and half == 0 and t == 2:
                            last_transposes()
                        if b == 0:
                            pe.wait_ge(L[low], B[low] + 2 * t + half + 1)
                        if half == 0 and free is not None:
                            free(b, t)
                        for k in range(4):
                            kb = 4 * half + k
                            ts = slice(t * P, (t + 1) * P)
                            if t < 2:
                                ins = split_mm(acc(b, t), a_hi[:, kb, ts], a_lo[:, kb, ts], hi[:, k, :], lo[:, k, :],
                                               start=(kb == 0), stop=(kb == KB - 1))
                            else:
                                mm(acc(b, t), a_hi[:, kb, ts], hi[:, k, :], start=(kb == 0), stop=False)
                                ins = mm(acc(b, t), a_hi[:, kb, ts], lo[:, k, :], start=False, stop=(kb == KB - 1))
                        if half == 1 and t < TILES - 1:
                            ins.then_inc(L[done], 1)
                    ins.then_inc(units_used, 1)

            pe.wait_ge(ident_loaded, 16)
            for l in range(2):
                B = BEFORE[l]
                transposes(B, h, "h_ready0", "tr0", tiles=(0, 1))

                def last_in():
                    transposes(B, h, "h_ready0", "tr0", tiles=(2,))

                def forget_logits():
                    pe.wait_ge(fox["wf_lo"], 1)
                    for t in range(TILES):
                        for kb in range(KB):
                            ts = slice(t * P, (t + 1) * P)
                            out = ps[:, 7, t * 16:(t + 1) * 16]
                            mm(out, hT_hi[:, kb, ts], w_f_hi[:, kb, :], start=(kb == 0), stop=False)
                            if t < 2:
                                mm(out, hT_lo[:, kb, ts], w_f_hi[:, kb, :], start=False, stop=False)
                            else:
                                mm(out[0:DEC, :], hT_hi[:, kb, 2 * P + DEC:3 * P], w_f_hi[:, kb, :], start=False, stop=False)
                            ins = mm(out, hT_hi[:, kb, ts], w_f_lo[:, kb, :], start=False, stop=(kb == KB - 1))
                    ins.then_inc(fox["f_done"], 1)

                def key_offsets():
                    pe.wait_ge(fox["logf_ready"], 1)
                    pe.wait_ge(fox["lp_loaded"], 16)
                    off = ps[0:FOX_HEADS, 7, :]
                    mm(off[:, 0:128], logf[:, 0, :], tri, start=True, stop=True)
                    mm(off[:, 128:256], logf[:, 0, :], ones, start=True, stop=False)
                    mm(off[:, 128:256], logf[:, 1, :], tri, start=False, stop=True)
                    mm(off[:, 256:320], logf[0:DEC, 2, :], tri[0:DEC, 0:DEC], start=True, stop=True)
                    for i in range(PTILES):
                        out = ps[0:FOX_HEADS, 6, i * P:(i + 1) * P]
                        ins = mm(out, logf_past[:, i, :], after, start=True, stop=(i == PTILES - 1))
                        for k in range(i + 1, PTILES):
                            ins = mm(out, logf_past[:, k, :], ones, start=False, stop=(k == PTILES - 1))
                    ins.then_inc(fox["off_done"], 1)

                def free_in(b, t):
                    if b >= 2 and t == 2:
                        pe.wait_ge(L["low_added"], B["low_added"] + b - 1)
                    elif b >= 2:
                        if in_kind(b - 2) in "qk":
                            pe.wait_ge(L["qk_n1"], B["qk_n1"] + 3 * (b - 2) + t + 1)
                        else:
                            pe.wait_ge(L["v_copied"], B["v_copied"] + 3 * (b - 6) + t + 1)

                def transpose_qk(b):
                    for t in range(TILES):
                        i = 3 * b + t
                        pe.wait_ge(L["qk_normed"], B["qk_normed"] + i + 1)
                        if i >= 2:
                            pe.wait_ge(L["qk_evac"], B["qk_evac"] + i - 1)
                        elif l == 1:
                            pe.wait_ge(fox["off_lo"], 2)
                        n = ROWS[t]
                        for k in range(4):
                            ins = tr(ps[:, 6 + i % 2, k * P:k * P + n], qk[0:n, b % 2, t, k * P:(k + 1) * P], ident[0:n, 0:n])
                        ins.then_inc(L["qk_tr"], 1)

                for b in range(IN_BLOCKS[l]):
                    project(B, BASE_IN[l], b, hT_hi, hT_lo, "lo0", "proj_done", free_in, last_in)
                    if l == 1 and b == 0:
                        forget_logits()
                    if l == 1 and b == 1:
                        key_offsets()
                    if 1 <= b <= 4:
                        transpose_qk(b - 1)

                its = list(items())

                def past_keys(p):
                    pe.wait_ge(L[f"k_loaded{p % 2}"], B["k_loaded0"] + 16 * (p // 2 + 1))
                    if p == 0:
                        pe.wait_ge(L["low_added"], B["low_added"] + IN_BLOCKS[l])
                    else:
                        pe.wait_ge(L["past_ev"], B["past_ev"] + p)
                        if l == 1 and p >= 2:
                            pe.wait_ge(L["dT_copied"], B["dT_copied"] + 3 * (p - 2) + 3)
                    for i in range(PTILES):
                        ins = tr(ps[:, 5, i * P:(i + 1) * P], k_past[:, p % 2, i, :], ident)
                    ins.then_inc(L["past_tr"], 1)

                def offsets(out, head, n, width, a, stop=True):
                    if width == P:
                        sel = ident_r[0:FOX_HEADS, head:head + 1].to_broadcast([FOX_HEADS, P])
                    else:
                        sel = pick_heads[:, head // 2, :]
                    mm(out, sel, off_hi[:, a:a + n], start=False, stop=False)
                    return mm(out, sel, off_lo[:, a:a + n], start=False, stop=True)

                def scores(j, p, t):
                    s = 2 * (j % 2)
                    if j >= 2:
                        pe.wait_ge(L["max_done"], B["max_done"] + j - 1)
                    fx = l == 1
                    if t < 2:
                        n = KEYS[t]
                        for c in range(2):
                            out = ps[:, s + c, 0:n]
                            cs = slice(c * HD, (c + 1) * HD)
                            ins = mm(out, qT[cs, p, t * P:(t + 1) * P], kT_new[cs, p, 0:n], start=True, stop=not fx)
                            if fx:
                                ins = offsets(out, 2 * p + c, n, P, 0)
                    else:
                        pe.wait_ge(L["past_ev"], B["past_ev"] + p + 1)
                        ins = mm(ps[:, s, :], q_diag[:, p, :], kT_past[:, p % 2, :], start=True, stop=not fx)
                        if fx:
                            offsets(ps[:, s, :], 2 * p, PAST, DEC, 320)
                        ins = mm(ps[:, s + 1, 0:DEC], q_diag[:, p, :], kT_new[:, p, SEQ:SEQ + DEC], start=True, stop=not fx)
                        if fx:
                            ins = offsets(ps[:, s + 1, 0:DEC], 2 * p, DEC, DEC, 256)
                    ins.then_inc(L["scores_done"], 1)

                def probs_T(j, p, t):
                    if l == 0:
                        pe.wait_ge(L["mixed"], B["mixed"] + j + 1)
                    else:
                        pe.wait_ge(L["exp_done"], B["exp_done"] + j + 1)
                    if j >= 2:
                        pe.wait_ge(L["dT_copied"], B["dT_copied"] + j - 1)
                    pr, bank = probs[:, j % 3, :], ps[:, DT_BANK[j % 2], :]
                    if t < 2:
                        for i in range(KEYS[t] // P * (1 if l == 0 else 2)):
                            ins = tr(bank[:, i * P:(i + 1) * P], pr[:, i * P:(i + 1) * P], ident)
                    elif l == 0:
                        for kb in range(PTILES):
                            mm(bank[:, kb * DEC:(kb + 1) * DEC], pr[:, kb * P:(kb + 1) * P], diag[:, :], start=True, stop=True)
                        ins = mm(new_keys_T(j, l), pr[:, PAST:PAST + DEC], diag[:, :], start=True, stop=True)
                    else:
                        pe.wait_ge(L["past_ev"], B["past_ev"] + min(p + 2, PAIRS))
                        for kb in range(PTILES):
                            tr(bank[:, kb * P:(kb + 1) * P], pr[:, kb * P:(kb + 1) * P], ident)
                        ins = tr(new_keys_T(j, l), pr[:, PAST:PAST + DEC], ident)
                    ins.then_inc(L["dT_done"], 1)

                def values(j, p, t):
                    pe.wait_ge(L["dT_copied"], B["dT_copied"] + j + 1)
                    if j >= 1:
                        pe.wait_ge(L["o_done"], B["o_done"] + j)
                    if j == 2:
                        pe.wait_ge(L["v_copied"], B["v_copied"] + 6)
                    if t == 2:
                        pe.wait_ge(L[f"v_loaded{p % 2}"], B["v_loaded0"] + 16 * (p // 2 + 1))
                    d = dT[:, j % 2, :]
                    col = p * P
                    members = [(0, P)] if l == 0 else [(0, HD), (HD, HD)]
                    for m, (c0, w) in enumerate(members):
                        out = ps[0:ROWS[t], 6, c0:c0 + w]
                        if t < 2:
                            nb = KEYS[t] // P
                            for kb in range(nb):
                                a = (m * nb + kb) * P
                                ins = mm(out, d[:, a:a + P], v_new[:, kb, col + c0:col + c0 + w], start=(kb == 0), stop=(kb == nb - 1))
                        else:
                            q = DEC if l == 0 else P
                            for kb in range(PTILES):
                                mm(out, d[:, kb * q + m * DEC:kb * q + m * DEC + DEC], v_past[:, p % 2, kb, c0:c0 + w], start=(kb == 0), stop=False)
                            ins = mm(out, d[0:DEC, PTILES * q + m * DEC:PTILES * q + m * DEC + DEC],
                                     v_new[0:DEC, 2, col + c0:col + c0 + w], start=False, stop=True)
                    ins.then_inc(L["pv_done"], 1)

                pe.wait_ge(L["qk_evac"], B["qk_evac"] + 12)
                if l == 0:
                    pe.wait_ge(const_loaded, 16)
                stay_busy(7, 2)
                last_block = ("v_copied", B["v_copied"] + 3) if l == 0 else ("g_done", B["g_done"] + 3)
                if l == 1:
                    pe.wait_ge(fox["heads_ready"], 1)
                pe.wait_ge(L[last_block[0]], last_block[1])
                scores(*its[0])
                pe.wait_ge(L[last_block[0]], last_block[1] + 1)
                scores(*its[1])
                past_keys(0)
                pe.wait_ge(L[last_block[0]], last_block[1] + 2)
                stay_busy(7, 3)
                for j, p, t in its:
                    if t == 1 and p + 1 < PAIRS:
                        past_keys(p + 1)
                    if j + 2 < len(its):
                        scores(*its[j + 2])
                    probs_T(j, p, t)
                    if j >= 1:
                        values(*its[j - 1])
                values(*its[-1])

                last_items = (3 * PAIRS - 2, 3 * PAIRS - 1, 3 * PAIRS)
                o_ready = "o_normed" if l == 0 else "o_done"
                transposes(B, o, o_ready, "o_tr", counts=last_items, tiles=(0, 1))

                def last_out():
                    transposes(B, o, o_ready, "o_tr", counts=last_items, tiles=(2,))

                for b in range(OUT_BLOCKS):
                    project(B, BASE_OUT[l], b, oT_hi, oT_lo, "o_lo", "out_done", None, last_out)

                transposes(B, h2, "h_ready1", "tr1", tiles=(0, 1))
                if l == 0:
                    pe.wait_ge(small_loaded, 16 * SMALL)
                for t in range(TILES):
                    if t == 1:
                        transposes(B, h2, "h_ready1", "tr1", tiles=(2,))
                    pe.wait_ge(L["ev1"], B["ev1"] + 2 * t + 2)
                    for kb in range(KB):
                        ins = mm(ps[:, 6, t * 20:(t + 1) * 20], h2T[:, kb, t * P:(t + 1) * P], w_router[:, l, kb, :],
                                 start=(kb == 0), stop=(kb == KB - 1))
                ins.then_inc(L["logits"], 1)
                pe.wait_ge(L["onehot"], B["onehot"] + 1)
                for t in range(TILES):
                    for s in range(t):
                        mm(ps[:, 7, 4 * t:4 * t + 4], ones, oh[:, s, :], start=(s == 0), stop=False)
                    ins = mm(ps[:, 7, 4 * t:4 * t + 4], before, oh[:, t, :], start=(t == 0), stop=True)
                    if t == TILES - 1:
                        ins.then_inc(L["ranks"], 1)
                pe.wait_ge(L["h2lo"], B["h2lo"] + TILES)

                def gather(g):
                    pe.wait_ge(L["pick_ready"], B["pick_ready"] + g + 1)
                    for i in range(2):
                        for t in range(TILES):
                            for part, src in enumerate((h2_hi, h2_lo)):
                                ins = mm(ps[:, 5 + i, :], pick[:, t, :], src[:, t, i * F:(i + 1) * F],
                                         start=(t == 0 and part == 0), stop=(t == TILES - 1 and part == 1))
                        ins.then_inc(L["gathered"], 1)

                def transpose_slots(g):
                    for i in range(2):
                        pe.wait_ge(L["slots_copied"], B["slots_copied"] + g * 2 + i + 1)
                        for k in range(4):
                            c = (4 * i + k) * P
                            ins = tr(ps[:, 5 + i, k * P:(k + 1) * P], x_slots[:, c:c + P], ident)
                        ins.then_inc(L["slots_tr"], 1)

                def slots(g):
                    for t in range(TILES):
                        mm(ps[:, 7, 384:392], pick[:, t, :], gates_hl[:, t, :], start=(t == 0), stop=(t == TILES - 1))
                    for t in range(TILES):
                        ins = tr(ps[:, 7, t * P:(t + 1) * P], pick[:, t, :].bitcast(F32), ident)
                    ins.then_inc(L["slot_done"], 1)

                def into(m, bank, g):
                    for half in range(2):
                        U = Unit(BASE_MOE[l], 2 * m + half, g)
                        pe.wait_ge(lo_ready, U.n + 1)
                        hi, lo = unit_parts(U, F)
                        for k in range(4):
                            kb = 4 * half + k
                            ins = split_mm(ps[:, bank, :], xT_hi[:, kb, :], xT_lo[:, kb, :], hi[:, k, :], lo[:, k, :],
                                           start=(kb == 0), stop=(kb == KB - 1))
                        ins.then_inc(units_used, 1)

                def down(m, e, g, between=None, a_hi=hidT_hi, a_lo=hidT_lo):
                    pe.wait_ge(L["hT_lo"], B["hT_lo"] + g * 4 + e + 1)
                    for half in range(2):
                        U = Unit(BASE_MOE[l], 2 * m + half, g)
                        pe.wait_ge(lo_ready, U.n + 1)
                        hi, lo = unit_parts(U, D)
                        for k in range(2):
                            fb = 2 * half + k
                            for c in range(2):
                                cs = slice(c * F, (c + 1) * F)
                                ins = split_mm(ps[:, 3 + c, :], a_hi[:, fb, :], a_lo[:, fb, :], hi[:, k, cs], lo[:, k, cs],
                                               start=(e == 0 and fb == 0), stop=(e == 3 and fb == 3))
                        ins.then_inc(units_used, 1)
                        if half == 0 and between is not None:
                            between()

                def hidden_T(e, g):
                    pe.wait_ge(L["hid_done"], B["hid_done"] + g * 4 + e + 1)
                    if e == 0:
                        pe.wait_ge(L["pickT_taken"], B["pickT_taken"] + g + 1)
                    for k in range(4):
                        ins = tr(ps[:, 2, k * P:(k + 1) * P], hid[:, k * P:(k + 1) * P], ident)
                    ins.then_inc(L["hT_done"], 1)

                def back(g):
                    for i in range(2 * TILES):
                        t, c = divmod(i, 2)
                        if i < 2:
                            pe.wait_ge(L["y_lo"], B["y_lo"] + g * 2 + i + 1)
                        if i == 5:
                            pe.wait_ge(L["x_added"], B["x_added"] + g * 6 + 1)
                        cs = slice(c * F, (c + 1) * F)
                        mm(ps[:, BACK[i], :], pickT[:, t, :], y_hi[:, cs], start=True, stop=False)
                        mm(ps[:, BACK[i], :], pickT[:, t, :], y_lo[:, cs], start=False, stop=True).then_inc(L["back_done"], 1)

                def moe_round(order, g):
                    last = order is LAST
                    for m, (kind, e) in enumerate(order):
                        if kind == "g":
                            pe.wait_ge(L["silu_done"], B["silu_done"] + g * 4 + e)
                            if e == PER_GROUP:
                                pe.wait_ge(L["x_lo"], B["x_lo"] + g * 2 + 4)
                            into(2 + m, 0, g)
                        elif kind == "u":
                            into(2 + m, 1, g)
                        else:
                            early = last and e == 2
                            parts = (hidT_last_hi, hidT_last_lo) if last and e == 3 else (hidT_hi, hidT_lo)
                            down(2 + m, e, g, (lambda: hidden_T(3, g)) if early else None, *parts)
                        if (kind, e) in (("g", 1), ("g", 2), ("g", 3)):
                            hidden_T(e - 1, g)
                        if (kind, e) == ("g", 3) and not last:
                            gather(g + 1)
                        if (kind, e) == ("u", 3) and not last:
                            transpose_slots(g + 1)
                            slots(g + 1)
                        if (kind, e) == ("d", 2) and not last:
                            hidden_T(3, g)
                    back(g)

                gather(0)
                for s in range(TILES):
                    ins = mm(ps[:, 7, 12:16], ones, oh[:, s, :], start=(s == 0), stop=(s == TILES - 1))
                ins.then_inc(L["ranks"], 1)
                transpose_slots(0)
                pe.wait_ge(L["x_lo"], B["x_lo"] + 2)
                into(0, 0, 0)
                pe.wait_ge(L["routed"], B["routed"] + 1)
                slots(0)
                into(1, 1, 0)
                with pe.Fori(0, GROUPS - 1) as g:
                    moe_round(ORDER, g)
                moe_round(LAST, GROUPS - 1)

                pe.wait_ge(OV[l]["flag_ready"], 1)
                flag_v = pe.value_load(flag[0:1, 0:1])
                with pe.If(flag_v > 0):
                    pe.sem_inc(OV[l]["over_used"], 1)
                    with pe.Fori(0, EXPERTS) as e:
                        for t in range(TILES):
                            ts = slice(t * P, (t + 1) * P)
                            wf = over_w[:, :].rearrange("p (k n) -> p k n", n=F)
                            wd = over_w[:, :].rearrange("p (k n) -> p k n", n=D)
                            for j in range(4):
                                pe.wait_ge(OV[l]["over_load"], e * 288 + 16 * (6 * t + j + 1))
                                bank, half = divmod(j, 2)
                                for k in range(4):
                                    kb = 4 * half + k
                                    ins = mm(ps[:, bank, :], h2T[:, kb, ts], wf[:, k, :], start=(kb == 0), stop=(kb == KB - 1))
                                ins.then_inc(OV[l]["over_used"], 1)
                            pe.wait_ge(OV[l]["over_hid"], e * TILES + t + 1)
                            for k in range(4):
                                ins = tr(ps[:, 2, k * P:(k + 1) * P], hid[:, k * P:(k + 1) * P], ident)
                            ins.then_inc(OV[l]["over_tr"], 1)
                            pe.wait_ge(OV[l]["over_ht"], e * TILES + t + 1)
                            for j in range(2):
                                pe.wait_ge(OV[l]["over_load"], e * 288 + 16 * (6 * t + 4 + j + 1))
                                for k in range(2):
                                    fb = 2 * j + k
                                    for c in range(2):
                                        ins = mm(ps[:, 3 + c, :], over_hT[:, fb * P:(fb + 1) * P], wd[:, k, c * F:(c + 1) * F],
                                                 start=(fb == 0), stop=(fb == 3))
                                ins.then_inc(OV[l]["over_used"], 1)
                            pe.wait_ge(OV[l]["over_x"], e * TILES + t + 1)

        @block.vector
        def _(dve):
            v = nc.vector

            def split_lo(U):
                dve.wait_ge(hi_ready, U.n + 1)
                v.tensor_tensor(w_lo[:, U.slot, :], w_raw[:, U.slot, :], w_hi[:, U.hslot, :].bitcast(F32), ALU.subtract).then_inc(lo_ready, 1)

            def split_slab(base, k, g=0):
                for half in range(2):
                    split_lo(Unit(base, 2 * k + half, g))

            def norm(B, rstd_name, which, l, dst, done, tiles=range(TILES)):
                for t in tiles:
                    dve.wait_ge(L[rstd_name], B[rstd_name] + t + 1)
                    v.scalar_tensor_tensor(dst[:, t, :], x[:, t, :], rstd[:, t:t + 1], gain[:, which, :], ALU.mult, ALU.mult).then_inc(L[done], 1)

            v.memset(x[DEC:P, 2, :], 0.0).then_inc(x_padded, 1)
            for l in range(2):
                B = BEFORE[l]
                dve.wait_ge(gain_loaded[l][0], 16)
                norm(B, "rstd0", 0, l, h, "h_ready0")
                for i in range(2 * TILES):
                    if l == 0 and i in (2, 4):
                        split_lo(Unit(0, i // 2 - 1))
                    t, half = divmod(i, 2)
                    dve.wait_ge(L["hi0"], B["hi0"] + i + 1)
                    hi, src = hi_part(hT_hi, i)
                    v.tensor_tensor(lo_part(hT_hi, hT_lo, i), src, hi.bitcast(F32), ALU.subtract).then_inc(L["lo0"], 1)
                split_slab(BASE_IN[l], 1)
                if l == 1:
                    v.tensor_copy(pick_heads[:, :, :].rearrange("h p (c n) -> h (p c) n", c=2),
                                  ident[0:FOX_HEADS, 0:FOX_HEADS].unsqueeze(2).to_broadcast([FOX_HEADS, FOX_HEADS, DEC])).then_inc(fox["heads_ready"], 1)
                    dve.wait_ge(fox["wf_hi"], 1)
                    v.tensor_tensor(w_f_lo[:, :, :], w_f[:, :, :], w_f_hi[:, :, :].bitcast(F32), ALU.subtract).then_inc(fox["wf_lo"], 1)

                def forget_gates():
                    dve.wait_ge(fox["f_done"], 1)
                    z, az, e, s, s2, q, m0 = (lf[:, i, :] for i in range(7))
                    z3 = z.rearrange("p (t h) -> p t h", t=3)
                    link(dve, "dve", v.tensor_tensor(z3, ps[:, 7, 0:48].rearrange("p (t h) -> p t h", t=3),
                                                     b_forget[:, :].unsqueeze(1).to_broadcast([P, 3, 16]), ALU.add))
                    link(dve, "dve", v.tensor_scalar(m0, z, -1.0, None, ALU.mult))
                    v.tensor_tensor(az, z, m0, ALU.max).then_inc(fox["f_z"], 1)
                    dve.wait_ge(fox["f_exp"], 1)
                    link(dve, "dve", v.tensor_scalar(m0, z, 0.0, None, ALU.min))
                    link(dve, "dve", v.tensor_scalar(q, e, 2.0, None, ALU.add))
                    link(dve, "dve", v.reciprocal(s2, q))
                    link(dve, "dve", v.tensor_tensor(s, e, s2, ALU.mult))
                    link(dve, "dve", v.tensor_tensor(s2, s, s, ALU.mult))
                    link(dve, "dve", v.tensor_scalar(q, s2, 1.0 / 17, 1.0 / 15, ALU.mult, ALU.add))
                    for n in (13, 11, 9, 7, 5, 3, 1):
                        link(dve, "dve", v.tensor_tensor(q, q, s2, ALU.mult))
                        link(dve, "dve", v.tensor_scalar(q, q, 1.0 / n, None, ALU.add))
                    link(dve, "dve", v.tensor_tensor(q, q, s, ALU.mult))
                    v.scalar_tensor_tensor(logf[:, :, :].rearrange("p t h -> p (t h)"), q, -2.0, m0, ALU.mult, ALU.add).then_inc(fox["logf_ready"], 1)

                def offsets_lo():
                    dve.wait_ge(fox["off_hi"], 1)
                    v.scalar_tensor_tensor(off_lo[:, 0:320], ps[0:FOX_HEADS, 7, 0:320], -1.0 / SCALE, off_hi[:, 0:320].bitcast(F32),
                                           ALU.mult, ALU.subtract).then_inc(fox["off_lo"], 1)
                    dve.wait_ge(fox["off_hi"], 2)
                    v.scalar_tensor_tensor(off_lo[:, 320:832], ps[0:FOX_HEADS, 6, 0:512], 1.0 / SCALE, off_hi[:, 320:832].bitcast(F32),
                                           ALU.mult, ALU.subtract).then_inc(fox["off_lo"], 1)

                def add_low(b):
                    dve.wait_ge(L["low_moved"], B["low_moved"] + b + 1)
                    low = low_rows[:, b % 2, :]
                    v.tensor_tensor(low, low, acc(b, 2)[0:DEC, :], ALU.add).then_inc(L["low_added"], 1)

                for b in range(IN_BLOCKS[l]):
                    kind = in_kind(b)
                    split_lo(Unit(BASE_IN[l], 2 * b + 4))
                    if kind in "vg":
                        add_low(b)
                        if b < IN_BLOCKS[l] - 1:
                            split_lo(Unit(BASE_IN[l], 2 * b + 5))
                    if l == 0 and b == 0:
                        dve.wait_ge(qk_gains_loaded, 16 * 4)
                        dve.wait_ge(halves_ready, 2)
                    if kind in "qk":
                        for t in range(TILES):
                            n = ROWS[t]
                            if t == 2:
                                add_low(b)
                                if l == 1 and b == 1:
                                    offsets_lo()
                            dve.wait_ge(L["qk_sq"], B["qk_sq"] + 3 * b + t + 1)
                            v.tensor_reduce(ms[b % 2][0:n, 8 * t:8 * t + 8], qk[0:n, b % 2, t, :].rearrange("p (n d) -> p n d", d=HD), AX, ALU.add).then_inc(L["qk_ms"], 1)
                        split_lo(Unit(BASE_IN[l], 2 * b + 5))
                        dve.wait_ge(L["qk_r"], B["qk_r"] + b + 1)
                        for t in range(TILES):
                            n = ROWS[t]
                            src = acc(b, t) if t < 2 else low_rows[:, b % 2, :]
                            v.tensor_tensor(qk[0:n, b % 2, t, :].rearrange("p (n d) -> p n d", d=HD), src[0:n, :].rearrange("p (n d) -> p n d", d=HD),
                                            rr[b % 2][0:n, 8 * t:8 * t + 8].unsqueeze(2).to_broadcast([n, 8, HD]), ALU.mult).then_inc(L["qk_n1"], 1)
                        for t in range(TILES):
                            dve.wait_ge(L["qk_n1"], B["qk_n1"] + 3 * b + t + 1)
                            n = ROWS[t]
                            vw = qk[0:n, b % 2, t, :].rearrange("p (n d) -> p n d", d=HD)
                            gn = qk_gain[0:n, 2 * l + b // 2, :].unsqueeze(1).to_broadcast([n, 8, HD])
                            v.tensor_tensor(vw, vw, gn, ALU.mult).then_inc(L["qk_normed"], 1)

                    if l == 1 and b == 0:
                        forget_gates()
                    if l == 0 and b == 4:
                        dve.wait_ge(lam_loaded, 16 * 5)
                        for i in range(2):
                            v.tensor_tensor_reduce(lamv[:, 2 * i, :], lamv[:, 2 * i, :], lamv[:, 2 * i + 1, :], 1.0, 0.0,
                                                   ALU.mult, ALU.add, lamw[:, i:i + 1]).then_inc(lam_dots, 1)
                        dve.wait_ge(lam_exps, 1)
                        link(dve, "dve", v.tensor_tensor(lamw[:, 4:5], lamw[:, 3:4], lamw[:, 2:3], ALU.subtract))
                        link(dve, "dve", v.tensor_scalar(lamw[:, 5:6], lamw[:, 4:5], -LAMBDA_INIT, None, ALU.add))
                        dve.wait_ge(ident_loaded, 16)
                        dve.wait_ge(const_loaded, 16)
                        link(dve, "dve", v.tensor_copy(lamw[0:HD, 6:7], ones[0:HD, 0:1]))
                        link(dve, "dve", v.tensor_copy(lamw[HD:P, 6:7], lamw[HD:P, 5:6]))
                        link(dve, "dve", v.tensor_tensor(ident2[:, :], ident[:, 0:HD], ident[:, HD:P], ALU.add))
                        link(dve, "dve", v.tensor_copy(ident_r[:, :], ident[:, 0:FOX_HEADS]))

                its = list(items())

                def row_max(j, p, t):
                    dve.wait_ge(L["scores_done"], B["scores_done"] + j + 1)
                    if l == 0:
                        dve.wait_ge(L["bias_ready"], B["bias_ready"] + p + 1)
                    else:
                        dve.wait_ge(L["alibi"], B["alibi"] + 16)
                    if j >= 3:
                        dve.wait_ge(L["dT_done"], B["dT_done"] + j - 2)
                    n, a = KEYS[t], BCOL[t]
                    s = 2 * (j % 2)
                    flat = ps[:, s:s + 2, :].rearrange("p b n -> p (b n)")
                    members = 2 if t < 2 else 1
                    for c in range(members):
                        src = flat[:, 0:n] if t == 2 else ps[:, s + c, 0:n]
                        ins = v.tensor_tensor_reduce(probs[:, j % 3, c * n:(c + 1) * n], src,
                                                     bias[:, (p % 2 if l == 0 else 1), a:a + n], 1.0, -3e38, ALU.add, ALU.max,
                                                     mx[:, j % 3, c:c + 1])
                    ins.then_inc(L["max_done"], 1)
                    dve.wait_ge(L["max_done"], B["max_done"] + j + 1)
                    v.tensor_scalar(nmx[:, j % 3, 0:members], mx[:, j % 3, 0:members], -SCALE, None, ALU.mult).then_inc(L["neg_done"], 1)

                def mix(j, p, t):
                    dve.wait_ge(L["exp_done"], B["exp_done"] + j + 1)
                    n = 2 if t < 2 else 1
                    r, sums = rs[:, j % 3, 0:n], sm[:, j % 3, 0:n]
                    if l == 1:
                        inv = v.reciprocal(r, sums)
                        if t == 2:
                            link(dve, "dve", inv)
                            inv = v.tensor_copy(rs[0:DEC, j % 3, 1:2], rs[DEC:P, j % 3, 0:1])
                        inv.then_inc(L["mixed"], 1)
                        return
                    link(dve, "dve", v.reciprocal(r, sums))
                    if t < 2:
                        w = KEYS[t]
                        link(dve, "dve", v.scalar_tensor_tensor(r[:, 1:2], r[:, 1:2], sums[:, 0:1], lamw[:, 5:6], ALU.mult, ALU.mult))
                        v.scalar_tensor_tensor(probs[:, j % 3, 0:w], probs[:, j % 3, w:2 * w], r[:, 1:2], probs[:, j % 3, 0:w],
                                               ALU.mult, ALU.add).then_inc(L["mixed"], 1)
                    else:
                        link(dve, "dve", v.tensor_tensor(r, r, lamw[:, 6:7], ALU.mult))
                        v.tensor_scalar(diag[:, :], ident2[:, :], r, None, ALU.mult).then_inc(L["mixed"], 1)

                def take_o(j, p, t):
                    dve.wait_ge(L["pv_done"], B["pv_done"] + j + 1)
                    n = ROWS[t]
                    cs = slice(p * P, (p + 1) * P)
                    if l == 0 and t < 2:
                        v.tensor_scalar(o[:, t, cs], ps[:, 6, 0:P], rs[:, j % 3, 0:1], None, ALU.mult).then_inc(L["o_done"], 1)
                    elif l == 0:
                        v.tensor_copy(o[0:n, t, cs], ps[0:n, 6, 0:P]).then_inc(L["o_done"], 1)
                    else:
                        dve.wait_ge(L["mixed"], B["mixed"] + j + 1)
                        for c in range(2):
                            hs = slice(p * P + c * HD, p * P + (c + 1) * HD)
                            ins = v.scalar_tensor_tensor(o[0:n, t, hs], ps[0:n, 6, c * HD:(c + 1) * HD], rs[0:n, j % 3, c:c + 1],
                                                         gate[0:n, t, hs], ALU.mult, ALU.mult)
                        ins.then_inc(L["o_done"], 1)

                def norm_head(j, p, t):
                    dve.wait_ge(L["o_r"], B["o_r"] + j + 1)
                    vw = o[:, t, p * P:(p + 1) * P]
                    v.scalar_tensor_tensor(vw, vw, rr[0][:, j:j + 1], subln[:, :], ALU.mult, ALU.mult).then_inc(L["o_normed"], 1)

                if l == 1:
                    dve.wait_ge(L["g_done"], B["g_done"] + 6)
                row_max(*its[0])
                row_max(*its[1])
                dve.wait_ge(L["o_zeroed"], B["o_zeroed"] + 1)
                for j, p, t in its:
                    if j >= 2:
                        take_o(*its[j - 2])
                    mix(j, p, t)
                    if j + 2 < len(its):
                        row_max(*its[j + 2])
                    if l == 0 and j >= 7:
                        norm_head(*its[j - 7])
                take_o(*its[-2])
                take_o(*its[-1])
                if l == 0:
                    for item in its[-7:]:
                        norm_head(*item)
                for i in range(2 * TILES):
                    t, half = divmod(i, 2)
                    dve.wait_ge(L["o_hi"], B["o_hi"] + i + 1)
                    hi, src = hi_part(oT_hi, i)
                    v.tensor_tensor(lo_part(oT_hi, oT_lo, i), src, hi.bitcast(F32), ALU.subtract).then_inc(L["o_lo"], 1)
                def add_out(b, t):
                    wait_sum(dve, B, "out_done", BASE_OUT[l], b, t)
                    n = ROWS[t]
                    xs = x[0:n, t, b * F:(b + 1) * F]
                    ins = v.tensor_tensor(xs, xs, acc(b, t)[0:n, :], ALU.add)
                    if t == 2:
                        link(dve, "dve", ins)
                        dve.wait_ge(L["low_out_moved"], B["low_out_moved"] + b + 1)
                        ins = v.tensor_tensor(xs, xs, low_out[:, b, :], ALU.add)
                    ins.then_inc(L["x_mid"], 1)

                split_lo(Unit(BASE_OUT[l], 3))
                split_lo(Unit(BASE_OUT[l], 4))
                for t in range(TILES):
                    add_out(0, t)
                split_lo(Unit(BASE_OUT[l], 5))
                add_out(1, 0)
                split_lo(Unit(BASE_OUT[l], 6))
                add_out(1, 1)
                dve.wait_ge(gain_loaded[l][1], 16)
                if l == 0:
                    dve.wait_ge(small_loaded, 16 * SMALL)
                norm(B, "rstd1", 1, l, h2, "h_ready1", tiles=(0,))
                add_out(1, 2)
                norm(B, "rstd1", 1, l, h2, "h_ready1", tiles=(1, 2))

                def low_parts(t):
                    dve.wait_ge(L["h2hi"], B["h2hi"] + t + 1)
                    v.tensor_tensor(h2_lo[:, t, :], h2[:, t, :], h2_hi[:, t, :].bitcast(F32), ALU.subtract).then_inc(L["h2lo"], 1)

                low_parts(0)
                low_parts(1)
                K = lambda ins: link(dve, "dve", ins)
                b4 = lambda ap: ap.unsqueeze(2).to_broadcast([P, 3, 4])
                prio3 = prio.unsqueeze(1).to_broadcast([P, 3, 4])

                def first_of(dst, vals, top_):
                    K(v.tensor_tensor(t4, vals, b4(top_), ALU.is_equal))
                    K(v.tensor_tensor(t4, t4, prio3, ALU.mult))
                    K(v.tensor_reduce(dv, t4, AX, ALU.max))
                    K(v.tensor_tensor(dst, t4, b4(dv), ALU.is_equal))

                dve.wait_ge(L["logits"], B["logits"] + 1)
                K(v.tensor_tensor(lg, ps[:, 6, 0:60].rearrange("p (t n) -> p t n", t=3), b_router[:, l, :].unsqueeze(1).to_broadcast([P, 3, 20]), ALU.add))
                gl = lg[:, :, 0:4]
                K(v.tensor_reduce(gmx, gl, AX, ALU.max))
                v.tensor_tensor(gd, gl, b4(gmx), ALU.subtract).then_inc(L["logit_sb"], 1)
                first_of(oh, gl, gmx)
                v.tensor_tensor(oh, oh, b4(valid), ALU.mult).then_inc(L["onehot"], 1)
                low_parts(2)
                dve.wait_ge(L["ranks"], B["ranks"] + 1)
                K(v.tensor_tensor(t4, ps[:, 7, 0:12].rearrange("p (t g) -> p t g", t=3), oh, ALU.mult))
                K(v.tensor_tensor(t4b, t4, oh, ALU.add))
                K(v.tensor_scalar(pos, t4b, -1.0, None, ALU.add))

                def build_pick(g):
                    K_ = v.tensor_copy(pos_g[:, :], pos[:, :, bass.ds(g, 1)].rearrange("p t g -> p (t g)"))
                    K_.then_inc(L["pos_copied"], 1)
                    dve.wait_ge(L["pos_copied"], B["pos_copied"] + g + 1)
                    for t in range(TILES):
                        ins = v.tensor_scalar(pick[:, t, :], iota, pos_g[:, t:t + 1], None, ALU.is_equal)
                    ins.then_inc(L["pick_ready"], 1)

                build_pick(0)
                K(v.tensor_reduce(rank, t4, AX, ALU.add))
                K(v.tensor_scalar(over, rank, float(CAP), None, ALU.is_ge))
                dve.wait_ge(L["onehot"], B["onehot"] + 1)
                for gi in range(GROUPS):
                    K(v.tensor_tensor(t16[:, 12 * gi:12 * gi + 12].rearrange("p (t e) -> p t e", t=3), lg[:, :, 4 + 4 * gi:8 + 4 * gi],
                                      oh[:, :, gi:gi + 1].to_broadcast([P, 3, 4]), ALU.mult))
                K(v.tensor_tensor(t16[:, 0:24], t16[:, 0:24], t16[:, 24:48], ALU.add))
                K(v.tensor_tensor(ig, t16[:, 0:12].rearrange("p (t e) -> p t e", t=3), t16[:, 12:24].rearrange("p (t e) -> p t e", t=3), ALU.add))
                K(v.tensor_reduce(v1, ig, AX, ALU.max))
                first_of(oh1, ig, v1)
                K(v.scalar_tensor_tensor(ig2, oh1, -1e30, ig, ALU.mult, ALU.add))
                K(v.tensor_reduce(v2, ig2, AX, ALU.max))
                first_of(oh2, ig2, v2)
                v.tensor_tensor(dv, v2, v1, ALU.subtract).then_inc(L["logit_sb"], 1)

                def gate_weights():
                    dve.wait_ge(L["ranks"], B["ranks"] + 2)
                    K(v.tensor_reduce(total, ps[:, 7, 12:16], AX, ALU.max))
                    v.tensor_scalar(flag[0:1, 0:1], total[0:1, :], float(CAP), None, ALU.is_gt).then_inc(OV[l]["flag_ready"], 1)
                    dve.wait_ge(L["gexp"], B["gexp"] + 1)
                    K(v.tensor_reduce(gsum, ge, AX, ALU.add))
                    K(v.reciprocal(ptop, gsum))
                    dve.wait_ge(L["gexp"], B["gexp"] + 2)
                    K(v.tensor_scalar(w1, e2, 1.0, None, ALU.add))
                    K(v.reciprocal(w1, w1))
                    K(v.tensor_tensor(w1, w1, ptop, ALU.mult))
                    K(v.tensor_tensor(w2, w1, e2, ALU.mult))
                    K(v.tensor_tensor(t4, oh1, b4(w1), ALU.mult))
                    K(v.tensor_tensor(t4b, oh2, b4(w2), ALU.mult))
                    K(v.tensor_tensor(gate4, t4, t4b, ALU.add))
                    K(v.tensor_copy(gates_hl[:, :, 0:4], gate4))
                    v.tensor_tensor(gates_hl[:, :, 4:8], gate4, gates_hl[:, :, 0:4].bitcast(F32), ALU.subtract).then_inc(L["routed"], 1)

                def hidden(order, e, g):
                    wait_matrix(dve, l, order, ("u", e), g)
                    dve.wait_ge(L["silu_done"], B["silu_done"] + g * 4 + e + 1)
                    dve.wait_ge(L["slot_gated"], B["slot_gated"] + g + (2 if e == PER_GROUP else 1))
                    ge_ = slot_gate[:, e % PER_GROUP:e % PER_GROUP + 1]
                    v.scalar_tensor_tensor(hid[:, :], act_g[:, :], ge_, ps[:, 1, :], ALU.mult, ALU.mult).then_inc(L["hid_done"], 1)

                def hidden_lo(e, g, hi=hidT_hi, lo=hidT_lo):
                    dve.wait_ge(L["hT_hi"], B["hT_hi"] + g * 4 + e + 1)
                    v.tensor_tensor(lo[:, :, :].rearrange("p k n -> p (k n)"), ps[:, 2, :],
                                    hi[:, :, :].rearrange("p k n -> p (k n)").bitcast(F32), ALU.subtract).then_inc(L["hT_lo"], 1)

                def gathered_lo(g):
                    for i in range(2):
                        dve.wait_ge(L["x_hi"], B["x_hi"] + g * 2 + i + 1)
                        xs = slice(4 * i, 4 * i + 4)
                        v.tensor_tensor(xT_lo[:, xs, :].rearrange("p k n -> p (k n)"), ps[:, 5 + i, :],
                                        xT_hi[:, xs, :].rearrange("p k n -> p (k n)").bitcast(F32), ALU.subtract).then_inc(L["x_lo"], 1)

                def take_gates(g, first=False):
                    dve.wait_ge(L["slot_done"], B["slot_done"] + g + 1)
                    if not first:
                        dve.wait_ge(L["hid_done"], B["hid_done"] + g * 4)
                    v.tensor_reduce(slot_gate[:, :], ps[:, 7, 384:392].rearrange("p (a e) -> p e a", a=2), AX, ALU.add).then_inc(L["slot_gated"], 1)

                def add_back(g):
                    for i in range(2 * TILES):
                        t, c = divmod(i, 2)
                        dve.wait_ge(L["back_done"], B["back_done"] + g * 6 + i + 1)
                        xs = x[:, t, c * F:(c + 1) * F]
                        v.tensor_tensor(xs, xs, ps[:, BACK[i], :], ALU.add).then_inc(L["x_added"], 1)

                def take_pickT():
                    v.tensor_copy(pickT[:, :, :].rearrange("p t n -> p (t n)"), ps[:, 7, 0:384]).then_inc(L["pickT_taken"], 1)

                def moe_round(order, g):
                    last = order is LAST
                    for m, (kind, e) in enumerate(order):
                        ahead = not (last and m >= len(order) - 2 and l == 1)
                        late = m == len(order) - 1 or last and m >= len(order) - 3
                        if ahead and not late:
                            split_lo(Unit(BASE_MOE[l], 2 * (m + 4), g))
                        if kind == "u" and e < PER_GROUP:
                            hidden(order, e, g)
                        if (kind, e) in (("g", 1), ("g", 2), ("g", 3)):
                            hidden_lo(e - 1, g)
                        if (kind, e) == ("u", 1) and not last:
                            build_pick(g + 1)
                        if (kind, e) == ("u", 3) and not last:
                            gathered_lo(g + 1)
                            take_gates(g + 1)
                        if (kind, e) == ("d", 2):
                            if last:
                                hidden_lo(3, g, hidT_last_hi, hidT_last_lo)
                            else:
                                hidden_lo(3, g)
                        if (kind, e) == ("d", 3):
                            for i in range(2):
                                dve.wait_ge(L["y_hi"], B["y_hi"] + g * 2 + i + 1)
                                cs = slice(i * F, (i + 1) * F)
                                v.tensor_tensor(y_lo[:, cs], ps[:, 3 + i, :], y_hi[:, cs].bitcast(F32), ALU.subtract).then_inc(L["y_lo"], 1)
                        if (kind, e) == ("u", PER_GROUP):
                            hidden(order, e, g)
                            add_back(g)
                            take_pickT()
                        if last and m == len(order) - 2:
                            split_lo(Unit(BASE_MOE[l], 2 * (m + 3) + 1, g))
                        if ahead and not (last and m == len(order) - 1):
                            if late:
                                split_lo(Unit(BASE_MOE[l], 2 * (m + 4), g))
                            if not (last and m == len(order) - 3):
                                split_lo(Unit(BASE_MOE[l], 2 * (m + 4) + 1, g))
                    if last:
                        add_back(g)

                split_lo(Unit(BASE_OUT[l], 7))
                gathered_lo(0)
                gate_weights()
                take_gates(0, first=True)
                take_pickT()
                split_slab(BASE_MOE[l], 2)
                hidden(FIRST, 0, 0)
                split_slab(BASE_MOE[l], 3)
                with dve.Fori(0, GROUPS - 1) as g:
                    moe_round(ORDER, g)
                moe_round(LAST, GROUPS - 1)

                dve.wait_ge(OV[l]["flag_ready"], 1)
                flag_v = dve.value_load(flag[0:1, 0:1])
                kept = chain["dve"]
                with dve.If(flag_v > 0):
                    v.tensor_tensor(t4, gate4, b4(over), ALU.mult).then_inc(OV[l]["over_done"], 1)
                    dve.wait_ge(OV[l]["over_done"], 1)
                    for gi in range(GROUPS):
                        ins = v.tensor_tensor(over_gate[:, :, 4 * gi:4 * gi + 4], t4, oh[:, :, gi:gi + 1].to_broadcast([P, 3, 4]), ALU.mult)
                    ins.then_inc(OV[l]["over_done"], 1)
                    with dve.Fori(0, EXPERTS) as e:
                        dve.wait_ge(OV[l]["over_done"], e + 2)
                        v.tensor_copy(over_col[:, :], over_gate[:, :, bass.ds(e, 1)].rearrange("p t e -> p (t e)")).then_inc(OV[l]["over_done"], 1)
                        dve.wait_ge(OV[l]["over_done"], e + 3)
                        for t in range(TILES):
                            dve.wait_ge(OV[l]["over_used"], e * 18 + 6 * t + 5)
                            dve.wait_ge(OV[l]["over_act"], e * TILES + t + 1)
                            v.scalar_tensor_tensor(hid[:, :], act_g[:, :], over_col[:, t:t + 1], ps[:, 1, :], ALU.mult, ALU.mult).then_inc(OV[l]["over_hid"], 1)
                            dve.wait_ge(OV[l]["over_used"], e * 18 + 6 * t + 7)
                            for c in range(2):
                                xs = x[:, t, c * F:(c + 1) * F]
                                ins = v.tensor_tensor(xs, xs, ps[:, 3 + c, :], ALU.add)
                            ins.then_inc(OV[l]["over_x"], 1)
                assert chain["dve"] == kept


_OUT_SHAPES = [
    ("y_prompt", (1, SEQ, D)), ("y_sample", (1, DEC, D)),
    ("new_diff_k_prompt", (1, 1, SEQ, 8, 128)), ("new_diff_v_prompt", (1, 1, SEQ, 8, 128)),
    ("new_fox_k_prompt", (1, 1, SEQ, 16, 64)), ("new_fox_v_prompt", (1, 1, SEQ, 16, 64)),
    ("new_fox_logf_prompt", (1, 1, SEQ, 16)),
    ("new_diff_k_sample", (1, 1, DEC, 8, 128)), ("new_diff_v_sample", (1, 1, DEC, 8, 128)),
    ("new_fox_k_sample", (1, 1, DEC, 16, 64)), ("new_fox_v_sample", (1, 1, DEC, 16, 64)),
    ("new_fox_logf_sample", (1, 1, DEC, 16)),
]


def kernel(**inputs):
    import concourse.bacc as _bacc
    from concourse.bass_utils import run_bass_kernel_spmd as _run

    nc = _bacc.Bacc("TRN2", target_bir_lowering=False, num_devices=1)
    arrays, aps = {}, {}
    host = {name: np.ascontiguousarray(a) for name, a in inputs.items()}
    host["c_consts"], host["c_dist"], host["c_mask"] = constants()
    for name, a in host.items():
        arrays[f"in_{name}"] = a
        aps[name] = nc.dram_tensor(f"in_{name}", a.shape, mybir.dt.from_np(a.dtype), kind="ExternalInput").ap()
    for name, shape in _OUT_SHAPES:
        aps[name] = nc.dram_tensor(f"out_{name}", shape, F32, kind="ExternalOutput").ap()
    build(nc, aps)
    r = _run(nc, [arrays], core_ids=[0])
    return tuple(r.results[0][f"out_{name}"] for name, _ in _OUT_SHAPES)
```
